# Optimizing a Trainium2 kernel written in Bass

```python
import jax, jax.numpy as jnp
from jax import lax
import numpy as np

D_MODEL = 1024
BATCH = 1
SEQ = 256
DEPTH = 1

CHUNK = 64
N_META = 16
CONV_CH = D_MODEL
CONV_WIDTH = 31
FOX_HEADS = 16
FOX_HEAD_DIM = 64
FOX_WIDTH = FOX_HEADS * FOX_HEAD_DIM
Q_BLOCK = 128
N_EXPERTS = 32
TOP_K = 4
D_EXPERT = D_MODEL
SWIGLU_ALPHA = 1.702
SWIGLU_LIMIT = 7.0
MOE_BLOCK = 256
RMS_EPS = 1e-5
LN_EPS = 1e-5
FORGET_BIAS_INIT = 3.0

OFF_GLU = 0
OFF_Q = OFF_GLU + 2 * CONV_CH
OFF_K = OFF_Q + FOX_WIDTH
OFF_V = OFF_K + FOX_WIDTH
OFF_F = OFF_V + FOX_WIDTH
OFF_GA = OFF_F + FOX_HEADS
OFF_GB = OFF_GA + D_MODEL
IN_COLS = OFF_GB + D_MODEL

kernel_name = 'hybrid_conv_fox_moe_streaming_block'

def rms_norm(x, g):
    xf = x.astype(jnp.float32)
    y = xf * lax.rsqrt(jnp.mean(xf * xf, axis=-1, keepdims=True) + RMS_EPS)
    return (y * g.astype(jnp.float32)).astype(x.dtype)

def layer_norm(x, g, b):
    xf = x.astype(jnp.float32)
    mu = jnp.mean(xf, axis=-1, keepdims=True)
    xc = xf - mu
    y = xc * lax.rsqrt(jnp.mean(xc * xc, axis=-1, keepdims=True) + LN_EPS)
    return (y * g.astype(jnp.float32) + b.astype(jnp.float32)).astype(x.dtype)

def fox_attention(q, k, v, log_f):
    b, l, h, dh = q.shape
    lp = -(-l // Q_BLOCK) * Q_BLOCK
    pad = ((0, 0), (0, lp - l), (0, 0), (0, 0))
    q = jnp.pad(q, pad)
    k = jnp.pad(k, pad)
    v = jnp.pad(v, pad)
    cum = jnp.cumsum(jnp.pad(log_f, ((0, 0), (0, lp - l), (0, 0))), axis=1).transpose(0, 2, 1)
    kpos = jnp.arange(lp)
    scale = FOX_HEAD_DIM ** -0.5

    def block(i):
        q0 = i * Q_BLOCK
        qb = lax.dynamic_slice_in_dim(q, q0, Q_BLOCK, axis=1)
        cq = lax.dynamic_slice_in_dim(cum, q0, Q_BLOCK, axis=2)
        s = jnp.einsum('bqhd,bkhd->bhqk', qb, k, preferred_element_type=jnp.float32) * scale
        s = s + cq[..., :, None] - cum[..., None, :]
        qpos = q0 + jnp.arange(Q_BLOCK)
        s = jnp.where(kpos[None, :] <= qpos[:, None], s, -jnp.inf)
        p = jax.nn.softmax(s, axis=-1).astype(v.dtype)
        return jnp.einsum('bhqk,bkhd->bqhd', p, v)

    out = lax.map(block, jnp.arange(lp // Q_BLOCK))
    out = out.transpose(1, 0, 2, 3, 4).reshape(b, lp, h, dh)
    return out[:, :l]

def hybrid_mixer(xn, w_in, b_in, conv_w, conv_b, ln_g, ln_b, w_conv_out, w_attn_out, w_mix_out):
    b, l, _ = xn.shape
    proj = xn @ w_in + b_in
    glu = proj[..., OFF_GLU:OFF_GLU + CONV_CH] * jax.nn.sigmoid(proj[..., OFF_GLU + CONV_CH:OFF_Q])
    u = lax.conv_general_dilated(glu, conv_w[:, None, :], window_strides=(1,),
                                 padding=[(CONV_WIDTH - 1, 0)],
                                 dimension_numbers=('NWC', 'WIO', 'NWC'),
                                 feature_group_count=CONV_CH) + conv_b
    u = jax.nn.silu(layer_norm(u, ln_g, ln_b))
    branch_a = u @ w_conv_out
    q = proj[..., OFF_Q:OFF_K].reshape(b, l, FOX_HEADS, FOX_HEAD_DIM)
    k = proj[..., OFF_K:OFF_V].reshape(b, l, FOX_HEADS, FOX_HEAD_DIM)
    v = proj[..., OFF_V:OFF_F].reshape(b, l, FOX_HEADS, FOX_HEAD_DIM)
    log_f = jax.nn.log_sigmoid(proj[..., OFF_F:OFF_GA].astype(jnp.float32))
    attn = fox_attention(q, k, v, log_f).reshape(b, l, FOX_WIDTH)
    branch_b = attn @ w_attn_out
    merged = (jax.nn.sigmoid(proj[..., OFF_GA:OFF_GB]) * branch_a
              + jax.nn.sigmoid(proj[..., OFF_GB:IN_COLS]) * branch_b)
    return merged @ w_mix_out

def moe_ffn(h, router_w, router_b, w_gu, b_gu, w_down, b_down):
    n, d = h.shape
    logits = jnp.dot(h, router_w, preferred_element_type=jnp.float32) + router_b.astype(jnp.float32)
    top_val, top_idx = lax.top_k(logits, TOP_K)
    gate = jax.nn.softmax(top_val, axis=-1).reshape(-1)
    n_assign = n * TOP_K
    flat_e = top_idx.reshape(-1)
    order = jnp.argsort(flat_e)
    sorted_e = flat_e[order]
    sorted_tok = order // TOP_K
    counts = jnp.bincount(flat_e, length=N_EXPERTS)
    blocks_per_e = (counts + MOE_BLOCK - 1) // MOE_BLOCK
    blk_end = jnp.cumsum(blocks_per_e)
    blk_start = blk_end - blocks_per_e
    grp_start = jnp.cumsum(counts) - counts
    slot = blk_start[sorted_e] * MOE_BLOCK + (jnp.arange(n_assign) - grp_start[sorted_e])
    n_blocks = -(-n_assign // MOE_BLOCK) + N_EXPERTS
    slot_tok = jnp.zeros((n_blocks * MOE_BLOCK,), jnp.int32).at[slot].set(sorted_tok.astype(jnp.int32))
    block_e = jnp.minimum(jnp.searchsorted(blk_end, jnp.arange(n_blocks), side='right'), N_EXPERTS - 1)

    def expert_block(args):
        tok, e = args
        xb = h[tok]
        gu = xb @ w_gu[e] + b_gu[e]
        g = jnp.minimum(gu[:, :D_EXPERT], SWIGLU_LIMIT)
        up = jnp.clip(gu[:, D_EXPERT:], -SWIGLU_LIMIT, SWIGLU_LIMIT)
        act = (g * jax.nn.sigmoid(SWIGLU_ALPHA * g)) * (up + 1)
        return act @ w_down[e] + b_down[e]

    y_slots = lax.map(expert_block, (slot_tok.reshape(n_blocks, MOE_BLOCK), block_e)).reshape(-1, d)
    y_assign = y_slots[slot] * gate[order][:, None].astype(h.dtype)
    return jax.ops.segment_sum(y_assign, sorted_tok, num_segments=n)

def setup_inputs(seed: int = 0) -> dict:
    key = jax.random.key(seed)
    ks = jax.random.split(key, 24)
    f32 = jnp.float32
    nrm = lambda k, shape, s: jax.random.normal(k, shape, f32) * s
    b_in = nrm(ks[4], (DEPTH, IN_COLS), 0.02).at[:, OFF_F:OFF_GA].add(FORGET_BIAS_INIT)
    return {
        'x': nrm(ks[0], (BATCH, SEQ, D_MODEL), 1.0),
        'meta_tokens': nrm(ks[1], (N_META, D_MODEL), 1.0),
        'attn_norm_g': 1.0 + nrm(ks[2], (DEPTH, D_MODEL), 0.05),
        'w_in': nrm(ks[3], (DEPTH, D_MODEL, IN_COLS), D_MODEL ** -0.5),
        'b_in': b_in,
        'conv_w': nrm(ks[5], (DEPTH, CONV_WIDTH, CONV_CH), CONV_WIDTH ** -0.5),
        'conv_b': nrm(ks[6], (DEPTH, CONV_CH), 0.02),
        'conv_ln_g': 1.0 + nrm(ks[7], (DEPTH, CONV_CH), 0.05),
        'conv_ln_b': nrm(ks[8], (DEPTH, CONV_CH), 0.02),
        'w_conv_out': nrm(ks[9], (DEPTH, CONV_CH, D_MODEL), CONV_CH ** -0.5),
        'w_attn_out': nrm(ks[10], (DEPTH, FOX_WIDTH, D_MODEL), FOX_WIDTH ** -0.5),
        'w_mix_out': nrm(ks[11], (DEPTH, D_MODEL, D_MODEL), D_MODEL ** -0.5),
        'ffn_norm_g': 1.0 + nrm(ks[12], (DEPTH, D_MODEL), 0.05),
        'router_w': nrm(ks[13], (DEPTH, D_MODEL, N_EXPERTS), D_MODEL ** -0.5),
        'router_b': nrm(ks[14], (DEPTH, N_EXPERTS), 0.01),
        'w_gu': nrm(ks[15], (DEPTH, N_EXPERTS, D_MODEL, 2 * D_EXPERT), D_MODEL ** -0.5),
        'b_gu': nrm(ks[16], (DEPTH, N_EXPERTS, 2 * D_EXPERT), 0.01),
        'w_down': nrm(ks[17], (DEPTH, N_EXPERTS, D_EXPERT, D_MODEL), D_EXPERT ** -0.5),
        'b_down': nrm(ks[18], (DEPTH, N_EXPERTS, D_MODEL), 0.01),
        'final_norm_g': 1.0 + nrm(ks[19], (D_MODEL,), 0.05),
    }

def reference(x, meta_tokens, attn_norm_g, w_in, b_in, conv_w, conv_b, conv_ln_g, conv_ln_b,
              w_conv_out, w_attn_out, w_mix_out, ffn_norm_g, router_w, router_b, w_gu, b_gu,
              w_down, b_down, final_norm_g):
    b = x.shape[0]
    meta = jnp.broadcast_to(meta_tokens[None].astype(x.dtype), (b, N_META, D_MODEL))
    h = jnp.concatenate([meta, x], axis=1)
    for i in range(DEPTH):
        h = h + hybrid_mixer(rms_norm(h, attn_norm_g[i]), w_in[i], b_in[i], conv_w[i], conv_b[i],
                             conv_ln_g[i], conv_ln_b[i], w_conv_out[i], w_attn_out[i], w_mix_out[i])
        hn = rms_norm(h, ffn_norm_g[i]).reshape(-1, D_MODEL)
        h = h + moe_ffn(hn, router_w[i], router_b[i], w_gu[i], b_gu[i], w_down[i], b_down[i]).reshape(h.shape)
    h = rms_norm(h, final_norm_g)
    return h[:, N_META:]


_drawn_inputs = setup_inputs


def setup_inputs(seed=0):
    import zlib

    import numpy as np

    out = dict(_drawn_inputs(seed))
    spreads = {}
    factors = {'b_gu': 8.0, 'b_down': 8.0}
    for name, (base, spread) in spreads.items():
        noise = np.random.default_rng([zlib.crc32(name.encode()), seed]).standard_normal(out[name].shape)
        drawn = base * np.exp(spread * noise) if base else spread * noise
        out[name] = __import__('jax').numpy.asarray(drawn.astype(out[name].dtype))
    for name, factor in factors.items():
        out[name] = (out[name] * factor).astype(out[name].dtype)
    return out
```

```python
from contextlib import ExitStack

import concourse.bass as bass
from concourse import mybir
from concourse.alu_op_type import AluOpType as ALU

ACT = mybir.ActivationFunctionType
AX_X = mybir.AxisListType.X
F32 = mybir.dt.float32
I32 = mybir.dt.int32
U32 = mybir.dt.uint32
ds = bass.ds

P = 128
BANK = 512
D = 1024
KC = D // P
META = 16
SEQ = 256
T = META + SEQ
TT = SEQ // P
TAPS = 31
HEADS, DH = 16, 64
PAIRS = HEADS // 2
E, TOPK = 32, 4
GU = 2 * D
SLOTS = 64
BLOCKS = SEQ // SLOTS
EXTRA = (SEQ * TOPK - 1) // SLOTS
EPS = 1e-5
ALPHA, LIMIT = 1.702, 7.0
MASKED = -1.0e30

OFF_A, OFF_B = 0, D
OFF_Q, OFF_K, OFF_V = 2 * D, 3 * D, 4 * D
OFF_F = 5 * D
OFF_GA = OFF_F + HEADS
OFF_GB = OFF_GA + D
COL_A, COL_B, COL_Q, COL_K, COL_V, COL_GA, COL_GB, COL_NORM, COL_CB, COL_LG, COL_LB = (
    KC * n for n in range(11))
NCOLS = 11 * KC
TAB_POS, TAB_W, TAB_BG, TAB_BD = 0, TT, 2 * TT, 2 * TT + GU // P
TABW = TAB_BD + KC
CONV_STEPS = TAPS + 1
K0, K1 = META + P, T
SCW = K0 + K1
CHUNK = 4 * D
GU_CHUNKS, CHUNKS = 4, 6


class Chain:

    def __init__(self, eng, sem, per_round=0):
        self.eng, self.sem, self.per_round, self.base, self.k = eng, sem, per_round, 0, 0

    def at(self, n):
        self.base, self.k = n * self.per_round, 0

    def link(self, ins):
        self.k += 1
        ins.then_inc(self.sem, 1)
        self.eng.wait_ge(self.sem, self.base + self.k)


def build(nc, x, meta_tokens, attn_norm_g, w_in, b_in, conv_w, conv_b, conv_ln_g, conv_ln_b,
          w_conv_out, w_attn_out, w_mix_out, ffn_norm_g, router_w, router_b, w_gu, b_gu,
          w_down, b_down, final_norm_g, out):
    ctx = ExitStack()
    with ctx:
        def sb(name, shape, dt=F32):
            return ctx.enter_context(nc.sbuf_tensor(name, shape, dt))

        def sem(name):
            return ctx.enter_context(nc.semaphore(name))

        ps = ctx.enter_context(nc.psum_tensor("ps", [P, 8, BANK], F32))

        ring = sb("ring", [P, CHUNKS, CHUNK])
        wbuf = sb("wbuf", [P, 2, 4 * D])
        x_tok = sb("x_tok", [P, TT, D])
        xn = sb("xn", [P, 3 * D])
        xnT = sb("xnT", [P, KC, T])
        u = sb("u", [P, KC * SEQ])
        gates = sb("gates", [P, 2 * KC * SEQ])
        gain = sb("gain", [P, D])
        glu = sb("glu", [P, 2, TAPS - 1 + T])
        sig_b = sb("sig_b", [P, T])
        conv_acc = sb("conv_acc", [P, 2, SEQ])
        cols = sb("cols", [P, NCOLS])
        taps = sb("taps", [P, KC, TAPS])
        table = sb("table", [P, E, TABW])
        ident = sb("ident", [P, P])
        ones = sb("ones", [P, P])
        before = sb("before", [P, P])
        mask0 = sb("mask0", [P, K0])
        mask1 = sb("mask1", [P, K1])
        neg_head = sb("neg_head", [HEADS, HEADS])
        iota = sb("iota", [P, SEQ])
        wf = sb("wf", [P, KC, HEADS])
        wr = sb("wr", [P, KC, E])
        rb = sb("rb", [P, E])
        bf = sb("bf", [HEADS, 1])
        cum = sb("cum", [HEADS, T])
        cum_q = sb("cum_q", [P, TT, HEADS])
        stat = sb("stat", [P, 16])
        stat2 = sb("stat2", [P, 16])
        lnb = sb("lnb", [P, 2, SEQ])
        route = sb("route", [P, 12 * E])
        route_i = sb("route_i", [P, 8], U32)
        work_f = sb("work_f", [1, 3 * 16])
        work = sb("work", [1, 3 * 16], I32)

        x_n = xn[:].rearrange("p (t d) -> p t d", t=3)
        u_c = u[:].rearrange("p (c t) -> p c t", c=KC)
        sigs = gates[:].rearrange("p (g c t) -> p g c t", g=2, c=KC)
        raw_cols = u[0:NCOLS, 0:P]
        raw_taps = u[0:TAPS, D:2 * D]
        raw_bg = gates[0:E, 0:GU]
        raw_bd = gates[0:E, GU:GU + D]
        x_meta = gates[0:META, GU + D:GU + 2 * D]
        attn_T = xn[:, 0:KC * SEQ].rearrange("p (c t) -> p c t", c=KC)
        squares = attn_T
        merged = xnT[:].rearrange("p c t -> p (c t)")[:, 0:KC * SEQ].rearrange("p (c t) -> p c t", c=KC)
        spare = [0]

        def lent(n):
            a = spare[0]
            spare[0] += n
            assert spare[0] <= 2 * CHUNK
            return ring[:, 4:6, :].rearrange("p a b -> p (a b)")[:, a:a + n]

        q_s = [lent(SEQ) for _ in range(2)]
        k_s = [lent(T) for _ in range(2)]
        v_s = [lent(3 * P) for _ in range(2)]
        v_T = lent(T)
        cd = [[lent(T) for _ in range(2)] for _ in range(2)]
        sc = [lent(SCW) for _ in range(2)]
        pr = [lent(SCW) for _ in range(2)]
        pT = [lent(3 * P) for _ in range(2)]
        pTm = [lent(SEQ) for _ in range(2)]
        tmp_m = [lent(SEQ) for _ in range(2)]
        ftmp = lent(3 * T)[0:HEADS, :].rearrange("p (a t) -> p a t", a=3)
        hn = xn[:, 0:TT * D].rearrange("p (t d) -> p t d", t=TT)
        hnT = wbuf[:, 0, 0:KC * SEQ].rearrange("p (c t) -> p c t", c=KC)
        squares_x = u[:, 0:D]
        result = wbuf[:, 1, D:3 * D].rearrange("p (t d) -> p t d", t=TT)
        W = KC * SLOTS
        gate_b = gates[:, 0:W]
        up_b = gates[:, W:2 * W]
        gate_m = gates[:, 2 * W:3 * W]
        sg = gates[:, 3 * W:4 * W]
        gs = gates[:, 4 * W:5 * W]
        act_s = gates[:, 5 * W:6 * W].rearrange("p (c s) -> p c s", c=KC)
        xg = gates[:, 6 * W:7 * W]
        yT = gates[:, 7 * W:8 * W]
        y_s = u[0:SLOTS, 0:D]
        G_s = u[0:SLOTS, D:D + SEQ]
        sel = u[:, D + SEQ:D + SEQ + TT * SLOTS].rearrange("p (t s) -> p t s", t=TT)
        sel_w = u[:, D + SEQ + TT * SLOTS:D + SEQ + 2 * TT * SLOTS].rearrange("p (t s) -> p t s", t=TT)
        cur_g = stat[:, 0:2 * TT]
        cur_s = stat[:, 4:4 + 2 * TT]
        cur_b = sb("cur_b", [P, GU // P])
        cur_d = sb("cur_d", [P, KC])

        x_loaded, meta_loaded, rows_loaded = sem("x_loaded"), sem("meta_loaded"), sem("rows_loaded")
        consts_loaded, gain_loaded, gain2_loaded = sem("consts_loaded"), sem("gain_loaded"), sem("gain2_loaded")
        raws_loaded = sem("raws_loaded")
        glu_w = [sem(f"glu_w{k}") for k in range(2)]
        qkv_w = [sem(f"qkv_w{k}") for k in range(2)]
        out_w = [sem(f"out_w{k}") for k in range(2)]
        mix_w = sem("mix_w")
        chunk_w = [sem(f"chunk_w{c}") for c in range(CHUNKS)]
        chunk_used = [sem(f"chunk_used{c}") for c in range(CHUNKS)]
        stored = sem("stored")
        masks_made, tri = sem("masks_made"), sem("tri")
        cols_ps, cols_made = sem("cols_ps"), sem("cols_made")
        taps_ps, taps_made = sem("taps_ps"), sem("taps_made")
        bias_ps, bias_made = sem("bias_ps"), sem("bias_made")
        sq_x, sq_meta, rms_var, rms_root, xn_made = (
            sem("sq_x"), sem("sq_meta"), sem("rms_var"), sem("rms_root"), sem("xn_made"))
        xnT_ps, xnT_made = sem("xnT_ps"), sem("xnT_made")
        pad_made = sem("pad_made")
        glu_ps, sig_made, glu_made, conv_step = sem("glu_ps"), sem("sig_made"), sem("glu_made"), sem("conv_step")
        gates_ps, gates_made = sem("gates_ps"), sem("gates_made")
        mean_ps, centred, sq_made, var_ps = sem("mean_ps"), sem("centred"), sem("sq_made"), sem("var_ps")
        ln_var, ln_root, ln_made, silu_in, silu_made = (
            sem("ln_var"), sem("ln_root"), sem("ln_made"), sem("silu_in"), sem("silu_made"))
        f_ps, f_abs, f_log, cum_made, cumT_ps, cum_q_made = (
            sem("f_ps"), sem("f_abs"), sem("f_log"), sem("cum_made"), sem("cumT_ps"), sem("cum_q_made"))
        q_ps, k_ps, v_ps = sem("q_ps"), sem("k_ps"), sem("v_ps")
        q_made, k_made, vT_made, vtr_ps, v_made = (
            sem("q_made"), sem("k_made"), sem("vT_made"), sem("vtr_ps"), sem("v_made"))
        cd_made = sem("cd_made")
        scores = [sem(f"scores{h}") for h in range(2)]
        scores_read = [sem(f"scores_read{h}") for h in range(2)]
        max_made = [sem(f"max_made{h}") for h in range(2)]
        exp_made = [sem(f"exp_made{h}") for h in range(2)]
        probs = [sem(f"probs{h}") for h in range(2)]
        probsT_ps = [sem(f"probsT_ps{h}") for h in range(2)]
        probsT = [sem(f"probsT{h}") for h in range(2)]
        heads_ps, heads_out = sem("heads_ps"), sem("heads_out")
        br_ps, merged_made = sem("br_ps"), sem("merged_made")
        h_ps = sem("h_ps")
        ffn_sq, ffn_var, ffn_root, hn_made = sem("ffn_sq"), sem("ffn_var"), sem("ffn_root"), sem("hn_made")
        hnT_ps, hnT_made = sem("hnT_ps"), sem("hnT_made")
        logits_ps, top_made, exps_made, picks_made, pos_ps, table_made = (
            sem("logits_ps"), sem("top_made"), sem("exps_made"), sem("picks_made"), sem("pos_ps"),
            sem("table_made"))
        work_made = sem("work_made")
        sel_made, sel_w_made = sem("sel_made"), sem("sel_w_made")
        xg_ps, xg_made = sem("xg_ps"), sem("xg_made")
        gu_ps, y_ps = chunk_used[GU_CHUNKS - 1], chunk_used[CHUNKS - 1]
        gu_read, gate_ready, sg_made, act_made = (
            sem("gu_read"), sem("gate_ready"), sem("sg_made"), sem("act_made"))
        yT_made, half_ps, half_made = sem("yT_made"), sem("half_ps"), sem("half_made")
        turn_begun = sem("turn_begun")
        G_ps, G_made, scattered = sem("G_ps"), sem("G_made"), sem("scattered")
        final_sq, final_var, final_root, final_made = (
            sem("final_sq"), sem("final_var"), sem("final_root"), sem("final_made"))
        dve_once, dve_merge, dve_pair = sem("dve_once"), sem("dve_merge"), sem("dve_pair")
        dve_y, dve_w, dve_s, dve_a = sem("dve_y"), sem("dve_w"), sem("dve_s"), sem("dve_a")
        act_once, pool_once = sem("act_once"), sem("pool_once")

        def fill(k, g):
            return wbuf[:, k, g * D:(g + 1) * D].rearrange("p (c m) -> p c m", c=KC)

        w_in0 = w_in[0]

        def load_chunk(sp, e, c):
            if c < GU_CHUNKS:
                src = w_gu[0][ds(e, 1), c * 2 * P:(c + 1) * 2 * P, :].rearrange("a (c p) n -> p (a c) n", p=P)
                dst = ring[:, c, :].rearrange("p (c n) -> p c n", c=2)
            else:
                c2 = c - GU_CHUNKS
                src = w_down[0][ds(e, 1), c2 * 4 * P:(c2 + 1) * 4 * P, :].rearrange("a (c p) n -> p (a c) n", p=P)
                dst = ring[:, c, :].rearrange("p (c n) -> p c n", c=4)
            sp.dma_start(dst, src).then_inc(chunk_w[c], 16)

        blk = ctx.enter_context(nc.Block())

        @blk.sync
        def _(sp):
            sp.dma_start(x_tok[:], x[0].rearrange("(t p) d -> p t d", p=P)).then_inc(x_loaded, 16)
            sp.dma_start(x_meta, meta_tokens).then_inc(meta_loaded, 16)

            def load_tiles(k, j, sources, loaded):
                for g, (w, c0) in enumerate(sources):
                    src = w[:, ds(j * P + c0, P)].rearrange("(c p) m -> p c m", p=P)
                    sp.dma_start(fill(k, g), src).then_inc(loaded[k], 16)

            glu_tiles = [(w_in0, c0) for c0 in (OFF_A, OFF_B, OFF_GA, OFF_GB)]
            qkv_tiles = [(w_in0, c0) for c0 in (OFF_Q, OFF_K, OFF_V)]
            out_tiles = [(w_conv_out[0], 0), (w_attn_out[0], 0)]
            for k in range(2):
                load_tiles(k, k, glu_tiles, glu_w)
            with sp.Fori(1, KC // 2) as i:
                for k in range(2):
                    sp.wait_ge(gates_ps, i * 2 + (k - 1))
                    load_tiles(k, i * 2 + k, glu_tiles, glu_w)
            for c in range(2):
                load_chunk(sp, 0, c)
            for k in range(2):
                sp.wait_ge(gates_ps, KC - 1 + k)
                load_tiles(k, k, qkv_tiles, qkv_w)
            with sp.Fori(1, PAIRS // 2) as i:
                for k in range(2):
                    sp.wait_ge(q_ps, i * 2 + (k - 1))
                    load_tiles(k, i * 2 + k, qkv_tiles, qkv_w)
            for c in range(2, 4):
                load_chunk(sp, 0, c)
            for k in range(2):
                sp.wait_ge(q_ps, PAIRS - 1 + k)
                load_tiles(k, k, out_tiles, out_w)
            with sp.Fori(1, KC // 2) as i:
                for k in range(2):
                    sp.wait_ge(br_ps, i * 2 + (k - 1))
                    load_tiles(k, i * 2 + k, out_tiles, out_w)
            for k in range(2):
                sp.wait_ge(br_ps, KC - 1 + k)
                src = w_mix_out[0][k * 4 * P:(k + 1) * 4 * P, :].rearrange("(c p) n -> p c n", p=P)
                sp.dma_start(wbuf[:, k, :].rearrange("p (c n) -> p c n", c=4), src).then_inc(mix_w, 16)
            sp.wait_ge(merged_made, KC)
            for c in range(4, 6):
                load_chunk(sp, 0, c)
            with sp.Fori(1, E) as e:
                for c in range(CHUNKS):
                    sp.wait_ge(chunk_used[c], e)
                    load_chunk(sp, e, c)
            sp.wait_ge(work_made, 1)
            n_work = sp.value_load(work[0:1, 32:33], min_val=0, max_val=EXTRA)
            with sp.Fori(0, EXTRA) as i:
                with sp.If(i < n_work):
                    e = sp.value_load(work[0:1, ds(i, 1)], min_val=0, max_val=E - 1)
                    for c in range(CHUNKS):
                        sp.wait_ge(chunk_used[c], i + E)
                        load_chunk(sp, e, c)
                with sp.Else():
                    sp.nop()
            for t in range(TT):
                sp.wait_ge(final_made, t + 1)
                sp.dma_start(out[0][t * P:(t + 1) * P, :], result[:, t, :]).then_inc(stored, 16)
            sp.wait_ge(stored, 16 * TT)

        @blk.gpsimd
        def _(pool):
            chain = Chain(pool, pool_once)
            chain.link(pool.memset(ident[:], 0.0))
            pool.affine_select(out=ident[:], in_=ident[:], compare_op=ALU.not_equal, fill=1.0, base=0,
                               pattern=[[-1, P]], channel_multiplier=1).then_inc(masks_made, 1)
            chain.link(pool.memset(ones[:], 1.0))
            pool.affine_select(out=before[:], in_=ones[:], compare_op=ALU.is_gt, fill=0.0, base=0,
                               pattern=[[1, P]], channel_multiplier=-1).then_inc(masks_made, 1)
            chain.link(pool.memset(mask0[:], 0.0))
            chain.link(pool.memset(mask1[:], 0.0))
            pool.affine_select(out=mask0[:, META:K0], in_=mask0[:, META:K0], compare_op=ALU.is_ge,
                               fill=MASKED, base=0, pattern=[[-1, P]],
                               channel_multiplier=1).then_inc(masks_made, 1)
            pool.affine_select(out=mask1[:, K0:K1], in_=mask1[:, K0:K1], compare_op=ALU.is_ge,
                               fill=MASKED, base=0, pattern=[[-1, P]],
                               channel_multiplier=1).then_inc(masks_made, 1)
            chain.link(pool.memset(neg_head[:], 0.0))
            pool.affine_select(out=neg_head[:], in_=neg_head[:], compare_op=ALU.not_equal, fill=-1.0,
                               base=0, pattern=[[-1, HEADS]], channel_multiplier=1).then_inc(masks_made, 1)
            pool.iota(iota[:], [[1, SEQ]], base=0, channel_multiplier=0,
                      allow_small_or_imprecise_dtypes=True).then_inc(masks_made, 1)

        @blk.scalar
        def _(act):
            vecs = [(COL_A, b_in[0, 0:OFF_F], 5 * KC), (COL_GA, b_in[0, OFF_GA:OFF_GB + D], 2 * KC),
                    (COL_NORM, attn_norm_g[0], KC), (COL_CB, conv_b[0], KC),
                    (COL_LG, conv_ln_g[0], KC), (COL_LB, conv_ln_b[0], KC)]
            for c0, v, n in vecs:
                act.dma_start(raw_cols[c0:c0 + n, :], v.rearrange("(c m) -> c m", m=P)).then_inc(rows_loaded, 16)
            act.dma_start(raw_taps, conv_w[0]).then_inc(raws_loaded, 16)
            act.dma_start(raw_bg, b_gu[0]).then_inc(raws_loaded, 16)
            act.dma_start(raw_bd, b_down[0]).then_inc(raws_loaded, 16)
            act.dma_start(wf[:], w_in0[:, OFF_F:OFF_GA].rearrange("(c p) m -> p c m", p=P)).then_inc(consts_loaded, 16)
            act.dma_start(bf[:], b_in[0, OFF_F:OFF_GA].rearrange("(h a) -> h a", a=1)).then_inc(consts_loaded, 16)
            act.dma_start(wr[:], router_w[0].rearrange("(c p) m -> p c m", p=P)).then_inc(consts_loaded, 16)
            act.dma_start(rb[:], router_b[0:1, :].to_broadcast([P, E])).then_inc(consts_loaded, 16)
            act.dma_start(gain[:], ffn_norm_g[0:1, :].to_broadcast([P, D])).then_inc(gain_loaded, 16)

            act.wait_ge(x_loaded, 16)
            for t in range(TT):
                nc.scalar.activation(x_n[:, t, :], x_tok[:, t, :], ACT.Square,
                                     accum_out=stat[:, t:t + 1]).then_inc(sq_x, 1)
            act.wait_ge(meta_loaded, 16)
            nc.scalar.activation(x_n[0:META, 2, :], x_meta, ACT.Square,
                                 accum_out=stat[0:META, 2:3]).then_inc(sq_x, 1)
            act.wait_ge(rms_var, 2)
            nc.scalar.activation(stat2[:, 0:2], stat2[:, 0:2], ACT.Sqrt).then_inc(rms_root, 1)
            nc.scalar.activation(stat2[0:META, 2:3], stat2[0:META, 2:3], ACT.Sqrt).then_inc(rms_root, 1)

            act.wait_ge(bias_ps, 2)
            nc.scalar.activation(table[:, :, TAB_BG:TAB_BD].rearrange("p e c -> p c e"),
                                 ps[:, 5, :].rearrange("p (c e) -> p c e", e=E), ACT.Copy).then_inc(bias_made, 1)
            nc.scalar.activation(table[:, :, TAB_BD:TABW].rearrange("p e c -> p c e"),
                                 ps[:, 4, 0:KC * E].rearrange("p (c e) -> p c e", e=E),
                                 ACT.Copy).then_inc(bias_made, 1)

            act.wait_ge(cols_made, 1)
            with act.Fori(0, KC // 2) as i:
                for k in range(2):
                    j = i * 2 + k
                    act.wait_ge(glu_ps, j + 1)
                    act.wait_ge(glu_made, j)
                    nc.scalar.activation(sig_b[:], ps[:, 4 * k + 1, 0:T], ACT.Sigmoid,
                                         bias=cols[:, ds(j + COL_B, 1)]).then_inc(sig_made, 1)
                    act.wait_ge(gates_ps, j + 1)
                    nc.scalar.activation(sigs[:, 0, ds(j, 1), :], ps[:, 4 * k + 2:4 * k + 3, 0:SEQ], ACT.Sigmoid,
                                         bias=cols[:, ds(j + COL_GA, 1)]).then_inc(gates_made, 1)
                    nc.scalar.activation(sigs[:, 1, ds(j, 1), :], ps[:, 4 * k + 3:4 * k + 4, 0:SEQ], ACT.Sigmoid,
                                         bias=cols[:, ds(j + COL_GB, 1)]).then_inc(gates_made, 1)

            act.wait_ge(f_abs, 1)
            nc.scalar.activation(ftmp[:, 1, :], ftmp[:, 1, :], ACT.Exp, scale=-1.0).then_inc(act_once, 1)
            act.wait_ge(act_once, 1)
            nc.scalar.activation(ftmp[:, 1, :], ftmp[:, 1, :], ACT.Ln, bias=1.0).then_inc(f_log, 1)

            act.wait_ge(centred, 1)
            nc.scalar.activation(squares, u_c, ACT.Square).then_inc(sq_made, 1)
            act.wait_ge(ln_var, 1)
            nc.scalar.activation(lnb[:, 1, :], lnb[:, 1, :], ACT.Sqrt).then_inc(ln_root, 1)
            act.wait_ge(ln_made, 1)
            for c in range(KC):
                nc.scalar.activation(squares[:, c, :], u_c[:, c, :], ACT.Sigmoid,
                                     bias=cols[:, COL_LB + c:COL_LB + c + 1],
                                     scale=cols[:, COL_LG + c:COL_LG + c + 1]).then_inc(silu_in, 1)

            def evacuate_kv(p, k):
                act.wait_ge(v_ps, p + 1)
                nc.scalar.activation(v_T, ps[:, 2, 0:T], ACT.Identity,
                                     bias=cols[:, ds(p + COL_V, 1)]).then_inc(vT_made, 1)
                act.wait_ge(k_ps, p + 1)
                nc.scalar.activation(k_s[k], ps[:, 1, 0:T], ACT.Identity,
                                     bias=cols[:, ds(p + COL_K, 1)]).then_inc(k_made, 1)
                act.wait_ge(vtr_ps, p + 1)
                nc.scalar.activation(v_s[k][0:META, 0:P], ps[0:META, 2, 0:P], ACT.Copy).then_inc(v_made, 1)
                nc.scalar.activation(v_s[k][:, P:3 * P], ps[:, 2, P:3 * P], ACT.Copy).then_inc(v_made, 1)

            def exponentials(p, h):
                act.wait_ge(max_made[h], p + 1)
                act.wait_ge(probsT_ps[h], p)
                nm = stat[:, 4 + 4 * h:6 + 4 * h]
                nc.scalar.activation(pr[h][:, 0:K0], sc[h][:, 0:K0], ACT.Exp, bias=nm[:, 0:1],
                                     accum_out=stat2[:, 4 + 4 * h:5 + 4 * h]).then_inc(exp_made[h], 1)
                nc.scalar.activation(pr[h][:, K0:SCW], sc[h][:, K0:SCW], ACT.Exp, bias=nm[:, 1:2],
                                     accum_out=stat2[:, 5 + 4 * h:6 + 4 * h]).then_inc(exp_made[h], 1)

            def evacuate_probs(p, h):
                act.wait_ge(probsT_ps[h], p + 1)
                nc.scalar.activation(pT[h], ps[:, 3 + h, 0:3 * P], ACT.Copy).then_inc(probsT[h], 1)
                nc.scalar.activation(pTm[h][0:META, :], ps[0:META, 5 + h, 0:SEQ], ACT.Copy).then_inc(probsT[h], 1)

            def pair(p, k, more):
                for h in range(2):
                    exponentials(p, h)
                if more:
                    evacuate_kv(p + 1, 1 - k)
                for h in range(2):
                    evacuate_probs(p, h)

            evacuate_kv(0, 0)
            with act.Fori(0, PAIRS // 2 - 1) as i:
                for k in range(2):
                    pair(i * 2 + k, k, True)
            pair(PAIRS - 2, 0, True)
            pair(PAIRS - 1, 1, False)

            for t in range(TT):
                act.wait_ge(h_ps, t + 1)
                nc.scalar.activation(squares_x, ps[:, 4 + 2 * t:6 + 2 * t, :].rearrange("p b n -> p (b n)"),
                                     ACT.Square, accum_out=stat[:, t:t + 1]).then_inc(ffn_sq, 1)
                act.wait_ge(ffn_sq, t + 1)
            act.wait_ge(ffn_var, 1)
            nc.scalar.activation(stat2[:, 0:TT], stat2[:, 0:TT], ACT.Sqrt).then_inc(ffn_root, 1)
            act.wait_ge(hn_made, TT)
            act.dma_start(gain[:], final_norm_g.rearrange("(a d) -> a d", a=1).to_broadcast([P, D])
                          ).then_inc(gain2_loaded, 16)
            for t in range(TT):
                act.wait_ge(hnT_ps, t + 1)
                nc.scalar.activation(hnT[:, :, t * P:(t + 1) * P],
                                     ps[:, 2 * t:2 * t + 2, :].rearrange("p b (c m) -> p (b c) m", m=P),
                                     ACT.Copy).then_inc(hnT_made, 1)
            act.wait_ge(top_made, TT)
            for t in range(TT):
                nc.scalar.activation(route[:, 6 * E + 8 * t:6 * E + 8 * t + TOPK],
                                     route[:, 5 * E + 8 * t:5 * E + 8 * t + TOPK], ACT.Exp,
                                     bias=stat[:, 8 + t:9 + t], accum_out=stat[:, 10 + t:11 + t]).then_inc(exps_made, 1)

            def scale_out(n):
                for h in range(2):
                    act.wait_ge(half_ps, n * 2 + h + 1)
                    act.wait_ge(scattered, n)
                    nc.scalar.activation(y_s[:, h * BANK:(h + 1) * BANK], ps[0:SLOTS, 2, :],
                                         ACT.Copy).then_inc(half_made, 1)
                act.wait_ge(G_ps, n + 1)
                nc.scalar.activation(G_s, ps[0:SLOTS, 2, 0:SEQ], ACT.Copy).then_inc(G_made, 1)

            def gathered(n):
                act.wait_ge(xg_ps, n + 1)
                nc.scalar.activation(xg, ps[:, 2, :], ACT.Copy).then_inc(xg_made, 1)

            def sigmoid(n):
                act.wait_ge(gate_ready, n + 1)
                nc.scalar.activation(sg, gate_m, ACT.Sigmoid, scale=ALPHA).then_inc(sg_made, 1)

            gathered(0)
            gathered(1)
            sigmoid(0)
            with act.Fori(1, E - 1) as n:
                scale_out(n - 1)
                gathered(n + 1)
                sigmoid(n)
            scale_out(E - 2)
            sigmoid(E - 1)
            scale_out(E - 1)
            act.wait_ge(work_made, 1)
            n_work = act.value_load(work[0:1, 32:33], min_val=0, max_val=EXTRA)
            with act.Fori(0, EXTRA) as i:
                with act.If(i < n_work):
                    gathered(i + E)
                    sigmoid(i + E)
                    scale_out(i + E)
                with act.Else():
                    act.nop()

            act.wait_ge(scattered, n_work + E)
            for t in range(TT):
                nc.scalar.activation(squares_x, ps[:, 4 + 2 * t:6 + 2 * t, :].rearrange("p b n -> p (b n)"),
                                     ACT.Square, accum_out=stat[:, t:t + 1]).then_inc(final_sq, 1)
                act.wait_ge(final_sq, t + 1)
            act.wait_ge(final_var, 1)
            nc.scalar.activation(stat2[:, 0:TT], stat2[:, 0:TT], ACT.Sqrt).then_inc(final_root, 1)

        @blk.vector
        def _(dve):
            V = nc.vector
            once = Chain(dve, dve_once)
            V.memset(glu[:, :, 0:TAPS - 1], 0.0).then_inc(pad_made, 1)
            dve.wait_ge(cols_ps, 1)
            V.tensor_copy(cols[:], ps[:, 7, 0:NCOLS]).then_inc(cols_made, 1)
            dve.wait_ge(sq_x, 3)
            V.tensor_scalar(stat2[:, 0:2], stat[:, 0:2], 1.0 / D, EPS, ALU.mult, ALU.add).then_inc(rms_var, 1)
            V.tensor_scalar(stat2[0:META, 2:3], stat[0:META, 2:3], 1.0 / D, EPS, ALU.mult, ALU.add).then_inc(rms_var, 1)
            dve.wait_ge(rms_root, 2)
            once.link(V.reciprocal(stat[:, 0:2], stat2[:, 0:2]))
            once.link(V.reciprocal(stat[0:META, 2:3], stat2[0:META, 2:3]))
            for t in range(TT):
                V.tensor_scalar(x_n[:, t, :], x_tok[:, t, :], stat[:, t:t + 1], None, ALU.mult).then_inc(xn_made, 1)
            V.tensor_scalar(x_n[0:META, 2, :], x_meta, stat[0:META, 2:3], None, ALU.mult).then_inc(xn_made, 1)
            dve.wait_ge(cols_made, 1)
            for c in range(KC):
                dve.wait_ge(xnT_ps, c + 1)
                V.tensor_scalar(xnT[:, c, :], ps[:, c % 4, 0:T], cols[:, COL_NORM + c:COL_NORM + c + 1],
                                None, ALU.mult).then_inc(xnT_made, 1)
            dve.wait_ge(taps_ps, 1)
            V.tensor_copy(taps[:], ps[:, 6, 0:KC * TAPS].rearrange("p (c w) -> p c w", w=TAPS)).then_inc(taps_made, 1)
            dve.wait_ge(taps_made, 1)
            dve.wait_ge(pad_made, 1)

            with dve.Fori(0, KC // 2) as i:
                for k in range(2):
                    j = i * 2 + k

                    def step(s):
                        return i * (2 * CONV_STEPS) + k * CONV_STEPS + s

                    dve.wait_ge(sig_made, j + 1)
                    V.scalar_tensor_tensor(out=glu[:, k, TAPS - 1:], in0=ps[:, 4 * k, 0:T],
                                           scalar=cols[:, ds(j + COL_A, 1)], in1=sig_b[:],
                                           op0=ALU.add, op1=ALU.mult).then_inc(glu_made, 1)
                    dve.wait_ge(glu_made, j + 1)
                    for w in range(TAPS):
                        src = glu[:, k, META + w:META + w + SEQ]
                        acc = conv_acc[:, w % 2, :]
                        tap = taps[:, ds(j, 1), w]
                        if w == 0:
                            dve.wait_ge(conv_step, step(0))
                            V.tensor_scalar(acc, src, tap, cols[:, ds(j + COL_CB, 1)],
                                            ALU.mult, ALU.add).then_inc(conv_step, 1)
                        elif w == 1:
                            V.tensor_scalar(acc, src, tap, None, ALU.mult).then_inc(conv_step, 1)
                        else:
                            dve.wait_ge(conv_step, step(w - 1))
                            V.scalar_tensor_tensor(out=acc, in0=src, scalar=tap, in1=acc,
                                                   op0=ALU.mult, op1=ALU.add).then_inc(conv_step, 1)
                    dve.wait_ge(conv_step, step(TAPS))
                    V.tensor_tensor(u_c[:, ds(j, 1), :], conv_acc[:, 0:1, :], conv_acc[:, 1:2, :],
                                    ALU.add).then_inc(conv_step, 1)

            dve.wait_ge(f_ps, 1)
            once.link(V.tensor_scalar(ftmp[:, 0, :], ps[0:HEADS, 7, 0:T], bf[:, 0:1], None, ALU.add))
            once.link(V.tensor_scalar(ftmp[:, 2, :], ftmp[:, 0, :], -1.0, None, ALU.mult))
            V.tensor_tensor(ftmp[:, 1, :], ftmp[:, 0, :], ftmp[:, 2, :], ALU.max).then_inc(f_abs, 1)
            dve.wait_ge(mean_ps, 1)
            once.link(V.tensor_scalar(lnb[:, 0, :], ps[:, 4, 0:SEQ], 1.0 / D, None, ALU.mult))
            V.tensor_tensor(u_c, u_c, lnb[:, 0:1, :].to_broadcast([P, KC, SEQ]), ALU.subtract).then_inc(centred, 1)
            dve.wait_ge(f_log, 1)
            once.link(V.scalar_tensor_tensor(out=ftmp[:, 2, :], in0=ftmp[:, 0, :], scalar=0.0,
                                             in1=ftmp[:, 1, :], op0=ALU.min, op1=ALU.subtract))
            once.link(V.memset(ftmp[:, 0, :], 1.0))
            V.tensor_tensor_scan(cum[:], ftmp[:, 0, :], ftmp[:, 2, :], 0.0, ALU.mult, ALU.add).then_inc(cum_made, 1)
            dve.wait_ge(var_ps, 1)
            V.tensor_scalar(lnb[:, 1, :], ps[:, 5, 0:SEQ], 1.0 / D, EPS, ALU.mult, ALU.add).then_inc(ln_var, 1)
            dve.wait_ge(cumT_ps, 1)
            V.tensor_copy(cum_q[:], ps[:, 6, 0:TT * HEADS].rearrange("p (t h) -> p t h", h=HEADS)).then_inc(cum_q_made, 1)
            dve.wait_ge(ln_root, 1)
            once.link(V.reciprocal(lnb[:, 1, :], lnb[:, 1, :]))
            V.tensor_tensor(u_c, u_c, lnb[:, 1:2, :].to_broadcast([P, KC, SEQ]), ALU.mult).then_inc(ln_made, 1)

            def evacuate_q(p, k):
                dve.wait_ge(q_ps, p + 1)
                V.tensor_scalar(q_s[k], ps[:, 0, 0:SEQ], cols[:, ds(p + COL_Q, 1)], DH ** -0.5,
                                ALU.add, ALU.mult).then_inc(q_made, 1)
                for h in range(2):
                    V.tensor_scalar(cd[k][h][0:HEADS, :], cum[:], neg_head[:, ds(p * 2 + h, 1)], None,
                                    ALU.mult).then_inc(cd_made, 1)

            PAIR_STEPS = 10
            pc = Chain(dve, dve_pair, PAIR_STEPS)

            def pair(p, k, more):
                pc.at(p)
                for h in range(2):
                    dve.wait_ge(scores[h], p + 1)
                    dve.wait_ge(exp_made[h], p * 2)
                    for t, (a, b, m) in enumerate(((0, K0, mask0), (K0, SCW, mask1))):
                        pc.link(V.scalar_tensor_tensor(out=sc[h][:, a:b], in0=ps[:, 3 + h, a:b],
                                                       scalar=cum_q[:, t, ds(p * 2 + h, 1)], in1=m[:],
                                                       op0=ALU.add, op1=ALU.add))
                    nm = stat[:, 4 + 4 * h:6 + 4 * h]
                    pc.link(V.tensor_reduce(nm[:, 0:1], sc[h][:, 0:K0], AX_X, ALU.max, negate=True))
                    V.tensor_reduce(nm[:, 1:2], sc[h][:, K0:SCW], AX_X, ALU.max,
                                    negate=True).then_inc(max_made[h], 1)
                for h in range(2):
                    dve.wait_ge(exp_made[h], p * 2 + 2)
                    pc.link(V.reciprocal(stat2[:, 6 + 4 * h:8 + 4 * h], stat2[:, 4 + 4 * h:6 + 4 * h]))
                    pc.link(V.tensor_scalar(pr[h][:, 0:K0], pr[h][:, 0:K0], stat2[:, 6 + 4 * h:7 + 4 * h],
                                            None, ALU.mult))
                    V.tensor_scalar(pr[h][:, K0:SCW], pr[h][:, K0:SCW], stat2[:, 7 + 4 * h:8 + 4 * h],
                                    None, ALU.mult).then_inc(probs[h], 1)
                assert pc.k == PAIR_STEPS
                if more:
                    evacuate_q(p + 1, 1 - k)
                dve.wait_ge(heads_ps, p + 1)
                V.tensor_scalar(attn_T[:, ds(p, 1), :], ps[:, 7:8, 0:SEQ], 1.0, None, ALU.mult).then_inc(heads_out, 1)

            dve.wait_ge(silu_in, KC)
            for c in range(KC):
                once.link(V.tensor_scalar(u_c[:, c, :], u_c[:, c, :], cols[:, COL_LG + c:COL_LG + c + 1],
                                          cols[:, COL_LB + c:COL_LB + c + 1], ALU.mult, ALU.add))
            once.link(V.tensor_tensor(u_c, u_c, squares, ALU.mult))
            dve.wait_ge(cum_made, 1)
            dve.wait_ge(cum_q_made, 1)
            dve.wait_ge(masks_made, 6)
            evacuate_q(0, 0)
            with dve.Fori(0, PAIRS // 2 - 1) as i:
                for k in range(2):
                    pair(i * 2 + k, k, True)
            pair(PAIRS - 2, 0, True)
            pair(PAIRS - 1, 1, False)

            with dve.Fori(0, KC // 2) as i:
                for k in range(2):
                    j = i * 2 + k
                    dve.wait_ge(br_ps, j + 1)
                    dve.wait_ge(merged_made, j)
                    V.tensor_tensor(tmp_m[0], sigs[:, 0, ds(j, 1), :].rearrange("p a t -> p (a t)"),
                                    ps[:, 2 * k, 0:SEQ], ALU.mult).then_inc(dve_merge, 1)
                    V.tensor_tensor(tmp_m[1], sigs[:, 1, ds(j, 1), :].rearrange("p a t -> p (a t)"),
                                    ps[:, 2 * k + 1, 0:SEQ], ALU.mult).then_inc(dve_merge, 1)
                    dve.wait_ge(dve_merge, j * 2 + 2)
                    V.tensor_tensor(merged[:, ds(j, 1), :].rearrange("p a t -> p (a t)"),
                                    tmp_m[0], tmp_m[1], ALU.add).then_inc(merged_made, 1)

            dve.wait_ge(ffn_sq, TT)
            V.tensor_scalar(stat2[:, 0:TT], stat[:, 0:TT], 1.0 / D, EPS, ALU.mult, ALU.add).then_inc(ffn_var, 1)
            dve.wait_ge(ffn_root, 1)
            once.link(V.reciprocal(stat[:, 0:TT], stat2[:, 0:TT]))
            dve.wait_ge(gain_loaded, 16)
            for t in range(TT):
                V.scalar_tensor_tensor(out=hn[:, t, :], in0=ps[:, 4 + 2 * t:6 + 2 * t, :].rearrange("p b n -> p (b n)"),
                                       scalar=stat[:, t:t + 1], in1=gain[:], op0=ALU.mult,
                                       op1=ALU.mult).then_inc(hn_made, 1)

            dve.wait_ge(consts_loaded, 64)
            for t in range(TT):
                lg = route[:, t * E:(t + 1) * E]
                top = route[:, 5 * E + 8 * t:5 * E + 8 * t + 8]
                idx_u = route_i[:, 0:8]
                idx = route[:, 7 * E + 8 * t:7 * E + 8 * t + 8]
                dve.wait_ge(logits_ps, t + 1)
                once.link(V.tensor_tensor(lg, ps[:, t, 0:E], rb[:], ALU.add))
                once.link(V.max(top, lg))
                once.link(V.tensor_scalar(stat[:, 8 + t:9 + t], top[:, 0:1], -1.0, None, ALU.mult))
                once.link(V.max_index(idx_u, top, lg))
                V.tensor_copy(idx, idx_u).then_inc(top_made, 1)
            dve.wait_ge(top_made, TT)
            dve.wait_ge(exps_made, TT)
            once.link(V.reciprocal(stat2[:, 10:10 + TT], stat[:, 10:10 + TT]))
            pick = route[:, 8 * E:12 * E]
            chosen = [route[:, (2 + t) * E:(3 + t) * E] for t in range(TT)]
            for t in range(TT):
                wts = route[:, 6 * E + 8 * t:6 * E + 8 * t + TOPK]
                idx = route[:, 7 * E + 8 * t:7 * E + 8 * t + 8]
                once.link(V.tensor_scalar(wts, wts, stat2[:, 10 + t:11 + t], None, ALU.mult))
                for c in range(TOPK):
                    once.link(V.tensor_scalar(pick[:, c * E:(c + 1) * E], iota[:, 0:E], idx[:, c:c + 1],
                                              None, ALU.is_equal))
                once.link(V.tensor_reduce(chosen[t], pick.rearrange("p (c e) -> p e c", c=TOPK), AX_X, ALU.add))
                for c in range(TOPK):
                    once.link(V.tensor_scalar(pick[:, c * E:(c + 1) * E], iota[:, 0:E], idx[:, c:c + 1],
                                              wts[:, c:c + 1], ALU.is_equal, ALU.mult))
                V.tensor_reduce(table[:, :, TAB_W + t:TAB_W + t + 1].rearrange("p e a -> p (e a)"),
                                pick.rearrange("p (c e) -> p e c", c=TOPK), AX_X, ALU.add).then_inc(picks_made, 1)
                dve.wait_ge(picks_made, t + 1)
            dve.wait_ge(pos_ps, 3)
            for t in range(TT):
                pos = pick[:, t * E:(t + 1) * E]
                once.link(V.scalar_tensor_tensor(out=pos, in0=ps[:, 3, t * E:(t + 1) * E], scalar=1.0,
                                                 in1=chosen[t], op0=ALU.add, op1=ALU.mult))
                V.tensor_scalar(table[:, :, TAB_POS + t:TAB_POS + t + 1].rearrange("p e a -> p (e a)"),
                                pos, -1.0, None, ALU.add).then_inc(table_made, 1)
            dve.wait_ge(table_made, TT)
            dve.wait_ge(bias_made, 2)

            y_chain = Chain(dve, dve_y, 1)
            w_chain = Chain(dve, dve_w, 1)
            s_chain = Chain(dve, dve_s, 1)
            a_chain = Chain(dve, dve_a, 4)

            def select(n, e, first):
                s_chain.at(n)
                dve.wait_ge(xg_ps, n)
                s_chain.link(V.tensor_scalar(cur_g, table[:, ds(e, 1), TAB_POS:TAB_BG].rearrange("p a c -> p (a c)"), 1.0, None, ALU.mult))
                for t in range(TT):
                    V.tensor_scalar(sel[:, t, :], iota[:, ds(first, SLOTS)], cur_g[:, TAB_POS + t:TAB_POS + t + 1],
                                    None, ALU.is_equal).then_inc(sel_made, 1)

            def select_weighted(n, e, first):
                w_chain.at(n)
                dve.wait_ge(G_ps, n)
                w_chain.link(V.tensor_scalar(cur_s, table[:, ds(e, 1), TAB_POS:TAB_BG].rearrange("p a c -> p (a c)"), 1.0, None, ALU.mult))
                for t in range(TT):
                    V.tensor_scalar(sel_w[:, t, :], iota[:, ds(first, SLOTS)], cur_s[:, TAB_POS + t:TAB_POS + t + 1],
                                    cur_s[:, TAB_W + t:TAB_W + t + 1], ALU.is_equal, ALU.mult).then_inc(sel_w_made, 1)

            def swiglu(n, e):
                a_chain.at(n)
                a_chain.link(V.tensor_scalar(cur_b[:], table[:, ds(e, 1), TAB_BG:TAB_BD].rearrange("p a c -> p (a c)"), 1.0, None, ALU.mult))
                dve.wait_ge(gu_ps, n + 1)
                bias = [cur_b[:, h * KC:(h + 1) * KC].rearrange("p (c a) -> p c a", a=1).to_broadcast([P, KC, SLOTS])
                        for h in range(2)]
                a_chain.link(V.tensor_tensor(gate_b.rearrange("p (c s) -> p c s", c=KC),
                                             ps[:, 0, :].rearrange("p (c s) -> p c s", c=KC), bias[0], ALU.add))
                V.tensor_tensor(up_b.rearrange("p (c s) -> p c s", c=KC),
                                ps[:, 1, :].rearrange("p (c s) -> p c s", c=KC), bias[1], ALU.add).then_inc(gu_read, 1)
                V.tensor_scalar(gate_m, gate_b, LIMIT, None, ALU.min).then_inc(gate_ready, 1)
                dve.wait_ge(gu_read, n + 1)
                a_chain.link(V.tensor_scalar(up_b, up_b, LIMIT, -LIMIT, ALU.min, ALU.max))
                dve.wait_ge(sg_made, n + 1)
                a_chain.link(V.tensor_tensor(gs, gate_m, sg, ALU.mult))
                V.scalar_tensor_tensor(out=act_s.rearrange("p c s -> p (c s)"), in0=up_b, scalar=1.0, in1=gs,
                                       op0=ALU.add, op1=ALU.mult).then_inc(act_made, 1)
                assert a_chain.k == a_chain.per_round

            def add_down_bias(n, e):
                y_chain.at(n)
                y_chain.link(V.tensor_scalar(cur_d[:], table[:, ds(e, 1), TAB_BD:TABW].rearrange("p a c -> p (a c)"), 1.0, None, ALU.mult))
                dve.wait_ge(y_ps, n + 1)
                dve.wait_ge(half_ps, n * 2)
                V.tensor_tensor(yT.rearrange("p (c s) -> p c s", c=KC),
                                ps[:, 3, :].rearrange("p (c s) -> p c s", c=KC),
                                cur_d[:].rearrange("p (c a) -> p c a", a=1).to_broadcast([P, KC, SLOTS]),
                                ALU.add).then_inc(yT_made, 1)

            select(0, 0, 0)
            select(1, 1, 0)

            n_more = (BLOCKS - 1) * E
            lst = [gates[0:1, a * n_more:(a + 1) * n_more] for a in range(5)]
            active, rank, of_e, of_s = lst[0:4]
            counts = lst[4][:, 0:E]
            match = gates[0:1, 5 * n_more:(5 + EXTRA) * n_more].rearrange("p (r i) -> p r i", i=n_more)
            assert (5 + EXTRA) * n_more <= 6 * W
            once.link(V.tensor_copy(counts, ps[0:1, 3, TT * E:TT * E + E]))
            for b in range(1, BLOCKS):
                part = slice((b - 1) * E, b * E)
                once.link(V.tensor_scalar(active[:, part], counts, float(b * SLOTS), None, ALU.is_gt))
                once.link(V.tensor_copy(of_e[:, part], iota[0:1, 0:E]))
                once.link(V.memset(of_s[:, part], float(b * SLOTS)))
            once.link(V.tensor_tensor_scan(rank, ones[0:1, 0:n_more], active, 0.0, ALU.mult, ALU.add))
            once.link(V.memset(work_f[:], 0.0))
            once.link(V.tensor_copy(work_f[:, 32:33], rank[:, n_more - 1:n_more]))
            once.link(V.tensor_tensor(rank, rank, active, ALU.mult))
            shape = [1, EXTRA, n_more]
            for a, values in enumerate((of_e, of_s)):
                once.link(V.tensor_tensor(match, rank.rearrange("p (a i) -> p a i", a=1).to_broadcast(shape),
                                          iota[0:1, 1:1 + EXTRA].rearrange("p (r a) -> p r a", a=1).to_broadcast(shape),
                                          ALU.is_equal))
                once.link(V.tensor_tensor(match, match, values.rearrange("p (a i) -> p a i", a=1).to_broadcast(shape),
                                          ALU.mult))
                once.link(V.tensor_reduce(work_f[:, 16 * a:16 * a + EXTRA], match, AX_X, ALU.add))
            V.tensor_copy(work[:], work_f[:]).then_inc(work_made, 1)
            dve.wait_ge(work_made, 1)

            swiglu(0, 0)
            with dve.Fori(1, E - 1) as n:
                add_down_bias(n - 1, n - 1)
                select_weighted(n - 1, n - 1, 0)
                select(n + 1, n + 1, 0)
                swiglu(n, n)
            add_down_bias(E - 2, E - 2)
            select_weighted(E - 2, E - 2, 0)
            swiglu(E - 1, E - 1)
            add_down_bias(E - 1, E - 1)
            select_weighted(E - 1, E - 1, 0)
            n_work = dve.value_load(work[0:1, 32:33], min_val=0, max_val=EXTRA)
            with dve.Fori(0, EXTRA) as i:
                with dve.If(i < n_work):
                    e = dve.value_load(work[0:1, ds(i, 1)], min_val=0, max_val=E - 1)
                    first = dve.value_load(work[0:1, ds(i + 16, 1)], min_val=0, max_val=SEQ - SLOTS)
                    select(i + E, e, first)
                    swiglu(i + E, e)
                    add_down_bias(i + E, e)
                    select_weighted(i + E, e, first)
                with dve.Else():
                    dve.nop()

            dve.wait_ge(final_sq, TT)
            V.tensor_scalar(stat2[:, 0:TT], stat[:, 0:TT], 1.0 / D, EPS, ALU.mult, ALU.add).then_inc(final_var, 1)
            dve.wait_ge(final_root, 1)
            once.link(V.reciprocal(stat[:, 0:TT], stat2[:, 0:TT]))
            dve.wait_ge(gain2_loaded, 16)
            for t in range(TT):
                V.scalar_tensor_tensor(out=result[:, t, :],
                                       in0=ps[:, 4 + 2 * t:6 + 2 * t, :].rearrange("p b n -> p (b n)"),
                                       scalar=stat[:, t:t + 1], in1=gain[:], op0=ALU.mult,
                                       op1=ALU.mult).then_inc(final_made, 1)

        @blk.tensor
        def _(pe):
            mm = nc.tensor.matmul

            pe.wait_ge(masks_made, 1)
            pe.wait_ge(rows_loaded, 16 * 6)
            nc.tensor.transpose(ps[:, 7, 0:NCOLS], raw_cols, ident[0:NCOLS, 0:NCOLS]).then_inc(cols_ps, 1)
            pe.wait_ge(raws_loaded, 16 * 3)
            for c in range(KC):
                last = nc.tensor.transpose(ps[:, 6, c * TAPS:(c + 1) * TAPS], raw_taps[:, c * P:(c + 1) * P],
                                           ident[0:TAPS, 0:TAPS])
            last.then_inc(taps_ps, 1)
            for c in range(GU // P):
                last = nc.tensor.transpose(ps[:, 5, c * E:(c + 1) * E], raw_bg[:, c * P:(c + 1) * P], ident[0:E, 0:E])
            last.then_inc(bias_ps, 1)
            for c in range(KC):
                last = nc.tensor.transpose(ps[:, 4, c * E:(c + 1) * E], raw_bd[:, c * P:(c + 1) * P], ident[0:E, 0:E])
            last.then_inc(bias_ps, 1)
            pe.wait_ge(xn_made, 3)
            for c in range(KC):
                if c >= 4:
                    pe.wait_ge(xnT_made, c - 3)
                for t in range(TT):
                    nc.tensor.transpose(ps[:, c % 4, META + t * P:META + (t + 1) * P],
                                        x_n[:, t, c * P:(c + 1) * P], ident[:])
                nc.tensor.transpose(ps[:, c % 4, 0:META], x_n[0:META, 2, c * P:(c + 1) * P],
                                    ident[0:META, 0:META]).then_inc(xnT_ps, 1)
            pe.wait_ge(xnT_made, KC)
            pe.wait_ge(cols_made, 1)
            pe.wait_ge(taps_made, 1)
            pe.wait_ge(bias_made, 2)

            def project(bank, w, act, n):
                for c in range(KC):
                    last = mm(ps[:, bank, 0:n], w[:, c, :], act[:, c, :], start=(c == 0), stop=(c == KC - 1))
                return last

            x_all, x_seq = xnT[:], xnT[:, :, META:T]
            with pe.Fori(0, KC // 2) as i:
                for k in range(2):
                    pe.wait_ge(glu_w[k], i * 64 + 64)
                    pe.wait_ge(sig_made, i * 2 + k)
                    project(4 * k + 1, fill(k, 1), x_all, T)
                    project(4 * k, fill(k, 0), x_all, T).then_inc(glu_ps, 1)
                    project(4 * k + 2, fill(k, 2), x_seq, SEQ)
                    project(4 * k + 3, fill(k, 3), x_seq, SEQ).then_inc(gates_ps, 1)

            pe.wait_ge(consts_loaded, 64)
            pe.wait_ge(gates_made, 2 * KC)
            for c in range(KC):
                last = mm(ps[0:HEADS, 7, 0:T], wf[:, c, :], xnT[:, c, :], start=(c == 0), stop=(c == KC - 1))
            last.then_inc(f_ps, 1)
            pe.wait_ge(masks_made, 2)
            pe.wait_ge(glu_made, KC)
            pe.wait_ge(conv_step, KC * CONV_STEPS)
            for c in range(KC):
                last = mm(ps[:, 4, 0:SEQ], ones[:], u_c[:, c, :], start=(c == 0), stop=(c == KC - 1))
            last.then_inc(mean_ps, 1)
            pe.wait_ge(sq_made, 1)
            for c in range(KC):
                last = mm(ps[:, 5, 0:SEQ], ones[:], squares[:, c, :], start=(c == 0), stop=(c == KC - 1))
            last.then_inc(var_ps, 1)
            pe.wait_ge(cum_made, 1)
            for t in range(TT):
                last = nc.tensor.transpose(ps[:, 6, t * HEADS:(t + 1) * HEADS],
                                           cum[:, META + t * P:META + (t + 1) * P], ident[0:HEADS, 0:HEADS])
            last.then_inc(cumT_ps, 1)

            def qkv(p, k, i):
                pe.wait_ge(qkv_w[k], i * 48 + 48)
                pe.wait_ge(v_made, p * 2)
                project(2, fill(k, 2), x_all, T).then_inc(v_ps, 1)
                pe.wait_ge(k_made, p)
                project(1, fill(k, 1), x_all, T).then_inc(k_ps, 1)
                pe.wait_ge(q_made, p)
                project(0, fill(k, 0), x_seq, SEQ).then_inc(q_ps, 1)
                pe.wait_ge(vT_made, p + 1)
                nc.tensor.transpose(ps[0:META, 2, 0:P], v_T[:, 0:META], ident[:])
                nc.tensor.transpose(ps[:, 2, P:2 * P], v_T[:, META:META + P], ident[:])
                nc.tensor.transpose(ps[:, 2, 2 * P:3 * P], v_T[:, META + P:T], ident[:]).then_inc(vtr_ps, 1)

            def attend(p, k, more):
                pe.wait_ge(q_made, p + 1)
                pe.wait_ge(k_made, p + 1)
                for h in range(2):
                    r = slice(h * DH, (h + 1) * DH)
                    pe.wait_ge(cd_made, p * 2 + h + 1)
                    mm(ps[:, 3 + h, 0:K0], q_s[k][r, 0:P], k_s[k][r, 0:K0], start=True, stop=False)
                    mm(ps[:, 3 + h, 0:K0], ones[0:HEADS, :], cd[k][h][0:HEADS, 0:K0], start=False, stop=True)
                    mm(ps[:, 3 + h, K0:SCW], q_s[k][r, P:2 * P], k_s[k][r, :], start=True, stop=False)
                    mm(ps[:, 3 + h, K0:SCW], ones[0:HEADS, :], cd[k][h][0:HEADS, :],
                       start=False, stop=True).then_inc(scores[h], 1)
                if more is not None:
                    qkv(p + 1, 1 - k, more)
                for h in range(2):
                    pe.wait_ge(probs[h], p + 1)
                    pe.wait_ge(probsT[h], p * 2)
                    b = 3 + h
                    nc.tensor.transpose(ps[:, b, 0:P], pr[h][:, META:K0], ident[:])
                    nc.tensor.transpose(ps[:, b, P:2 * P], pr[h][:, K0 + META:K0 + K0], ident[:])
                    nc.tensor.transpose(ps[:, b, 2 * P:3 * P], pr[h][:, K0 + K0:SCW], ident[:])
                    nc.tensor.transpose(ps[0:META, 5 + h, 0:P], pr[h][:, 0:META], ident[:])
                    nc.tensor.transpose(ps[0:META, 5 + h, P:2 * P], pr[h][:, K0:K0 + META],
                                        ident[:]).then_inc(probsT_ps[h], 1)
                pe.wait_ge(v_made, p * 2 + 2)
                pe.wait_ge(heads_out, p)
                for h in range(2):
                    pe.wait_ge(probsT[h], p * 2 + 2)
                    o = ps[h * DH:(h + 1) * DH, 7, :]
                    hs = slice(h * DH, (h + 1) * DH)
                    for t in range(TT):
                        q = slice(t * P, (t + 1) * P)
                        mm(o[:, q], v_s[k][:, P + h * DH:P + (h + 1) * DH], pT[h][:, q], start=True, stop=False)
                        if t == 1:
                            mm(o[:, q], v_s[k][:, 2 * P + h * DH:2 * P + (h + 1) * DH], pT[h][:, SEQ:3 * P],
                               start=False, stop=False)
                        last = mm(o[:, q], v_s[k][0:META, hs], pTm[h][0:META, q], start=False, stop=True)
                last.then_inc(heads_ps, 1)

            qkv(0, 0, 0)
            with pe.Fori(0, PAIRS // 2 - 1) as i:
                for k in range(2):
                    attend(i * 2 + k, k, i + k)
            attend(PAIRS - 2, 0, PAIRS // 2 - 1)
            attend(PAIRS - 1, 1, None)

            pe.wait_ge(heads_out, PAIRS)
            with pe.Fori(0, KC // 2) as i:
                for k in range(2):
                    pe.wait_ge(out_w[k], i * 32 + 32)
                    pe.wait_ge(merged_made, i * 2)
                    project(2 * k, fill(k, 0), u_c, SEQ)
                    project(2 * k + 1, fill(k, 1), attn_T, SEQ).then_inc(br_ps, 1)

            pe.wait_ge(merged_made, KC)
            pe.wait_ge(mix_w, 32)
            pe.wait_ge(x_loaded, 16)
            for t in range(TT):
                for b in range(2):
                    acc = ps[:, 4 + 2 * t + b, :]
                    mm(acc, ident[:], x_tok[:, t, b * BANK:(b + 1) * BANK], start=True, stop=False)
                    for c in range(KC):
                        w = wbuf[:, c // 4, (c % 4) * D + b * BANK:(c % 4) * D + (b + 1) * BANK]
                        last = mm(acc, merged[:, c, t * P:(t + 1) * P], w, start=False, stop=(c == KC - 1))
                last.then_inc(h_ps, 1)

            for t in range(TT):
                pe.wait_ge(hn_made, t + 1)
                for c in range(KC):
                    last = nc.tensor.transpose(ps[:, 2 * t + c // 4, (c % 4) * P:(c % 4 + 1) * P],
                                               hn[:, t, c * P:(c + 1) * P], ident[:])
                last.then_inc(hnT_ps, 1)
            for t in range(TT):
                pe.wait_ge(hnT_made, t + 1)
                for c in range(KC):
                    last = mm(ps[:, t, 0:E], hnT[:, c, t * P:(t + 1) * P], wr[:, c, :],
                              start=(c == 0), stop=(c == KC - 1))
                last.then_inc(logits_ps, 1)
            pe.wait_ge(picks_made, TT)
            pos = ps[:, 3, :]
            mm(pos[:, 0:E], before[:], route[:, 2 * E:3 * E], start=True, stop=True).then_inc(pos_ps, 1)
            mm(pos[:, E:2 * E], ones[:], route[:, 2 * E:3 * E], start=True, stop=False)
            mm(pos[:, E:2 * E], before[:], route[:, 3 * E:4 * E], start=False, stop=True).then_inc(pos_ps, 1)
            mm(pos[0:1, 2 * E:3 * E], ones[:, 0:1], route[:, 2 * E:3 * E], start=True, stop=False)
            mm(pos[0:1, 2 * E:3 * E], ones[:, 0:1], route[:, 3 * E:4 * E], start=False, stop=True).then_inc(pos_ps, 1)

            def gather(n):
                pe.wait_ge(sel_made, n * 2 + 2)
                for c in range(KC):
                    for t in range(TT):
                        last = mm(ps[:, 2, c * SLOTS:(c + 1) * SLOTS], hn[:, t, c * P:(c + 1) * P], sel[:, t, :],
                                  start=(t == 0), stop=(t == TT - 1))
                last.then_inc(xg_ps, 1)

            def gate_up(n, q):
                if q == 0:
                    pe.wait_ge(xg_made, n + 1)
                    pe.wait_ge(gu_read, n)
                pe.wait_ge(chunk_w[q], n * 16 + 16)
                w = ring[:, q, :].rearrange("p (c n) -> p c n", c=2)
                for cc in range(2):
                    c = 2 * q + cc
                    for f in range(GU // P):
                        last = mm(ps[:, f // KC, (f % KC) * SLOTS:(f % KC + 1) * SLOTS],
                                  w[:, cc, f * P:(f + 1) * P], xg[:, c * SLOTS:(c + 1) * SLOTS],
                                  start=(c == 0 and f % KC == 0), stop=(c == KC - 1), skip_group_check=True)
                last.then_inc(chunk_used[q], 1)

            def down(n):
                pe.wait_ge(act_made, n + 1)
                pe.wait_ge(yT_made, n)
                for q in range(GU_CHUNKS, CHUNKS):
                    pe.wait_ge(chunk_w[q], n * 16 + 16)
                    w = ring[:, q, :].rearrange("p (c n) -> p c n", c=4)
                    for cc in range(4):
                        c = 4 * (q - GU_CHUNKS) + cc
                        for d in range(KC):
                            last = mm(ps[:, 3, d * SLOTS:(d + 1) * SLOTS], w[:, cc, d * P:(d + 1) * P],
                                      act_s[:, c, :], start=(c == 0 and d == 0), stop=(c == KC - 1),
                                      skip_group_check=True)
                    last.then_inc(chunk_used[q], 1)

            def turn_half(n, h):
                pe.wait_ge(yT_made, n + 1)
                if h == 1:
                    pe.wait_ge(half_made, n * 2 + 1)
                pe.sem_inc(turn_begun, 1)
                for d in range(4):
                    last = nc.tensor.transpose(ps[0:SLOTS, 2, d * P:(d + 1) * P],
                                               yT[:, (4 * h + d) * SLOTS:(4 * h + d + 1) * SLOTS], ident[:])
                last.then_inc(half_ps, 1)

            def turn_weights(n):
                pe.wait_ge(sel_w_made, n * 2 + 2)
                pe.wait_ge(half_made, n * 2 + 2)
                pe.sem_inc(turn_begun, 1)
                for t in range(TT):
                    last = nc.tensor.transpose(ps[0:SLOTS, 2, t * P:(t + 1) * P], sel_w[:, t, :], ident[:])
                last.then_inc(G_ps, 1)

            def scatter(n):
                pe.wait_ge(G_made, n + 1)
                for t in range(TT):
                    for b in range(2):
                        last = mm(ps[:, 4 + 2 * t + b, :], G_s[:, t * P:(t + 1) * P], y_s[:, b * BANK:(b + 1) * BANK],
                                  start=False, stop=True, skip_group_check=True)
                last.then_inc(scattered, 1)

            gather(0)
            for q in range(GU_CHUNKS):
                gate_up(0, q)
            pe.wait_ge(xg_made, 1)
            gather(1)
            down(0)
            with pe.Fori(1, E - 1) as n:
                gate_up(n, 0)
                turn_half(n - 1, 0)
                gate_up(n, 1)
                turn_half(n - 1, 1)
                gate_up(n, 2)
                turn_weights(n - 1)
                gate_up(n, 3)
                pe.wait_ge(G_made, n)
                gather(n + 1)
                scatter(n - 1)
                down(n)
            gate_up(E - 1, 0)
            turn_half(E - 2, 0)
            gate_up(E - 1, 1)
            turn_half(E - 2, 1)
            gate_up(E - 1, 2)
            turn_weights(E - 2)
            gate_up(E - 1, 3)
            scatter(E - 2)
            down(E - 1)
            turn_half(E - 1, 0)
            turn_half(E - 1, 1)
            turn_weights(E - 1)
            scatter(E - 1)
            pe.wait_ge(work_made, 1)
            n_work = pe.value_load(work[0:1, 32:33], min_val=0, max_val=EXTRA)
            with pe.Fori(0, EXTRA) as i:
                with pe.If(i < n_work):
                    gather(i + E)
                    for q in range(GU_CHUNKS):
                        gate_up(i + E, q)
                    down(i + E)
                    turn_half(i + E, 0)
                    turn_half(i + E, 1)
                    turn_weights(i + E)
                    scatter(i + E)
                with pe.Else():
                    pe.nop()


_INS = ['x', 'meta_tokens', 'attn_norm_g', 'w_in', 'b_in', 'conv_w', 'conv_b', 'conv_ln_g', 'conv_ln_b',
        'w_conv_out', 'w_attn_out', 'w_mix_out', 'ffn_norm_g', 'router_w', 'router_b', 'w_gu', 'b_gu',
        'w_down', 'b_down', 'final_norm_g']
_OUTS = [((1, SEQ, D), 'float32')]


def kernel(**inputs):
    import numpy as _np
    import concourse.bacc as _bacc
    from concourse import mybir as _mybir
    from concourse.bass_utils import run_bass_kernel_spmd as _run

    nc = _bacc.Bacc("TRN2", target_bir_lowering=False, num_devices=1)
    arrays, args = {}, []
    for name in _INS:
        a = _np.ascontiguousarray(inputs[name])
        arrays[f"in_{name}_dram"] = a
        args.append(nc.dram_tensor(f"in_{name}_dram", a.shape, _mybir.dt.from_np(a.dtype), kind="ExternalInput").ap())
    for i, (shape, dtype) in enumerate(_OUTS):
        dt = _mybir.dt.from_np(_np.dtype(dtype))
        args.append(nc.dram_tensor(f"out_{i}_dram", shape, dt, kind="ExternalOutput").ap())
    build(nc, *args)
    r = _run(nc, [arrays], core_ids=[0])
    return _np.asarray(r.results[0]["out_0_dram"])
```

```python
from contextlib import ExitStack

import concourse.bass as bass
from concourse import mybir
from concourse.alu_op_type import AluOpType as ALU

ACT = mybir.ActivationFunctionType
AX_X = mybir.AxisListType.X
F32 = mybir.dt.float32
I32 = mybir.dt.int32
U32 = mybir.dt.uint32
ds = bass.ds

P = 128
BANK = 512
D = 1024
KC = D // P
META = 16
SEQ = 256
T = META + SEQ
TT = SEQ // P
TAPS = 31
HEADS, DH = 16, 64
PAIRS = HEADS // 2
E, TOPK = 32, 4
GU = 2 * D
SLOTS = 64
BLOCKS = SEQ // SLOTS
EXTRA = (SEQ * TOPK - 1) // SLOTS
EPS = 1e-5
ALPHA, LIMIT = 1.702, 7.0
MASKED = -1.0e30

OFF_A, OFF_B = 0, D
OFF_Q, OFF_K, OFF_V = 2 * D, 3 * D, 4 * D
OFF_F = 5 * D
OFF_GA = OFF_F + HEADS
OFF_GB = OFF_GA + D
COL_A, COL_B, COL_Q, COL_K, COL_V, COL_GA, COL_GB, COL_NORM, COL_CB, COL_LG, COL_LB = (
    KC * n for n in range(11))
NCOLS = 11 * KC
CONV_STEPS = TAPS + 1
K0, K1 = META + P, T
SCW = K0 + K1
CHUNK = 4 * D
GU_CHUNKS, CHUNKS = 4, 6


class Chain:

    def __init__(self, eng, sem, per_round=0):
        self.eng, self.sem, self.per_round, self.base, self.k = eng, sem, per_round, 0, 0

    def at(self, n):
        self.base, self.k = n * self.per_round, 0

    def link(self, ins):
        self.k += 1
        ins.then_inc(self.sem, 1)
        self.eng.wait_ge(self.sem, self.base + self.k)


def build(nc, x, meta_tokens, attn_norm_g, w_in, b_in, conv_w, conv_b, conv_ln_g, conv_ln_b,
          w_conv_out, w_attn_out, w_mix_out, ffn_norm_g, router_w, router_b, w_gu, b_gu,
          w_down, b_down, final_norm_g, out):
    ctx = ExitStack()
    with ctx:
        def sb(name, shape, dt=F32):
            return ctx.enter_context(nc.sbuf_tensor(name, shape, dt))

        def sem(name):
            return ctx.enter_context(nc.semaphore(name))

        ps = ctx.enter_context(nc.psum_tensor("ps", [P, 8, BANK], F32))

        ring = sb("ring", [P, CHUNKS, CHUNK])
        wbuf = sb("wbuf", [P, 2, 4 * D])
        x_tok = sb("x_tok", [P, TT, D])
        xn = sb("xn", [P, 3 * D])
        xnT = sb("xnT", [P, KC, T])
        u = sb("u", [P, KC * SEQ])
        gates = sb("gates", [P, 2 * KC * SEQ])
        gain = sb("gain", [P, D])
        glu = sb("glu", [P, 2, TAPS - 1 + T])
        sig_b = sb("sig_b", [P, T])
        conv_acc = sb("conv_acc", [P, 2, SEQ])
        cols = sb("cols", [P, NCOLS])
        taps = sb("taps", [P, KC, TAPS])
        slot_of = sb("slot_of", [P, TT, E])
        weight = sb("weight", [P, TT, P])
        ident = sb("ident", [P, P])
        ones = sb("ones", [P, P])
        before = sb("before", [P, P])
        mask0 = sb("mask0", [P, K0])
        mask1 = sb("mask1", [P, K1])
        neg_head = sb("neg_head", [HEADS, HEADS])
        iota = sb("iota", [P, SEQ])
        wf = sb("wf", [P, KC, HEADS])
        wr = sb("wr", [P, KC, E])
        rb = sb("rb", [P, E])
        bf = sb("bf", [HEADS, 1])
        cum = sb("cum", [HEADS, T])
        cum_q = sb("cum_q", [P, TT, HEADS])
        stat = sb("stat", [P, 16])
        stat2 = sb("stat2", [P, 16])
        lnb = sb("lnb", [P, 2, SEQ])
        route = sb("route", [P, 12 * E])
        route_i = sb("route_i", [P, 8], U32)
        work_f = sb("work_f", [1, 3 * 16])
        work = sb("work", [1, 3 * 16], I32)

        x_n = xn[:].rearrange("p (t d) -> p t d", t=3)
        u_c = u[:].rearrange("p (c t) -> p c t", c=KC)
        sigs = gates[:].rearrange("p (g c t) -> p g c t", g=2, c=KC)
        raw_cols = u[0:NCOLS, 0:P]
        raw_taps = u[0:TAPS, D:2 * D]
        x_meta = gates[0:META, GU + D:GU + 2 * D]
        attn_T = xn[:, 0:KC * SEQ].rearrange("p (c t) -> p c t", c=KC)
        squares = attn_T
        merged = xnT[:].rearrange("p c t -> p (c t)")[:, 0:KC * SEQ].rearrange("p (c t) -> p c t", c=KC)
        spare = [0]

        def lent(n):
            a = spare[0]
            spare[0] += n
            assert spare[0] <= 2 * CHUNK
            return ring[:, 4:6, :].rearrange("p a b -> p (a b)")[:, a:a + n]

        q_s = [[lent(SEQ) for _ in range(2)] for _ in range(2)]
        k_s = [[lent(T) for _ in range(2)] for _ in range(2)]
        v_s = [lent(3 * P) for _ in range(2)]
        v_T = lent(T)
        sc = [lent(SCW) for _ in range(2)]
        pr = [lent(SCW) for _ in range(2)]
        pT = [lent(3 * P) for _ in range(2)]
        pTm = [lent(SEQ) for _ in range(2)]
        tmp_m = [lent(SEQ) for _ in range(2)]
        ftmp = lent(3 * T)[0:HEADS, :].rearrange("p (a t) -> p a t", a=3)
        hn = xn[:, 0:TT * D].rearrange("p (t d) -> p t d", t=TT)
        hnT = wbuf[:, 0, 0:KC * SEQ].rearrange("p (c t) -> p c t", c=KC)
        squares_x = u[:, 0:D]
        result = wbuf[:, 1, D:3 * D].rearrange("p (t d) -> p t d", t=TT)
        moe = [gates[:, a * BANK:(a + 1) * BANK] for a in range(8)]
        gate_m, up_m, sg, gu_m, act_s, act_T, xg, xT = moe
        bias_gu = wbuf[:, 0, GU:2 * GU]
        bias_down = wbuf[:, 1, 3 * D:4 * D]
        y_s = u[:, 0:BANK]
        G_s = u[:, BANK:2 * BANK]
        sel = u[:, 1024:1024 + TT * SLOTS].rearrange("p (t s) -> p t s", t=TT)
        sel_w = u[:, 1152:1152 + TT * 3 * SLOTS].rearrange("p (t s) -> p t s", t=TT)
        sel_e = u[:, 1536:1536 + SLOTS]
        weight_T = u[:, 1600:1600 + SEQ]

        x_loaded, meta_loaded, rows_loaded = sem("x_loaded"), sem("meta_loaded"), sem("rows_loaded")
        consts_loaded, gain_loaded, gain2_loaded = sem("consts_loaded"), sem("gain_loaded"), sem("gain2_loaded")
        raws_loaded = sem("raws_loaded")
        glu_w = [sem(f"glu_w{k}") for k in range(2)]
        qkv_w = [sem(f"qkv_w{k}") for k in range(2)]
        out_w = [sem(f"out_w{k}") for k in range(2)]
        mix_w = sem("mix_w")
        chunk_w = [sem(f"chunk_w{c}") for c in range(CHUNKS)]
        chunk_used = [sem(f"chunk_used{c}") for c in range(CHUNKS)]
        stored = sem("stored")
        masks_made, tri = sem("masks_made"), sem("tri")
        cols_ps, cols_made = sem("cols_ps"), sem("cols_made")
        taps_ps, taps_made = sem("taps_ps"), sem("taps_made")
        pads_made, bias_zero, bias_loaded = sem("pads_made"), sem("bias_zero"), sem("bias_loaded")
        sq_x, sq_meta, rms_var, rms_root, xn_made = (
            sem("sq_x"), sem("sq_meta"), sem("rms_var"), sem("rms_root"), sem("xn_made"))
        xnT_ps, xnT_made = sem("xnT_ps"), sem("xnT_made")
        pad_made = sem("pad_made")
        glu_ps, sig_made, glu_made, conv_step = sem("glu_ps"), sem("sig_made"), sem("glu_made"), sem("conv_step")
        gates_ps, gates_made = sem("gates_ps"), sem("gates_made")
        mean_ps, centred, sq_made, var_ps = sem("mean_ps"), sem("centred"), sem("sq_made"), sem("var_ps")
        ln_var, ln_root, ln_made, silu_in, silu_made = (
            sem("ln_var"), sem("ln_root"), sem("ln_made"), sem("silu_in"), sem("silu_made"))
        f_ps, f_abs, f_log, cum_made, cumT_ps, cum_q_made = (
            sem("f_ps"), sem("f_abs"), sem("f_log"), sem("cum_made"), sem("cumT_ps"), sem("cum_q_made"))
        q_ps, k_ps, v_ps = sem("q_ps"), sem("k_ps"), sem("v_ps")
        q_made, k_made, vT_made, vtr_ps, v_made = (
            sem("q_made"), sem("k_made"), sem("vT_made"), sem("vtr_ps"), sem("v_made"))
        kc_made = sem("kc_made")
        scores = [sem(f"scores{h}") for h in range(2)]
        scores_read = [sem(f"scores_read{h}") for h in range(2)]
        max_made = [sem(f"max_made{h}") for h in range(2)]
        exp_made = [sem(f"exp_made{h}") for h in range(2)]
        probs = [sem(f"probs{h}") for h in range(2)]
        probsT_ps = [sem(f"probsT_ps{h}") for h in range(2)]
        probsT = [sem(f"probsT{h}") for h in range(2)]
        heads_ps, heads_out = sem("heads_ps"), sem("heads_out")
        br_ps, merged_made = sem("br_ps"), sem("merged_made")
        h_ps = sem("h_ps")
        ffn_sq, ffn_var, ffn_root, hn_made = sem("ffn_sq"), sem("ffn_var"), sem("ffn_root"), sem("hn_made")
        hnT_ps, hnT_made = sem("hnT_ps"), sem("hnT_made")
        logits_ps, top_made, exps_made, picks_made, pos_ps, table_made = (
            sem("logits_ps"), sem("top_made"), sem("exps_made"), sem("picks_made"), sem("pos_ps"),
            sem("table_made"))
        work_made = sem("work_made")
        sel_made, sel_w_made, sel_e_made, biased = (
            sem("sel_made"), sem("sel_w_made"), sem("sel_e_made"), sem("biased"))
        weight_ps, weight_T_made = sem("weight_ps"), sem("weight_T_made")
        xg_ps, xg_made, xT_ps, xT_made = sem("xg_ps"), sem("xg_made"), sem("xT_ps"), sem("xT_made")
        gu_ps, y_ps = chunk_used[GU_CHUNKS - 1], chunk_used[CHUNKS - 1]
        gate_ready, up_ready, sg_made, act_made = (
            sem("gate_ready"), sem("up_ready"), sem("sg_made"), sem("act_made"))
        act_T_ps, act_T_made, y_made = sem("act_T_ps"), sem("act_T_made"), sem("y_made")
        G_ps, G_made, scattered = sem("G_ps"), sem("G_made"), sem("scattered")
        final_sq, final_var, final_root, final_made = (
            sem("final_sq"), sem("final_var"), sem("final_root"), sem("final_made"))
        dve_once, dve_merge, dve_pair = sem("dve_once"), sem("dve_merge"), sem("dve_pair")
        gu_m_made = sem("gu_m_made")
        act_once, pool_once = sem("act_once"), sem("pool_once")

        def wait_seeded(eng, s, n):
            eng.wait_ge(s, n + 1)

        def fill(k, g):
            return wbuf[:, k, g * D:(g + 1) * D].rearrange("p (c m) -> p c m", c=KC)

        w_in0 = w_in[0]

        def load_chunk(sp, e, c):
            if c < GU_CHUNKS:
                src = w_gu[0][ds(e, 1), c * 2 * P:(c + 1) * 2 * P, :].rearrange("a (c p) n -> p (a c) n", p=P)
                dst = ring[:, c, :].rearrange("p (c n) -> p c n", c=2)
            else:
                c2 = c - GU_CHUNKS
                src = w_down[0][ds(e, 1), c2 * 4 * P:(c2 + 1) * 4 * P, :].rearrange("a (c p) n -> p (a c) n", p=P)
                dst = ring[:, c, :].rearrange("p (c n) -> p c n", c=4)
            sp.dma_start(dst, src).then_inc(chunk_w[c], 16)

        blk = ctx.enter_context(nc.Block())

        @blk.sync
        def _(sp):
            sp.dma_start(x_tok[:], x[0].rearrange("(t p) d -> p t d", p=P)).then_inc(x_loaded, 16)
            sp.dma_start(x_meta, meta_tokens).then_inc(meta_loaded, 16)

            def load_tiles(k, j, sources, loaded):
                for g, (w, c0) in enumerate(sources):
                    src = w[:, ds(j * P + c0, P)].rearrange("(c p) m -> p c m", p=P)
                    sp.dma_start(fill(k, g), src).then_inc(loaded[k], 16)

            glu_tiles = [(w_in0, c0) for c0 in (OFF_A, OFF_B, OFF_GA, OFF_GB)]
            qkv_tiles = [(w_in0, c0) for c0 in (OFF_Q, OFF_K, OFF_V)]
            out_tiles = [(w_conv_out[0], 0), (w_attn_out[0], 0)]
            for k in range(2):
                load_tiles(k, k, glu_tiles, glu_w)
            with sp.Fori(1, KC // 2) as i:
                for k in range(2):
                    sp.wait_ge(gates_ps, i * 2 + (k - 1))
                    load_tiles(k, i * 2 + k, glu_tiles, glu_w)
            for c in range(2):
                load_chunk(sp, 0, c)
            for k in range(2):
                sp.wait_ge(gates_ps, KC - 1 + k)
                load_tiles(k, k, qkv_tiles, qkv_w)
            with sp.Fori(1, PAIRS // 2) as i:
                for k in range(2):
                    sp.wait_ge(q_ps, i * 2 + (k - 1))
                    load_tiles(k, i * 2 + k, qkv_tiles, qkv_w)
            for c in range(2, 4):
                load_chunk(sp, 0, c)
            for k in range(2):
                sp.wait_ge(q_ps, PAIRS - 1 + k)
                load_tiles(k, k, out_tiles, out_w)
            with sp.Fori(1, KC // 2) as i:
                for k in range(2):
                    sp.wait_ge(br_ps, i * 2 + (k - 1))
                    load_tiles(k, i * 2 + k, out_tiles, out_w)
            for k in range(2):
                sp.wait_ge(br_ps, KC - 1 + k)
                src = w_mix_out[0][k * 4 * P:(k + 1) * 4 * P, :].rearrange("(c p) n -> p c n", p=P)
                sp.dma_start(wbuf[:, k, :].rearrange("p (c n) -> p c n", c=4), src).then_inc(mix_w, 16)
            wait_seeded(sp, merged_made, KC)
            for c in range(4, 6):
                load_chunk(sp, 0, c)
            with sp.Fori(1, E) as e:
                for c in range(CHUNKS):
                    sp.wait_ge(chunk_used[c], e)
                    load_chunk(sp, e, c)
            sp.wait_ge(work_made, 1)
            n_work = sp.value_load(work[0:1, 32:33], min_val=0, max_val=EXTRA)
            with sp.Fori(0, EXTRA) as i:
                with sp.If(i < n_work):
                    e = sp.value_load(work[0:1, ds(i, 1)], min_val=0, max_val=E - 1)
                    for c in range(CHUNKS):
                        sp.wait_ge(chunk_used[c], i + E)
                        load_chunk(sp, e, c)
                with sp.Else():
                    sp.nop()
            for t in range(TT):
                sp.wait_ge(final_made, t + 1)
                sp.dma_start(out[0][t * P:(t + 1) * P, :], result[:, t, :]).then_inc(stored, 16)
            sp.wait_ge(stored, 16 * TT)

        @blk.gpsimd
        def _(pool):
            chain = Chain(pool, pool_once)
            chain.link(pool.memset(ident[:], 0.0))
            pool.affine_select(out=ident[:], in_=ident[:], compare_op=ALU.not_equal, fill=1.0, base=0,
                               pattern=[[-1, P]], channel_multiplier=1).then_inc(masks_made, 1)
            chain.link(pool.memset(ones[:], 1.0))
            pool.affine_select(out=before[:], in_=ones[:], compare_op=ALU.is_gt, fill=0.0, base=0,
                               pattern=[[1, P]], channel_multiplier=-1).then_inc(masks_made, 1)
            chain.link(pool.memset(mask0[:], 0.0))
            chain.link(pool.memset(mask1[:], 0.0))
            pool.affine_select(out=mask0[:, META:K0], in_=mask0[:, META:K0], compare_op=ALU.is_ge,
                               fill=MASKED, base=0, pattern=[[-1, P]],
                               channel_multiplier=1).then_inc(masks_made, 1)
            pool.affine_select(out=mask1[:, K0:K1], in_=mask1[:, K0:K1], compare_op=ALU.is_ge,
                               fill=MASKED, base=0, pattern=[[-1, P]],
                               channel_multiplier=1).then_inc(masks_made, 1)
            for k in range(2):
                for h in range(2):
                    other = slice((1 - h) * DH, (1 - h) * DH + HEADS)
                    chain.link(pool.memset(q_s[k][h], 0.0))
                    chain.link(pool.memset(q_s[k][h][other, :], 1.0))
                    pool.memset(k_s[k][h], 0.0).then_inc(pads_made, 1)
                pool.memset(v_s[k], 0.0).then_inc(pads_made, 1)
                pool.memset(pTm[k], 0.0).then_inc(pads_made, 1)
            chain.link(pool.memset(neg_head[:], 0.0))
            pool.affine_select(out=neg_head[:], in_=neg_head[:], compare_op=ALU.not_equal, fill=-1.0,
                               base=0, pattern=[[-1, HEADS]], channel_multiplier=1).then_inc(masks_made, 1)
            pool.iota(iota[:], [[1, SEQ]], base=0, channel_multiplier=0,
                      allow_small_or_imprecise_dtypes=True).then_inc(masks_made, 1)
            pool.wait_ge(h_ps, TT)
            pool.memset(bias_gu, 0.0).then_inc(bias_zero, 1)
            pool.memset(bias_down, 0.0).then_inc(bias_zero, 1)
            pool.wait_ge(bias_zero, 2)
            pool.dma_start(bias_gu[0:E, :], b_gu[0]).then_inc(bias_loaded, 16)
            pool.dma_start(bias_down[0:E, :], b_down[0]).then_inc(bias_loaded, 16)

        @blk.scalar
        def _(act):
            for s in (sig_made, exp_made[0], exp_made[1], probsT[0], probsT[1]):
                act.sem_inc(s, 1)
            vecs = [(COL_A, b_in[0, 0:OFF_F], 5 * KC), (COL_GA, b_in[0, OFF_GA:OFF_GB + D], 2 * KC),
                    (COL_NORM, attn_norm_g[0], KC), (COL_CB, conv_b[0], KC),
                    (COL_LG, conv_ln_g[0], KC), (COL_LB, conv_ln_b[0], KC)]
            for c0, v, n in vecs:
                act.dma_start(raw_cols[c0:c0 + n, :], v.rearrange("(c m) -> c m", m=P)).then_inc(rows_loaded, 16)
            act.dma_start(raw_taps, conv_w[0]).then_inc(raws_loaded, 16)
            act.dma_start(wf[:], w_in0[:, OFF_F:OFF_GA].rearrange("(c p) m -> p c m", p=P)).then_inc(consts_loaded, 16)
            act.dma_start(bf[:], b_in[0, OFF_F:OFF_GA].rearrange("(h a) -> h a", a=1)).then_inc(consts_loaded, 16)
            act.dma_start(wr[:], router_w[0].rearrange("(c p) m -> p c m", p=P)).then_inc(consts_loaded, 16)
            act.dma_start(rb[:], router_b[0:1, :].to_broadcast([P, E])).then_inc(consts_loaded, 16)
            act.dma_start(gain[:], ffn_norm_g[0:1, :].to_broadcast([P, D])).then_inc(gain_loaded, 16)

            act.wait_ge(x_loaded, 16)
            for t in range(TT):
                nc.scalar.activation(x_n[:, t, :], x_tok[:, t, :], ACT.Square,
                                     accum_out=stat[:, t:t + 1]).then_inc(sq_x, 1)
            act.wait_ge(meta_loaded, 16)
            nc.scalar.activation(x_n[0:META, 2, :], x_meta, ACT.Square,
                                 accum_out=stat[0:META, 2:3]).then_inc(sq_x, 1)
            act.wait_ge(rms_var, 2)
            nc.scalar.activation(stat2[:, 0:2], stat2[:, 0:2], ACT.Sqrt).then_inc(rms_root, 1)
            nc.scalar.activation(stat2[0:META, 2:3], stat2[0:META, 2:3], ACT.Sqrt).then_inc(rms_root, 1)

            act.wait_ge(cols_made, 1)
            with act.Fori(0, KC // 2) as i:
                for k in range(2):
                    j = i * 2 + k
                    act.wait_ge(glu_ps, j + 1)
                    wait_seeded(act, glu_made, j)
                    nc.scalar.activation(sig_b[:], ps[:, 4 * k + 1, 0:T], ACT.Sigmoid,
                                         bias=cols[:, ds(j + COL_B, 1)]).then_inc(sig_made, 1)
                    act.wait_ge(gates_ps, j + 1)
                    nc.scalar.activation(sigs[:, 0, ds(j, 1), :], ps[:, 4 * k + 2:4 * k + 3, 0:SEQ], ACT.Sigmoid,
                                         bias=cols[:, ds(j + COL_GA, 1)]).then_inc(gates_made, 1)
                    nc.scalar.activation(sigs[:, 1, ds(j, 1), :], ps[:, 4 * k + 3:4 * k + 4, 0:SEQ], ACT.Sigmoid,
                                         bias=cols[:, ds(j + COL_GB, 1)]).then_inc(gates_made, 1)

            act.wait_ge(f_abs, 1)
            nc.scalar.activation(ftmp[:, 1, :], ftmp[:, 1, :], ACT.Exp, scale=-1.0).then_inc(act_once, 1)
            act.wait_ge(act_once, 1)
            nc.scalar.activation(ftmp[:, 1, :], ftmp[:, 1, :], ACT.Ln, bias=1.0).then_inc(f_log, 1)

            act.wait_ge(centred, 1)
            nc.scalar.activation(squares, u_c, ACT.Square).then_inc(sq_made, 1)
            act.wait_ge(ln_var, 1)
            nc.scalar.activation(lnb[:, 1, :], lnb[:, 1, :], ACT.Sqrt).then_inc(ln_root, 1)
            act.wait_ge(ln_made, 1)
            for c in range(KC):
                nc.scalar.activation(squares[:, c, :], u_c[:, c, :], ACT.Sigmoid,
                                     bias=cols[:, COL_LB + c:COL_LB + c + 1],
                                     scale=cols[:, COL_LG + c:COL_LG + c + 1]).then_inc(silu_in, 1)

            def evacuate_kv(p, k):
                act.wait_ge(v_ps, p + 1)
                nc.scalar.activation(v_T, ps[:, 2, 0:T], ACT.Identity,
                                     bias=cols[:, ds(p + COL_V, 1)]).then_inc(vT_made, 1)
                act.wait_ge(k_ps, p + 1)
                for h in range(2):
                    r = slice(h * DH, (h + 1) * DH)
                    nc.scalar.activation(k_s[k][h][r, :], ps[r, 1, 0:T], ACT.Identity,
                                         bias=cols[r, ds(p + COL_K, 1)]).then_inc(k_made, 1)
                act.wait_ge(vtr_ps, p + 1)
                nc.scalar.activation(v_s[k][0:META, 0:P], ps[0:META, 2, 0:P], ACT.Copy).then_inc(v_made, 1)
                nc.scalar.activation(v_s[k][:, P:3 * P], ps[:, 2, P:3 * P], ACT.Copy).then_inc(v_made, 1)

            def exponentials(p, h):
                act.wait_ge(max_made[h], p + 1)
                wait_seeded(act, probsT_ps[h], p)
                nm = stat[:, 4 + 4 * h:6 + 4 * h]
                nc.scalar.activation(pr[h][:, 0:K0], sc[h][:, 0:K0], ACT.Exp, bias=nm[:, 0:1],
                                     accum_out=stat2[:, 4 + 4 * h:5 + 4 * h]).then_inc(exp_made[h], 1)
                nc.scalar.activation(pr[h][:, K0:SCW], sc[h][:, K0:SCW], ACT.Exp, bias=nm[:, 1:2],
                                     accum_out=stat2[:, 5 + 4 * h:6 + 4 * h]).then_inc(exp_made[h], 1)

            def evacuate_probs(p, h):
                wait_seeded(act, probsT_ps[h], p + 1)
                nc.scalar.activation(pT[h], ps[:, 3 + h, 0:3 * P], ACT.Copy).then_inc(probsT[h], 1)
                nc.scalar.activation(pTm[h][0:META, :], ps[0:META, 5 + h, 0:SEQ], ACT.Copy).then_inc(probsT[h], 1)

            def pair(p, k, more):
                for h in range(2):
                    exponentials(p, h)
                if more:
                    evacuate_kv(p + 1, 1 - k)
                for h in range(2):
                    evacuate_probs(p, h)

            act.wait_ge(pads_made, 8)
            evacuate_kv(0, 0)
            with act.Fori(0, PAIRS // 2 - 1) as i:
                for k in range(2):
                    pair(i * 2 + k, k, True)
            pair(PAIRS - 2, 0, True)
            pair(PAIRS - 1, 1, False)

            for t in range(TT):
                act.wait_ge(h_ps, t + 1)
                nc.scalar.activation(squares_x, ps[:, 4 + 2 * t:6 + 2 * t, :].rearrange("p b n -> p (b n)"),
                                     ACT.Square, accum_out=stat[:, t:t + 1]).then_inc(ffn_sq, 1)
                act.wait_ge(ffn_sq, t + 1)
            act.wait_ge(ffn_var, 1)
            nc.scalar.activation(stat2[:, 0:TT], stat2[:, 0:TT], ACT.Sqrt).then_inc(ffn_root, 1)
            act.wait_ge(hn_made, TT)
            act.dma_start(gain[:], final_norm_g.rearrange("(a d) -> a d", a=1).to_broadcast([P, D])
                          ).then_inc(gain2_loaded, 16)
            for t in range(TT):
                act.wait_ge(hnT_ps, t + 1)
                nc.scalar.activation(hnT[:, :, t * P:(t + 1) * P],
                                     ps[:, 2 * t:2 * t + 2, :].rearrange("p b (c m) -> p (b c) m", m=P),
                                     ACT.Copy).then_inc(hnT_made, 1)
            act.wait_ge(top_made, TT)
            for t in range(TT):
                nc.scalar.activation(route[:, 6 * E + 8 * t:6 * E + 8 * t + TOPK],
                                     route[:, 5 * E + 8 * t:5 * E + 8 * t + TOPK], ACT.Exp,
                                     bias=stat[:, 8 + t:9 + t], accum_out=stat[:, 10 + t:11 + t]).then_inc(exps_made, 1)

            def gathered(n):
                act.wait_ge(xg_ps, n + 1)
                nc.scalar.activation(xg, ps[:, 2, :], ACT.Copy).then_inc(xg_made, 1)

            def gathered_turned(n):
                act.wait_ge(xT_ps, n + 1)
                nc.scalar.activation(xT, ps[:, 2, :], ACT.Copy).then_inc(xT_made, 1)

            def sigmoid(n):
                act.wait_ge(gate_ready, n + 1)
                nc.scalar.activation(sg, gate_m, ACT.Sigmoid, scale=ALPHA).then_inc(sg_made, 1)

            def activations_turned(n):
                act.wait_ge(act_T_ps, n + 1)
                nc.scalar.activation(act_T, ps[:, 0, :], ACT.Copy).then_inc(act_T_made, 1)

            def weights_turned(n):
                act.wait_ge(G_ps, n + 1)
                nc.scalar.activation(G_s, ps[:, 1, :], ACT.Copy).then_inc(G_made, 1)

            def outputs(n):
                act.wait_ge(y_ps, n + 1)
                nc.scalar.activation(y_s, ps[:, 3, :], ACT.Copy).then_inc(y_made, 1)

            gathered(0)
            gathered_turned(0)
            act.wait_ge(weight_ps, 1)
            nc.scalar.activation(weight_T, ps[:, 3, 0:SEQ], ACT.Copy).then_inc(weight_T_made, 1)
            sigmoid(0)
            activations_turned(0)
            gathered(1)
            weights_turned(0)
            gathered_turned(1)
            with act.Fori(1, E - 1) as n:
                outputs(n - 1)
                sigmoid(n)
                activations_turned(n)
                gathered(n + 1)
                weights_turned(n)
                gathered_turned(n + 1)
            outputs(E - 2)
            sigmoid(E - 1)
            activations_turned(E - 1)
            weights_turned(E - 1)
            outputs(E - 1)
            act.wait_ge(work_made, 1)
            n_work = act.value_load(work[0:1, 32:33], min_val=0, max_val=EXTRA)
            with act.Fori(0, EXTRA) as i:
                with act.If(i < n_work):
                    gathered(i + E)
                    gathered_turned(i + E)
                    sigmoid(i + E)
                    activations_turned(i + E)
                    weights_turned(i + E)
                    outputs(i + E)
                with act.Else():
                    act.nop()

            act.wait_ge(scattered, n_work + E)
            for t in range(TT):
                nc.scalar.activation(squares_x, ps[:, 4 + 2 * t:6 + 2 * t, :].rearrange("p b n -> p (b n)"),
                                     ACT.Square, accum_out=stat[:, t:t + 1]).then_inc(final_sq, 1)
                act.wait_ge(final_sq, t + 1)
            act.wait_ge(final_var, 1)
            nc.scalar.activation(stat2[:, 0:TT], stat2[:, 0:TT], ACT.Sqrt).then_inc(final_root, 1)

        @blk.vector
        def _(dve):
            V = nc.vector
            once = Chain(dve, dve_once)
            for s in (glu_made, conv_step, heads_out, merged_made):
                dve.sem_inc(s, 1)
            V.memset(glu[:, :, 0:TAPS - 1], 0.0).then_inc(pad_made, 1)
            dve.wait_ge(cols_ps, 1)
            V.tensor_copy(cols[:], ps[:, 7, 0:NCOLS]).then_inc(cols_made, 1)
            dve.wait_ge(sq_x, 3)
            V.tensor_scalar(stat2[:, 0:2], stat[:, 0:2], 1.0 / D, EPS, ALU.mult, ALU.add).then_inc(rms_var, 1)
            V.tensor_scalar(stat2[0:META, 2:3], stat[0:META, 2:3], 1.0 / D, EPS, ALU.mult, ALU.add).then_inc(rms_var, 1)
            dve.wait_ge(rms_root, 2)
            once.link(V.reciprocal(stat[:, 0:2], stat2[:, 0:2]))
            once.link(V.reciprocal(stat[0:META, 2:3], stat2[0:META, 2:3]))
            for t in range(TT):
                V.tensor_scalar(x_n[:, t, :], x_tok[:, t, :], stat[:, t:t + 1], None, ALU.mult).then_inc(xn_made, 1)
            V.tensor_scalar(x_n[0:META, 2, :], x_meta, stat[0:META, 2:3], None, ALU.mult).then_inc(xn_made, 1)
            dve.wait_ge(cols_made, 1)
            for c in range(KC):
                dve.wait_ge(xnT_ps, c + 1)
                V.tensor_scalar(xnT[:, c, :], ps[:, c % 4, 0:T], cols[:, COL_NORM + c:COL_NORM + c + 1],
                                None, ALU.mult).then_inc(xnT_made, 1)
            dve.wait_ge(taps_ps, 1)
            V.tensor_copy(taps[:], ps[:, 6, 0:KC * TAPS].rearrange("p (c w) -> p c w", w=TAPS)).then_inc(taps_made, 1)
            dve.wait_ge(taps_made, 1)
            dve.wait_ge(pad_made, 1)

            with dve.Fori(0, KC // 2) as i:
                for k in range(2):
                    j = i * 2 + k

                    def step(s):
                        return i * (2 * CONV_STEPS) + k * CONV_STEPS + s

                    wait_seeded(dve, sig_made, j + 1)
                    V.scalar_tensor_tensor(out=glu[:, k, TAPS - 1:], in0=ps[:, 4 * k, 0:T],
                                           scalar=cols[:, ds(j + COL_A, 1)], in1=sig_b[:],
                                           op0=ALU.add, op1=ALU.mult).then_inc(glu_made, 1)
                    wait_seeded(dve, glu_made, j + 1)
                    for w in range(TAPS):
                        src = glu[:, k, META + w:META + w + SEQ]
                        acc = conv_acc[:, w % 2, :]
                        tap = taps[:, ds(j, 1), w]
                        if w == 0:
                            wait_seeded(dve, conv_step, step(0))
                            V.tensor_scalar(acc, src, tap, cols[:, ds(j + COL_CB, 1)],
                                            ALU.mult, ALU.add).then_inc(conv_step, 1)
                        elif w == 1:
                            V.tensor_scalar(acc, src, tap, None, ALU.mult).then_inc(conv_step, 1)
                        else:
                            wait_seeded(dve, conv_step, step(w - 1))
                            V.scalar_tensor_tensor(out=acc, in0=src, scalar=tap, in1=acc,
                                                   op0=ALU.mult, op1=ALU.add).then_inc(conv_step, 1)
                    wait_seeded(dve, conv_step, step(TAPS))
                    V.tensor_tensor(u_c[:, ds(j, 1), :], conv_acc[:, 0:1, :], conv_acc[:, 1:2, :],
                                    ALU.add).then_inc(conv_step, 1)

            dve.wait_ge(f_ps, 1)
            once.link(V.tensor_scalar(ftmp[:, 0, :], ps[0:HEADS, 7, 0:T], bf[:, 0:1], None, ALU.add))
            once.link(V.tensor_scalar(ftmp[:, 2, :], ftmp[:, 0, :], -1.0, None, ALU.mult))
            V.tensor_tensor(ftmp[:, 1, :], ftmp[:, 0, :], ftmp[:, 2, :], ALU.max).then_inc(f_abs, 1)
            dve.wait_ge(mean_ps, 1)
            once.link(V.tensor_scalar(lnb[:, 0, :], ps[:, 4, 0:SEQ], 1.0 / D, None, ALU.mult))
            V.tensor_tensor(u_c, u_c, lnb[:, 0:1, :].to_broadcast([P, KC, SEQ]), ALU.subtract).then_inc(centred, 1)
            dve.wait_ge(f_log, 1)
            once.link(V.scalar_tensor_tensor(out=ftmp[:, 2, :], in0=ftmp[:, 0, :], scalar=0.0,
                                             in1=ftmp[:, 1, :], op0=ALU.min, op1=ALU.subtract))
            once.link(V.memset(ftmp[:, 0, :], 1.0))
            V.tensor_tensor_scan(cum[:], ftmp[:, 0, :], ftmp[:, 2, :], 0.0, ALU.mult, ALU.add).then_inc(cum_made, 1)
            dve.wait_ge(var_ps, 1)
            V.tensor_scalar(lnb[:, 1, :], ps[:, 5, 0:SEQ], 1.0 / D, EPS, ALU.mult, ALU.add).then_inc(ln_var, 1)
            dve.wait_ge(cumT_ps, 1)
            V.tensor_copy(cum_q[:], ps[:, 6, 0:TT * HEADS].rearrange("p (t h) -> p t h", h=HEADS)).then_inc(cum_q_made, 1)
            dve.wait_ge(ln_root, 1)
            once.link(V.reciprocal(lnb[:, 1, :], lnb[:, 1, :]))
            V.tensor_tensor(u_c, u_c, lnb[:, 1:2, :].to_broadcast([P, KC, SEQ]), ALU.mult).then_inc(ln_made, 1)

            def evacuate_q(p, k):
                dve.wait_ge(q_ps, p + 1)
                for h in range(2):
                    r = slice(h * DH, (h + 1) * DH)
                    other = slice((1 - h) * DH, (1 - h) * DH + HEADS)
                    V.tensor_scalar(q_s[k][h][r, :], ps[r, 0, 0:SEQ], cols[r, ds(p + COL_Q, 1)], DH ** -0.5,
                                    ALU.add, ALU.mult).then_inc(q_made, 1)
                    V.tensor_scalar(k_s[k][h][other, :], cum[:], neg_head[:, ds(p * 2 + h, 1)], None,
                                    ALU.mult).then_inc(kc_made, 1)

            PAIR_STEPS = 10
            pc = Chain(dve, dve_pair, PAIR_STEPS)

            def pair(p, k, more):
                pc.at(p)
                for h in range(2):
                    dve.wait_ge(scores[h], p + 1)
                    wait_seeded(dve, exp_made[h], p * 2)
                    for t, (a, b, m) in enumerate(((0, K0, mask0), (K0, SCW, mask1))):
                        pc.link(V.scalar_tensor_tensor(out=sc[h][:, a:b], in0=ps[:, 3 + h, a:b],
                                                       scalar=cum_q[:, t, ds(p * 2 + h, 1)], in1=m[:],
                                                       op0=ALU.add, op1=ALU.add))
                    nm = stat[:, 4 + 4 * h:6 + 4 * h]
                    pc.link(V.tensor_reduce(nm[:, 0:1], sc[h][:, 0:K0], AX_X, ALU.max, negate=True))
                    V.tensor_reduce(nm[:, 1:2], sc[h][:, K0:SCW], AX_X, ALU.max,
                                    negate=True).then_inc(max_made[h], 1)
                for h in range(2):
                    wait_seeded(dve, exp_made[h], p * 2 + 2)
                    pc.link(V.reciprocal(stat2[:, 6 + 4 * h:8 + 4 * h], stat2[:, 4 + 4 * h:6 + 4 * h]))
                    pc.link(V.tensor_scalar(pr[h][:, 0:K0], pr[h][:, 0:K0], stat2[:, 6 + 4 * h:7 + 4 * h],
                                            None, ALU.mult))
                    V.tensor_scalar(pr[h][:, K0:SCW], pr[h][:, K0:SCW], stat2[:, 7 + 4 * h:8 + 4 * h],
                                    None, ALU.mult).then_inc(probs[h], 1)
                assert pc.k == PAIR_STEPS
                if more:
                    evacuate_q(p + 1, 1 - k)
                dve.wait_ge(heads_ps, p + 1)
                V.tensor_scalar(attn_T[:, ds(p, 1), :], ps[:, 7:8, 0:SEQ], 1.0, None, ALU.mult).then_inc(heads_out, 1)

            dve.wait_ge(silu_in, KC)
            for c in range(KC):
                once.link(V.tensor_scalar(u_c[:, c, :], u_c[:, c, :], cols[:, COL_LG + c:COL_LG + c + 1],
                                          cols[:, COL_LB + c:COL_LB + c + 1], ALU.mult, ALU.add))
            once.link(V.tensor_tensor(u_c, u_c, squares, ALU.mult))
            dve.wait_ge(cum_made, 1)
            dve.wait_ge(cum_q_made, 1)
            dve.wait_ge(masks_made, 6)
            dve.wait_ge(pads_made, 8)
            evacuate_q(0, 0)
            with dve.Fori(0, PAIRS // 2 - 1) as i:
                for k in range(2):
                    pair(i * 2 + k, k, True)
            pair(PAIRS - 2, 0, True)
            pair(PAIRS - 1, 1, False)

            with dve.Fori(0, KC // 2) as i:
                for k in range(2):
                    j = i * 2 + k
                    dve.wait_ge(br_ps, j + 1)
                    wait_seeded(dve, merged_made, j)
                    V.tensor_tensor(tmp_m[0], sigs[:, 0, ds(j, 1), :].rearrange("p a t -> p (a t)"),
                                    ps[:, 2 * k, 0:SEQ], ALU.mult).then_inc(dve_merge, 1)
                    V.tensor_tensor(tmp_m[1], sigs[:, 1, ds(j, 1), :].rearrange("p a t -> p (a t)"),
                                    ps[:, 2 * k + 1, 0:SEQ], ALU.mult).then_inc(dve_merge, 1)
                    dve.wait_ge(dve_merge, j * 2 + 2)
                    V.tensor_tensor(merged[:, ds(j, 1), :].rearrange("p a t -> p (a t)"),
                                    tmp_m[0], tmp_m[1], ALU.add).then_inc(merged_made, 1)

            dve.wait_ge(ffn_sq, TT)
            V.tensor_scalar(stat2[:, 0:TT], stat[:, 0:TT], 1.0 / D, EPS, ALU.mult, ALU.add).then_inc(ffn_var, 1)
            dve.wait_ge(ffn_root, 1)
            once.link(V.reciprocal(stat[:, 0:TT], stat2[:, 0:TT]))
            dve.wait_ge(gain_loaded, 16)
            for t in range(TT):
                V.scalar_tensor_tensor(out=hn[:, t, :], in0=ps[:, 4 + 2 * t:6 + 2 * t, :].rearrange("p b n -> p (b n)"),
                                       scalar=stat[:, t:t + 1], in1=gain[:], op0=ALU.mult,
                                       op1=ALU.mult).then_inc(hn_made, 1)

            dve.wait_ge(consts_loaded, 64)
            for t in range(TT):
                lg = route[:, t * E:(t + 1) * E]
                top = route[:, 5 * E + 8 * t:5 * E + 8 * t + 8]
                idx_u = route_i[:, 0:8]
                idx = route[:, 7 * E + 8 * t:7 * E + 8 * t + 8]
                dve.wait_ge(logits_ps, t + 1)
                once.link(V.tensor_tensor(lg, ps[:, t, 0:E], rb[:], ALU.add))
                once.link(V.max(top, lg))
                once.link(V.tensor_scalar(stat[:, 8 + t:9 + t], top[:, 0:1], -1.0, None, ALU.mult))
                once.link(V.max_index(idx_u, top, lg))
                V.tensor_copy(idx, idx_u).then_inc(top_made, 1)
            dve.wait_ge(top_made, TT)
            dve.wait_ge(exps_made, TT)
            once.link(V.reciprocal(stat2[:, 10:10 + TT], stat[:, 10:10 + TT]))
            once.link(V.memset(weight[:], 0.0))
            pick = route[:, 8 * E:12 * E]
            chosen = [route[:, (2 + t) * E:(3 + t) * E] for t in range(TT)]
            for t in range(TT):
                wts = route[:, 6 * E + 8 * t:6 * E + 8 * t + TOPK]
                idx = route[:, 7 * E + 8 * t:7 * E + 8 * t + 8]
                once.link(V.tensor_scalar(wts, wts, stat2[:, 10 + t:11 + t], None, ALU.mult))
                for c in range(TOPK):
                    once.link(V.tensor_scalar(pick[:, c * E:(c + 1) * E], iota[:, 0:E], idx[:, c:c + 1],
                                              None, ALU.is_equal))
                once.link(V.tensor_reduce(chosen[t], pick.rearrange("p (c e) -> p e c", c=TOPK), AX_X, ALU.add))
                for c in range(TOPK):
                    once.link(V.tensor_scalar(pick[:, c * E:(c + 1) * E], iota[:, 0:E], idx[:, c:c + 1],
                                              wts[:, c:c + 1], ALU.is_equal, ALU.mult))
                V.tensor_reduce(weight[:, t, 0:E], pick.rearrange("p (c e) -> p e c", c=TOPK), AX_X, ALU.add).then_inc(picks_made, 1)
                dve.wait_ge(picks_made, t + 1)
            dve.wait_ge(pos_ps, 3)
            for t in range(TT):
                pos = pick[:, t * E:(t + 1) * E]
                once.link(V.scalar_tensor_tensor(out=pos, in0=ps[:, 3, t * E:(t + 1) * E], scalar=1.0,
                                                 in1=chosen[t], op0=ALU.add, op1=ALU.mult))
                V.tensor_scalar(slot_of[:, t, :], pos, -1.0, None, ALU.add).then_inc(table_made, 1)
            dve.wait_ge(table_made, TT)
            once.link(V.memset(sel_w, 0.0))

            def select(n, e, first):
                if not isinstance(n, int) or n > 0:
                    dve.wait_ge(xg_ps, n)
                for t in range(TT):
                    V.tensor_scalar(sel[:, t, :], iota[:, ds(first, SLOTS)], slot_of[:, t, ds(e, 1)],
                                    None, ALU.is_equal).then_inc(sel_made, 1)

            def select_expert(n, e):
                if not isinstance(n, int) or n > 0:
                    dve.wait_ge(biased, n)
                V.tensor_scalar(sel_e, ones[:, 0:SLOTS], ident[:, ds(e, 1)], None, ALU.mult).then_inc(sel_e_made, 1)

            def select_weighted(n, e, first):
                if not isinstance(n, int) or n > 0:
                    dve.wait_ge(G_ps, n)
                for t in range(TT):
                    V.tensor_scalar(sel_w[:, t, SLOTS:2 * SLOTS], iota[:, ds(first, SLOTS)],
                                    slot_of[:, t, ds(e, 1)], weight[:, t, ds(e, 1)],
                                    ALU.is_equal, ALU.mult).then_inc(sel_w_made, 1)

            def swiglu(n):
                dve.wait_ge(gu_ps, n + 1)
                V.tensor_scalar(gate_m, ps[:, 0, :], LIMIT, None, ALU.min).then_inc(gate_ready, 1)
                V.tensor_scalar(up_m, ps[:, 1, :], LIMIT, -LIMIT, ALU.min, ALU.max).then_inc(up_ready, 1)
                dve.wait_ge(up_ready, n + 1)
                V.scalar_tensor_tensor(out=gu_m, in0=up_m, scalar=1.0, in1=gate_m, op0=ALU.add,
                                       op1=ALU.mult).then_inc(gu_m_made, 1)
                dve.wait_ge(gu_m_made, n + 1)
                dve.wait_ge(sg_made, n + 1)
                V.tensor_tensor(act_s, gu_m, sg, ALU.mult).then_inc(act_made, 1)

            select(0, 0, 0)
            select_expert(0, 0)
            select(1, 1, 0)

            n_more = (BLOCKS - 1) * E
            lst = [gates[0:1, a * n_more:(a + 1) * n_more] for a in range(5)]
            active, rank, of_e, of_s = lst[0:4]
            counts = lst[4][:, 0:E]
            match = gates[0:1, 5 * n_more:(5 + EXTRA) * n_more].rearrange("p (r i) -> p r i", i=n_more)
            assert (5 + EXTRA) * n_more <= 4 * BANK
            once.link(V.tensor_copy(counts, ps[0:1, 3, TT * E:TT * E + E]))
            for b in range(1, BLOCKS):
                part = slice((b - 1) * E, b * E)
                once.link(V.tensor_scalar(active[:, part], counts, float(b * SLOTS), None, ALU.is_gt))
                once.link(V.tensor_copy(of_e[:, part], iota[0:1, 0:E]))
                once.link(V.memset(of_s[:, part], float(b * SLOTS)))
            once.link(V.tensor_tensor_scan(rank, ones[0:1, 0:n_more], active, 0.0, ALU.mult, ALU.add))
            once.link(V.memset(work_f[:], 0.0))
            once.link(V.tensor_copy(work_f[:, 32:33], rank[:, n_more - 1:n_more]))
            once.link(V.tensor_tensor(rank, rank, active, ALU.mult))
            shape = [1, EXTRA, n_more]
            for a, values in enumerate((of_e, of_s)):
                once.link(V.tensor_tensor(match, rank.rearrange("p (a i) -> p a i", a=1).to_broadcast(shape),
                                          iota[0:1, 1:1 + EXTRA].rearrange("p (r a) -> p r a", a=1).to_broadcast(shape),
                                          ALU.is_equal))
                once.link(V.tensor_tensor(match, match, values.rearrange("p (a i) -> p a i", a=1).to_broadcast(shape),
                                          ALU.mult))
                once.link(V.tensor_reduce(work_f[:, 16 * a:16 * a + EXTRA], match, AX_X, ALU.add))
            V.tensor_copy(work[:], work_f[:]).then_inc(work_made, 1)
            dve.wait_ge(work_made, 1)

            select_expert(1, 1)
            select_weighted(0, 0, 0)
            swiglu(0)
            with dve.Fori(1, E - 1) as n:
                select(n + 1, n + 1, 0)
                select_expert(n + 1, n + 1)
                select_weighted(n, n, 0)
                swiglu(n)
            select_weighted(E - 1, E - 1, 0)
            swiglu(E - 1)
            n_work = dve.value_load(work[0:1, 32:33], min_val=0, max_val=EXTRA)
            with dve.Fori(0, EXTRA) as i:
                with dve.If(i < n_work):
                    e = dve.value_load(work[0:1, ds(i, 1)], min_val=0, max_val=E - 1)
                    first = dve.value_load(work[0:1, ds(i + 16, 1)], min_val=0, max_val=SEQ - SLOTS)
                    select(i + E, e, first)
                    select_expert(i + E, e)
                    select_weighted(i + E, e, first)
                    swiglu(i + E)
                with dve.Else():
                    dve.nop()

            dve.wait_ge(final_sq, TT)
            V.tensor_scalar(stat2[:, 0:TT], stat[:, 0:TT], 1.0 / D, EPS, ALU.mult, ALU.add).then_inc(final_var, 1)
            dve.wait_ge(final_root, 1)
            once.link(V.reciprocal(stat[:, 0:TT], stat2[:, 0:TT]))
            dve.wait_ge(gain2_loaded, 16)
            for t in range(TT):
                V.scalar_tensor_tensor(out=result[:, t, :],
                                       in0=ps[:, 4 + 2 * t:6 + 2 * t, :].rearrange("p b n -> p (b n)"),
                                       scalar=stat[:, t:t + 1], in1=gain[:], op0=ALU.mult,
                                       op1=ALU.mult).then_inc(final_made, 1)

        @blk.tensor
        def _(pe):
            mm = nc.tensor.matmul

            for s in probsT_ps:
                pe.sem_inc(s, 1)
            pe.wait_ge(masks_made, 1)
            pe.wait_ge(rows_loaded, 16 * 6)
            nc.tensor.transpose(ps[:, 7, 0:NCOLS], raw_cols, ident[0:NCOLS, 0:NCOLS]).then_inc(cols_ps, 1)
            pe.wait_ge(raws_loaded, 16)
            for c in range(KC):
                last = nc.tensor.transpose(ps[:, 6, c * TAPS:(c + 1) * TAPS], raw_taps[:, c * P:(c + 1) * P],
                                           ident[0:TAPS, 0:TAPS])
            last.then_inc(taps_ps, 1)
            pe.wait_ge(xn_made, 3)
            for c in range(KC):
                if c >= 4:
                    pe.wait_ge(xnT_made, c - 3)
                for t in range(TT):
                    nc.tensor.transpose(ps[:, c % 4, META + t * P:META + (t + 1) * P],
                                        x_n[:, t, c * P:(c + 1) * P], ident[:])
                nc.tensor.transpose(ps[:, c % 4, 0:META], x_n[0:META, 2, c * P:(c + 1) * P],
                                    ident[0:META, 0:META]).then_inc(xnT_ps, 1)
            pe.wait_ge(xnT_made, KC)
            pe.wait_ge(cols_made, 1)
            pe.wait_ge(taps_made, 1)

            def project(bank, w, act, n):
                for c in range(KC):
                    last = mm(ps[:, bank, 0:n], w[:, c, :], act[:, c, :], start=(c == 0), stop=(c == KC - 1))
                return last

            x_all, x_seq = xnT[:], xnT[:, :, META:T]
            with pe.Fori(0, KC // 2) as i:
                for k in range(2):
                    pe.wait_ge(glu_w[k], i * 64 + 64)
                    wait_seeded(pe, sig_made, i * 2 + k)
                    project(4 * k + 1, fill(k, 1), x_all, T)
                    project(4 * k, fill(k, 0), x_all, T).then_inc(glu_ps, 1)
                    project(4 * k + 2, fill(k, 2), x_seq, SEQ)
                    project(4 * k + 3, fill(k, 3), x_seq, SEQ).then_inc(gates_ps, 1)

            pe.wait_ge(consts_loaded, 64)
            pe.wait_ge(gates_made, 2 * KC)
            for c in range(KC):
                last = mm(ps[0:HEADS, 7, 0:T], wf[:, c, :], xnT[:, c, :], start=(c == 0), stop=(c == KC - 1))
            last.then_inc(f_ps, 1)
            pe.wait_ge(masks_made, 2)
            wait_seeded(pe, glu_made, KC)
            wait_seeded(pe, conv_step, KC * CONV_STEPS)
            for c in range(KC):
                last = mm(ps[:, 4, 0:SEQ], ones[:], u_c[:, c, :], start=(c == 0), stop=(c == KC - 1))
            last.then_inc(mean_ps, 1)
            pe.wait_ge(sq_made, 1)
            for c in range(KC):
                last = mm(ps[:, 5, 0:SEQ], ones[:], squares[:, c, :], start=(c == 0), stop=(c == KC - 1))
            last.then_inc(var_ps, 1)
            pe.wait_ge(cum_made, 1)
            for t in range(TT):
                last = nc.tensor.transpose(ps[:, 6, t * HEADS:(t + 1) * HEADS],
                                           cum[:, META + t * P:META + (t + 1) * P], ident[0:HEADS, 0:HEADS])
            last.then_inc(cumT_ps, 1)

            def qkv(p, k, i):
                pe.wait_ge(qkv_w[k], i * 48 + 48)
                if not isinstance(p, int) or p > 0:
                    pe.wait_ge(v_made, p * 2)
                    pe.wait_ge(k_made, p * 2)
                    pe.wait_ge(q_made, p * 2)
                project(2, fill(k, 2), x_all, T).then_inc(v_ps, 1)
                project(1, fill(k, 1), x_all, T).then_inc(k_ps, 1)
                project(0, fill(k, 0), x_seq, SEQ).then_inc(q_ps, 1)
                pe.wait_ge(vT_made, p + 1)
                nc.tensor.transpose(ps[0:META, 2, 0:P], v_T[:, 0:META], ident[:])
                nc.tensor.transpose(ps[:, 2, P:2 * P], v_T[:, META:META + P], ident[:])
                nc.tensor.transpose(ps[:, 2, 2 * P:3 * P], v_T[:, META + P:T], ident[:]).then_inc(vtr_ps, 1)

            def attend(p, k, more):
                for h in range(2):
                    pe.wait_ge(q_made, p * 2 + h + 1)
                    pe.wait_ge(k_made, p * 2 + h + 1)
                    pe.wait_ge(kc_made, p * 2 + h + 1)
                    mm(ps[:, 3 + h, 0:K0], q_s[k][h][:, 0:P], k_s[k][h][:, 0:K0], start=True, stop=True)
                    mm(ps[:, 3 + h, K0:SCW], q_s[k][h][:, P:2 * P], k_s[k][h], start=True,
                       stop=True).then_inc(scores[h], 1)
                if more is not None:
                    qkv(p + 1, 1 - k, more)
                for h in range(2):
                    pe.wait_ge(probs[h], p + 1)
                    wait_seeded(pe, probsT[h], p * 2)
                    b = 3 + h
                    nc.tensor.transpose(ps[:, b, 0:P], pr[h][:, META:K0], ident[:])
                    nc.tensor.transpose(ps[:, b, P:2 * P], pr[h][:, K0 + META:K0 + K0], ident[:])
                    nc.tensor.transpose(ps[:, b, 2 * P:3 * P], pr[h][:, K0 + K0:SCW], ident[:])
                    nc.tensor.transpose(ps[0:META, 5 + h, 0:P], pr[h][:, 0:META], ident[:])
                    nc.tensor.transpose(ps[0:META, 5 + h, P:2 * P], pr[h][:, K0:K0 + META],
                                        ident[:]).then_inc(probsT_ps[h], 1)
                pe.wait_ge(v_made, p * 2 + 2)
                wait_seeded(pe, heads_out, p)
                for h in range(2):
                    wait_seeded(pe, probsT[h], p * 2 + 2)
                    o = ps[h * DH:(h + 1) * DH, 7, :]
                    hs = slice(h * DH, (h + 1) * DH)
                    for t in range(TT):
                        q = slice(t * P, (t + 1) * P)
                        mm(o[:, q], v_s[k][:, P + h * DH:P + (h + 1) * DH], pT[h][:, q], start=True, stop=False)
                        if t == 1:
                            mm(o[:, q], v_s[k][:, 2 * P + h * DH:2 * P + (h + 1) * DH], pT[h][:, SEQ:3 * P],
                               start=False, stop=False)
                        last = mm(o[:, q], v_s[k][:, hs], pTm[h][:, q], start=False, stop=True)
                last.then_inc(heads_ps, 1)

            qkv(0, 0, 0)
            with pe.Fori(0, PAIRS // 2 - 1) as i:
                for k in range(2):
                    attend(i * 2 + k, k, i + k)
            attend(PAIRS - 2, 0, PAIRS // 2 - 1)
            attend(PAIRS - 1, 1, None)

            wait_seeded(pe, heads_out, PAIRS)
            with pe.Fori(0, KC // 2) as i:
                for k in range(2):
                    pe.wait_ge(out_w[k], i * 32 + 32)
                    wait_seeded(pe, merged_made, i * 2)
                    project(2 * k, fill(k, 0), u_c, SEQ)
                    project(2 * k + 1, fill(k, 1), attn_T, SEQ).then_inc(br_ps, 1)

            wait_seeded(pe, merged_made, KC)
            pe.wait_ge(mix_w, 32)
            pe.wait_ge(x_loaded, 16)
            for t in range(TT):
                for b in range(2):
                    acc = ps[:, 4 + 2 * t + b, :]
                    mm(acc, ident[:], x_tok[:, t, b * BANK:(b + 1) * BANK], start=True, stop=False)
                    for c in range(KC):
                        w = wbuf[:, c // 4, (c % 4) * D + b * BANK:(c % 4) * D + (b + 1) * BANK]
                        last = mm(acc, merged[:, c, t * P:(t + 1) * P], w, start=False, stop=(c == KC - 1))
                last.then_inc(h_ps, 1)

            for t in range(TT):
                pe.wait_ge(hn_made, t + 1)
                for c in range(KC):
                    last = nc.tensor.transpose(ps[:, 2 * t + c // 4, (c % 4) * P:(c % 4 + 1) * P],
                                               hn[:, t, c * P:(c + 1) * P], ident[:])
                last.then_inc(hnT_ps, 1)
            for t in range(TT):
                pe.wait_ge(hnT_made, t + 1)
                for c in range(KC):
                    last = mm(ps[:, t, 0:E], hnT[:, c, t * P:(t + 1) * P], wr[:, c, :],
                              start=(c == 0), stop=(c == KC - 1))
                last.then_inc(logits_ps, 1)
            pe.wait_ge(picks_made, TT)
            pos = ps[:, 3, :]
            mm(pos[:, 0:E], before[:], route[:, 2 * E:3 * E], start=True, stop=True).then_inc(pos_ps, 1)
            mm(pos[:, E:2 * E], ones[:], route[:, 2 * E:3 * E], start=True, stop=False)
            mm(pos[:, E:2 * E], before[:], route[:, 3 * E:4 * E], start=False, stop=True).then_inc(pos_ps, 1)
            mm(pos[0:1, 2 * E:3 * E], ones[:, 0:1], route[:, 2 * E:3 * E], start=True, stop=False)
            mm(pos[0:1, 2 * E:3 * E], ones[:, 0:1], route[:, 3 * E:4 * E], start=False, stop=True).then_inc(pos_ps, 1)

            def halves(bank, lhsT, rhs, start, stop, **kw):
                for h in range(2):
                    last = mm(ps[h * SLOTS:(h + 1) * SLOTS, bank, :], lhsT, rhs[:, h * BANK:(h + 1) * BANK],
                              start=start, stop=stop, **kw)
                return last

            def turn(bank, src):
                for j in range(4):
                    last = nc.tensor.transpose(ps[:, bank, j * P:(j + 1) * P], src[:, j * P:(j + 1) * P], ident[:])
                return last

            def chunk_of(turned, c):
                a = (c % 4) * P + (c // 4) * SLOTS
                return turned[:, a:a + SLOTS]

            def gather(n):
                pe.wait_ge(sel_made, n * 2 + 2)
                if not isinstance(n, int) or n > 0:
                    pe.wait_ge(xT_made, n)
                for t in range(TT):
                    last = halves(2, sel[:, t, :], hn[:, t, :], t == 0, t == TT - 1)
                last.then_inc(xg_ps, 1)

            def turn_gathered(n):
                pe.wait_ge(xg_made, n + 1)
                turn(2, xg).then_inc(xT_ps, 1)

            def gate_up(n):
                pe.wait_ge(sel_e_made, n + 1)
                if not isinstance(n, int) or n > 0:
                    pe.wait_ge(act_T_made, n)
                    pe.wait_ge(G_made, n)
                for b in range(2):
                    last = halves(b, sel_e, bias_gu[:, b * D:(b + 1) * D], True, False)
                last.then_inc(biased, 1)
                pe.wait_ge(xT_made, n + 1)
                for q in range(GU_CHUNKS):
                    pe.wait_ge(chunk_w[q], n * 16 + 16)
                    w = ring[:, q, :].rearrange("p (c n) -> p c n", c=2)
                    for cc in range(2):
                        c = 2 * q + cc
                        for b in range(2):
                            last = halves(b, chunk_of(xT, c), w[:, cc, b * D:(b + 1) * D], False, c == KC - 1)
                    last.then_inc(chunk_used[q], 1)

            def turn_activations(n):
                pe.wait_ge(act_made, n + 1)
                turn(0, act_s).then_inc(act_T_ps, 1)

            def down(n, q):
                if q == GU_CHUNKS:
                    pe.wait_ge(act_T_made, n + 1)
                    if not isinstance(n, int) or n > 0:
                        pe.wait_ge(y_made, n)
                pe.wait_ge(chunk_w[q], n * 16 + 16)
                w = ring[:, q, :].rearrange("p (c n) -> p c n", c=4)
                for cc in range(4):
                    c = 4 * (q - GU_CHUNKS) + cc
                    last = halves(3, chunk_of(act_T, c), w[:, cc, :], c == 0, c == KC - 1)
                last.then_inc(chunk_used[q], 1)

            def turn_weights(n):
                pe.wait_ge(sel_w_made, n * 2 + 2)
                for h in range(2):
                    for t in range(TT):
                        a = (2 * h + t) * P
                        last = nc.tensor.transpose(ps[:, 1, a:a + P],
                                                   sel_w[:, t, (1 - h) * SLOTS:(3 - h) * SLOTS], ident[:])
                last.then_inc(G_ps, 1)

            def scatter(n):
                pe.wait_ge(G_made, n + 1)
                pe.wait_ge(y_made, n + 1)
                for t in range(TT):
                    for h in range(2):
                        a = (2 * h + t) * P
                        last = mm(ps[:, 4 + 2 * t + h, :], G_s[:, a:a + P], y_s, start=False, stop=True,
                                  skip_group_check=True)
                last.then_inc(scattered, 1)

            gather(0)
            turn_gathered(0)
            pe.wait_ge(bias_loaded, 32)
            gate_up(0)
            pe.wait_ge(work_made, 1)
            for t in range(TT):
                last = nc.tensor.transpose(ps[:, 3, t * P:(t + 1) * P], weight[:, t, :], ident[:])
            last.then_inc(weight_ps, 1)
            pe.wait_ge(weight_T_made, 1)
            for t in range(TT):
                for h in range(2):
                    mm(ps[:, 4 + 2 * t + h, :], weight_T[:, t * P:(t + 1) * P], bias_down[:, h * BANK:(h + 1) * BANK],
                       start=False, stop=True, skip_group_check=True)
            turn_activations(0)
            gather(1)
            down(0, 4)
            turn_weights(0)
            turn_gathered(1)
            down(0, 5)
            with pe.Fori(1, E - 1) as n:
                gate_up(n)
                scatter(n - 1)
                turn_activations(n)
                gather(n + 1)
                down(n, 4)
                turn_weights(n)
                turn_gathered(n + 1)
                down(n, 5)
            gate_up(E - 1)
            scatter(E - 2)
            turn_activations(E - 1)
            down(E - 1, 4)
            turn_weights(E - 1)
            down(E - 1, 5)
            scatter(E - 1)
            n_work = pe.value_load(work[0:1, 32:33], min_val=0, max_val=EXTRA)
            with pe.Fori(0, EXTRA) as i:
                with pe.If(i < n_work):
                    gather(i + E)
                    turn_gathered(i + E)
                    gate_up(i + E)
                    turn_activations(i + E)
                    down(i + E, 4)
                    turn_weights(i + E)
                    down(i + E, 5)
                    scatter(i + E)
                with pe.Else():
                    pe.nop()


_INS = ['x', 'meta_tokens', 'attn_norm_g', 'w_in', 'b_in', 'conv_w', 'conv_b', 'conv_ln_g', 'conv_ln_b',
        'w_conv_out', 'w_attn_out', 'w_mix_out', 'ffn_norm_g', 'router_w', 'router_b', 'w_gu', 'b_gu',
        'w_down', 'b_down', 'final_norm_g']
_OUTS = [((1, SEQ, D), 'float32')]


def kernel(**inputs):
    import numpy as _np
    import concourse.bacc as _bacc
    from concourse import mybir as _mybir
    from concourse.bass_utils import run_bass_kernel_spmd as _run

    nc = _bacc.Bacc("TRN2", target_bir_lowering=False, num_devices=1)
    arrays, args = {}, []
    for name in _INS:
        a = _np.ascontiguousarray(inputs[name])
        arrays[f"in_{name}_dram"] = a
        args.append(nc.dram_tensor(f"in_{name}_dram", a.shape, _mybir.dt.from_np(a.dtype), kind="ExternalInput").ap())
    for i, (shape, dtype) in enumerate(_OUTS):
        dt = _mybir.dt.from_np(_np.dtype(dtype))
        args.append(nc.dram_tensor(f"out_{i}_dram", shape, dt, kind="ExternalOutput").ap())
    build(nc, *args)
    r = _run(nc, [arrays], core_ids=[0])
    return _np.asarray(r.results[0]["out_0_dram"])
```

```python
from contextlib import ExitStack

import concourse.bass as bass
from concourse import mybir
from concourse.alu_op_type import AluOpType as ALU

ACT = mybir.ActivationFunctionType
AX_X = mybir.AxisListType.X
F32 = mybir.dt.float32
I32 = mybir.dt.int32
U32 = mybir.dt.uint32
ds = bass.ds

P = 128
BANK = 512
D = 1024
KC = D // P
META = 16
SEQ = 256
T = META + SEQ
TT = SEQ // P
TAPS = 31
HEADS, DH = 16, 64
PAIRS = HEADS // 2
E, TOPK = 32, 4
GU = 2 * D
SLOTS = 64
BLOCKS = SEQ // SLOTS
EXTRA = (SEQ * TOPK - 1) // SLOTS
EPS = 1e-5
ALPHA, LIMIT = 1.702, 7.0
MASKED = -1.0e30

OFF_A, OFF_B = 0, D
OFF_Q, OFF_K, OFF_V = 2 * D, 3 * D, 4 * D
OFF_F = 5 * D
OFF_GA = OFF_F + HEADS
OFF_GB = OFF_GA + D
COL_A, COL_B, COL_Q, COL_K, COL_V, COL_GA, COL_GB, COL_NORM, COL_CB, COL_LG, COL_LB = (
    KC * n for n in range(11))
NCOLS = 11 * KC
CONV_STEPS = TAPS + 1
K0, K1 = META + P, T
SCW = K0 + K1
CHUNK = 4 * D
GU_CHUNKS, CHUNKS = 4, 6


class Chain:

    def __init__(self, eng, sem, per_round=0):
        self.eng, self.sem, self.per_round, self.base, self.k = eng, sem, per_round, 0, 0

    def at(self, n):
        self.base, self.k = n * self.per_round, 0

    def link(self, ins):
        self.k += 1
        ins.then_inc(self.sem, 1)
        self.eng.wait_ge(self.sem, self.base + self.k)


def build(nc, x, meta_tokens, attn_norm_g, w_in, b_in, conv_w, conv_b, conv_ln_g, conv_ln_b,
          w_conv_out, w_attn_out, w_mix_out, ffn_norm_g, router_w, router_b, w_gu, b_gu,
          w_down, b_down, final_norm_g, out):
    ctx = ExitStack()
    with ctx:
        def sb(name, shape, dt=F32):
            return ctx.enter_context(nc.sbuf_tensor(name, shape, dt))

        def sem(name):
            return ctx.enter_context(nc.semaphore(name))

        ps = ctx.enter_context(nc.psum_tensor("ps", [P, 8, BANK], F32))

        ring = sb("ring", [P, CHUNKS, CHUNK])
        wbuf = sb("wbuf", [P, 2, 4 * D])
        x_tok = sb("x_tok", [P, TT, D])
        xn = sb("xn", [P, 3 * D])
        xnT = sb("xnT", [P, KC, T])
        u = sb("u", [P, KC * SEQ])
        gates = sb("gates", [P, 2 * KC * SEQ])
        gain = sb("gain", [P, D])
        glu = sb("glu", [P, 2, TAPS - 1 + T])
        sig_b = sb("sig_b", [P, T])
        conv_acc = sb("conv_acc", [P, 2, SEQ])
        cols = sb("cols", [P, NCOLS])
        taps = sb("taps", [P, KC, TAPS])
        slot_of = sb("slot_of", [P, TT, E])
        weight = sb("weight", [P, TT, P])
        ident = sb("ident", [P, P])
        ones = sb("ones", [P, P])
        before = sb("before", [P, P])
        mask0 = sb("mask0", [P, K0])
        mask1 = sb("mask1", [P, K1])
        neg_head = sb("neg_head", [HEADS, HEADS])
        iota = sb("iota", [P, SEQ])
        wf = sb("wf", [P, KC, HEADS])
        wr = sb("wr", [P, KC, E])
        rb = sb("rb", [P, E])
        bf = sb("bf", [HEADS, 1])
        cum = sb("cum", [HEADS, T])
        cum_q = sb("cum_q", [P, TT, HEADS])
        stat = sb("stat", [P, 16])
        stat2 = sb("stat2", [P, 16])
        lnb = sb("lnb", [P, 2, SEQ])
        route = sb("route", [P, 16 * E])
        route_i = sb("route_i", [P, 8], U32)
        work_f = sb("work_f", [1, 3 * 16])
        work = sb("work", [1, 3 * 16], I32)

        x_n = xn[:].rearrange("p (t d) -> p t d", t=3)
        u_c = u[:].rearrange("p (c t) -> p c t", c=KC)
        sigs = gates[:].rearrange("p (g c t) -> p g c t", g=2, c=KC)
        raw_cols = u[0:NCOLS, 0:P]
        raw_taps = u[0:TAPS, D:2 * D]
        x_meta = gates[0:META, GU + D:GU + 2 * D]
        attn_T = xn[:, 0:KC * SEQ].rearrange("p (c t) -> p c t", c=KC)
        squares = wbuf[:, :, 3 * D:4 * D].rearrange("p k (c t) -> p k c t", c=KC // 2)
        squares_of = [conv_acc[:, n, :] for n in range(2)]
        u_kc = u[:].rearrange("p (k c t) -> p k c t", k=2, c=KC // 2)
        merged = xnT[:].rearrange("p c t -> p (c t)")[:, 0:KC * SEQ].rearrange("p (c t) -> p c t", c=KC)
        spare = [0]

        def lent(n):
            a = spare[0]
            spare[0] += n
            assert spare[0] <= 2 * CHUNK
            return ring[:, 4:6, :].rearrange("p a b -> p (a b)")[:, a:a + n]

        q_s = [[lent(SEQ) for _ in range(2)] for _ in range(2)]
        k_s = [[lent(T) for _ in range(2)] for _ in range(2)]
        v_s = [lent(3 * P) for _ in range(2)]
        v_T = lent(T)
        sc = [lent(SCW) for _ in range(2)]
        pr = [lent(SCW) for _ in range(2)]
        pT = [lent(3 * P) for _ in range(2)]
        pTm = [lent(SEQ) for _ in range(2)]
        tmp_m = [lent(SEQ) for _ in range(2)]
        ftmp = lent(3 * T)[0:HEADS, :].rearrange("p (a t) -> p a t", a=3)
        hn = xn[:, 0:TT * D].rearrange("p (t d) -> p t d", t=TT)
        hnT = wbuf[:, 0, 0:KC * SEQ].rearrange("p (c t) -> p c t", c=KC)
        squares_x, squares_y = u[:, 0:D], gates[:, 6 * BANK:8 * BANK]
        result = ring[:, 0, 0:TT * D].rearrange("p (t d) -> p t d", t=TT)
        moe = [gates[:, a * BANK:(a + 1) * BANK] for a in range(8)]
        gate_m, up_m, sg, gu_m, act_s, act_T, xg, xT = moe
        bias_gu = wbuf[:, 0, GU:2 * GU]
        bias_down = xn[:, 2 * D:3 * D]
        ahead = [[wbuf[:, 1, 0:GU], wbuf[:, 1, GU:2 * GU]],
                 [x_tok[:].rearrange("p t d -> p (t d)"), xnT[:].rearrange("p c t -> p (c t)")[:, 0:GU]]]
        y_s = u[:, 0:BANK]
        G_s = u[:, BANK:2 * BANK]
        sel = u[:, 1024:1024 + TT * SLOTS].rearrange("p (t s) -> p t s", t=TT)
        sel_w = u[:, 1152:1152 + TT * 3 * SLOTS].rearrange("p (t s) -> p t s", t=TT)
        sel_e = u[:, 1536:1536 + SLOTS]
        weight_T = u[:, 1600:1600 + SEQ]

        x_loaded = [sem(f"x_loaded{t}") for t in range(TT)]
        meta_loaded, rows_loaded = sem("meta_loaded"), sem("rows_loaded")
        consts_loaded, gain_loaded, gain2_loaded = sem("consts_loaded"), sem("gain_loaded"), sem("gain2_loaded")
        raws_loaded = sem("raws_loaded")
        glu_w = [sem(f"glu_w{k}") for k in range(2)]
        qkv_w = [sem(f"qkv_w{k}") for k in range(2)]
        out_w = [sem(f"out_w{k}") for k in range(2)]
        mix_w = sem("mix_w")
        chunk_w = [sem(f"chunk_w{c}") for c in range(CHUNKS)]
        ahead_w = [sem(f"ahead_w{c}") for c in range(2)]
        chunk_used = [sem(f"chunk_used{c}") for c in range(CHUNKS)]
        stored = sem("stored")
        masks_made = sem("masks_made")
        cols_ps, cols_made = sem("cols_ps"), sem("cols_made")
        taps_ps, taps_made = sem("taps_ps"), sem("taps_made")
        pads_made, bias_zero, bias_loaded = sem("pads_made"), sem("bias_zero"), sem("bias_loaded")
        sq_x, rms_var, rms_root, rms_inv, xn_made = (
            sem("sq_x"), sem("rms_var"), sem("rms_root"), sem("rms_inv"), sem("xn_made"))
        xnT_ps = sem("xnT_ps")
        xnT_made = [sem("xnT_made_even"), sem("xnT_made_odd")]
        pad_made = sem("pad_made")
        glu_ps, sig_made, glu_made, conv_step = sem("glu_ps"), sem("sig_made"), sem("glu_made"), sem("conv_step")
        gates_ps, gates_made = sem("gates_ps"), sem("gates_made")
        mean_ps, centred, sq_made, var_ps = sem("mean_ps"), sem("centred"), sem("sq_made"), sem("var_ps")
        ln_var, ln_root, ln_made, silu_in, silu_made = (
            sem("ln_var"), sem("ln_root"), sem("ln_made"), sem("silu_in"), sem("silu_made"))
        u_sum, sq_sum = sem("u_sum"), sem("sq_sum")
        f_ps, f_abs, f_log, cum_made, cumT_ps, cum_q_made = (
            sem("f_ps"), sem("f_abs"), sem("f_log"), sem("cum_made"), sem("cumT_ps"), sem("cum_q_made"))
        q_ps, k_ps, v_ps = sem("q_ps"), sem("k_ps"), sem("v_ps")
        q_made, k_made, vT_made, vtr_ps, v_made = (
            sem("q_made"), sem("k_made"), sem("vT_made"), sem("vtr_ps"), sem("v_made"))
        kc_made = sem("kc_made")
        scores = [sem(f"scores{h}") for h in range(2)]
        scores_read = [sem(f"scores_read{h}") for h in range(2)]
        max_made = [sem(f"max_made{h}") for h in range(2)]
        exp_made = [sem(f"exp_made{h}") for h in range(2)]
        probs = [sem(f"probs{h}") for h in range(2)]
        probsT_ps = [sem(f"probsT_ps{h}") for h in range(2)]
        probsT = [sem(f"probsT{h}") for h in range(2)]
        heads_ps, heads_out = sem("heads_ps"), sem("heads_out")
        br_ps, merged_made = sem("br_ps"), sem("merged_made")
        h_ps = sem("h_ps")
        ffn_sq, ffn_var, ffn_root, hn_made = sem("ffn_sq"), sem("ffn_var"), sem("ffn_root"), sem("hn_made")
        hnT_ps, hnT_made = sem("hnT_ps"), sem("hnT_made")
        logits_ps, top_made, exps_made, picks_made, pos_ps, table_made = (
            sem("logits_ps"), sem("top_made"), sem("exps_made"), sem("picks_made"), sem("pos_ps"),
            sem("table_made"))
        weights_made, work_made = sem("weights_made"), sem("work_made")
        sel_made, sel_w_made, sel_e_made, biased = (
            sem("sel_made"), sem("sel_w_made"), sem("sel_e_made"), sem("biased"))
        weight_ps, weight_T_made = sem("weight_ps"), sem("weight_T_made")
        xg_ps, xg_made, xT_ps, xT_made = sem("xg_ps"), sem("xg_made"), sem("xT_ps"), sem("xT_made")
        gu_ps, y_ps = chunk_used[GU_CHUNKS - 1], chunk_used[CHUNKS - 1]
        gate_ready, up_ready, sg_made, act_made = (
            sem("gate_ready"), sem("up_ready"), sem("sg_made"), sem("act_made"))
        act_T_ps, act_T_made, y_made = sem("act_T_ps"), sem("act_T_made"), sem("y_made")
        G_ps, G_made, scattered = sem("G_ps"), sem("G_made"), sem("scattered")
        final_sq, final_var, final_root, final_made = (
            sem("final_sq"), sem("final_var"), sem("final_root"), sem("final_made"))
        dve_once, dve_merge, dve_pair = sem("dve_once"), sem("dve_merge"), sem("dve_pair")
        gu_m_made = sem("gu_m_made")
        act_once, pool_once = sem("act_once"), sem("pool_once")

        def wait_seeded(eng, s, n):
            eng.wait_ge(s, n + 1)

        def fill(k, g):
            return wbuf[:, k, g * D:(g + 1) * D].rearrange("p (c m) -> p c m", c=KC)

        w_in0 = w_in[0]
        vecs = [(COL_A, b_in[0, 0:OFF_F], 5 * KC), (COL_GA, b_in[0, OFF_GA:OFF_GB + D], 2 * KC),
                (COL_NORM, attn_norm_g[0], KC), (COL_CB, conv_b[0], KC),
                (COL_LG, conv_ln_g[0], KC), (COL_LB, conv_ln_b[0], KC)]

        def load_chunk(sp, e, c):
            if c < GU_CHUNKS:
                src = w_gu[0][ds(e, 1), c * 2 * P:(c + 1) * 2 * P, :].rearrange("a (c p) n -> p (a c) n", p=P)
                dst = ring[:, c, :].rearrange("p (c n) -> p c n", c=2)
            else:
                c2 = c - GU_CHUNKS
                src = w_down[0][ds(e, 1), c2 * 4 * P:(c2 + 1) * 4 * P, :].rearrange("a (c p) n -> p (a c) n", p=P)
                dst = ring[:, c, :].rearrange("p (c n) -> p c n", c=4)
            sp.dma_start(dst, src).then_inc(chunk_w[c], 16)

        blk = ctx.enter_context(nc.Block())

        @blk.sync
        def _(sp):
            for t in range(TT):
                sp.dma_start(x_tok[:, t, :], x[0][t * P:(t + 1) * P, :]).then_inc(x_loaded[t], 16)
            sp.dma_start(x_meta, meta_tokens).then_inc(meta_loaded, 16)

            def load_tiles(k, j, sources, loaded):
                for g, (w, c0) in enumerate(sources):
                    src = w[:, ds(j * P + c0, P)].rearrange("(c p) m -> p c m", p=P)
                    sp.dma_start(fill(k, g), src).then_inc(loaded[k], 16)

            glu_tiles = [(w_in0, c0) for c0 in (OFF_A, OFF_B, OFF_GA, OFF_GB)]
            qkv_tiles = [(w_in0, c0) for c0 in (OFF_Q, OFF_K, OFF_V)]
            out_tiles = [(w_conv_out[0], 0), (w_attn_out[0], 0)]
            for k in range(2):
                load_tiles(k, k, glu_tiles, glu_w)
            with sp.Fori(1, KC // 2) as i:
                for k in range(2):
                    sp.wait_ge(gates_ps, i * 2 + (k - 1))
                    load_tiles(k, i * 2 + k, glu_tiles, glu_w)
            for c in range(2):
                load_chunk(sp, 0, c)
            for k in range(2):
                sp.wait_ge(gates_ps, KC - 1 + k)
                load_tiles(k, k, qkv_tiles, qkv_w)
            with sp.Fori(1, PAIRS // 2) as i:
                for k in range(2):
                    sp.wait_ge(q_ps, i * 2 + (k - 1))
                    load_tiles(k, i * 2 + k, qkv_tiles, qkv_w)
            for k in range(2):
                src = w_mix_out[0][k * 4 * P:(k + 1) * 4 * P, :].rearrange("(c p) n -> p c n", p=P)
                sp.dma_start(ring[:, 2 + k, :].rearrange("p (c n) -> p c n", c=4), src).then_inc(mix_w, 16)
            for k in range(2):
                sp.wait_ge(q_ps, PAIRS - 1 + k)
                load_tiles(k, k, out_tiles, out_w)
            with sp.Fori(1, KC // 2) as i:
                for k in range(2):
                    sp.wait_ge(br_ps, i * 2 + (k - 1))
                    load_tiles(k, i * 2 + k, out_tiles, out_w)
            wait_seeded(sp, merged_made, KC)
            for c in range(4, 6):
                load_chunk(sp, 0, c)

            def load_ahead(e, c):
                for a in range(2):
                    r = (2 * c + a) * P
                    sp.dma_start(ahead[c][a], w_gu[0][e, r:r + P, :]).then_inc(ahead_w[c], 16)

            sp.wait_ge(br_ps, KC)
            load_ahead(1, 0)
            sp.wait_ge(h_ps, 2 * TT)
            for c in range(2, 4):
                load_chunk(sp, 0, c)
            load_ahead(1, 1)
            for c in range(2):
                sp.wait_ge(chunk_used[c], 1)
                load_chunk(sp, 2, c)
            for c in range(2, CHUNKS):
                sp.wait_ge(chunk_used[c], 1)
                load_chunk(sp, 1, c)
            sp.wait_ge(chunk_used[0], 2)
            load_ahead(3, 0)
            for c in range(2, CHUNKS):
                sp.wait_ge(chunk_used[c], 2)
                load_chunk(sp, 2, c)
            for c in range(1, CHUNKS):
                sp.wait_ge(chunk_used[c], 3)
                load_chunk(sp, 3, c)
            with sp.Fori(4, E) as e:
                for c in range(CHUNKS):
                    sp.wait_ge(chunk_used[c], e)
                    load_chunk(sp, e, c)
            sp.wait_ge(work_made, 1)
            n_work = sp.value_load(work[0:1, 32:33], min_val=0, max_val=EXTRA)
            with sp.If(n_work > 0):
                with sp.Fori(0, EXTRA) as i:
                    with sp.If(i < n_work):
                        e = sp.value_load(work[0:1, ds(i, 1)], min_val=0, max_val=E - 1)
                        for c in range(CHUNKS):
                            sp.wait_ge(chunk_used[c], i + E)
                            load_chunk(sp, e, c)
                    with sp.Else():
                        sp.nop()
            with sp.Else():
                sp.nop()
            for t in range(TT):
                sp.wait_ge(final_made, t + 1)
                sp.dma_start(out[0][t * P:(t + 1) * P, :], result[:, t, :]).then_inc(stored, 16)
            sp.wait_ge(stored, 16 * TT)

        @blk.gpsimd
        def _(pool):
            chain = Chain(pool, pool_once)
            pool.dma_start(raw_taps, conv_w[0]).then_inc(raws_loaded, 16)
            for c0, v, n in vecs[:3]:
                pool.dma_start(raw_cols[c0:c0 + n, :], v.rearrange("(c m) -> c m", m=P)).then_inc(raws_loaded, 16)
            chain.link(pool.memset(ident[:], 0.0))
            pool.affine_select(out=ident[:], in_=ident[:], compare_op=ALU.not_equal, fill=1.0, base=0,
                               pattern=[[-1, P]], channel_multiplier=1).then_inc(masks_made, 1)
            chain.link(pool.memset(ones[:], 1.0))
            pool.affine_select(out=before[:], in_=ones[:], compare_op=ALU.is_gt, fill=0.0, base=0,
                               pattern=[[1, P]], channel_multiplier=-1).then_inc(masks_made, 1)
            chain.link(pool.memset(mask0[:], 0.0))
            chain.link(pool.memset(mask1[:], 0.0))
            pool.affine_select(out=mask0[:, META:K0], in_=mask0[:, META:K0], compare_op=ALU.is_ge,
                               fill=MASKED, base=0, pattern=[[-1, P]],
                               channel_multiplier=1).then_inc(masks_made, 1)
            pool.affine_select(out=mask1[:, K0:K1], in_=mask1[:, K0:K1], compare_op=ALU.is_ge,
                               fill=MASKED, base=0, pattern=[[-1, P]],
                               channel_multiplier=1).then_inc(masks_made, 1)
            for k in range(2):
                for h in range(2):
                    other = slice((1 - h) * DH, (1 - h) * DH + HEADS)
                    chain.link(pool.memset(q_s[k][h], 0.0))
                    chain.link(pool.memset(q_s[k][h][other, :], 1.0))
                    pool.memset(k_s[k][h], 0.0).then_inc(pads_made, 1)
                pool.memset(v_s[k], 0.0).then_inc(pads_made, 1)
                pool.memset(pTm[k], 0.0).then_inc(pads_made, 1)
            chain.link(pool.memset(neg_head[:], 0.0))
            pool.affine_select(out=neg_head[:], in_=neg_head[:], compare_op=ALU.not_equal, fill=-1.0,
                               base=0, pattern=[[-1, HEADS]], channel_multiplier=1).then_inc(masks_made, 1)
            pool.iota(iota[:], [[1, SEQ]], base=0, channel_multiplier=0,
                      allow_small_or_imprecise_dtypes=True).then_inc(masks_made, 1)
            pool.wait_ge(br_ps, KC)
            pool.memset(bias_gu, 0.0).then_inc(bias_zero, 1)
            pool.memset(bias_down, 0.0).then_inc(bias_zero, 1)
            pool.wait_ge(bias_zero, 2)
            pool.dma_start(bias_gu[0:E, :], b_gu[0]).then_inc(bias_loaded, 16)
            pool.dma_start(bias_down[0:E, :], b_down[0]).then_inc(bias_loaded, 16)

        @blk.scalar
        def _(act):
            for s in (sig_made, exp_made[0], exp_made[1], probsT[0], probsT[1]):
                act.sem_inc(s, 1)
            for c0, v, n in vecs[3:]:
                act.dma_start(raw_cols[c0:c0 + n, :], v.rearrange("(c m) -> c m", m=P)).then_inc(rows_loaded, 16)

            for t in range(TT):
                act.wait_ge(x_loaded[t], 16)
                nc.scalar.activation(x_n[:, t, :], x_tok[:, t, :], ACT.Square,
                                     accum_out=stat[:, t:t + 1]).then_inc(sq_x, 1)
            act.wait_ge(rms_var, 2)
            nc.scalar.activation(stat2[:, 0:2], stat2[:, 0:2], ACT.Sqrt).then_inc(rms_root, 1)
            nc.scalar.activation(stat2[0:META, 2:3], stat2[0:META, 2:3], ACT.Sqrt).then_inc(rms_root, 1)
            act.wait_ge(rms_inv, 2)
            act.wait_ge(sq_x, 2)
            nc.scalar.activation(x_n[:, 1, :], x_tok[:, 1, :], ACT.Copy, scale=stat[:, 1:2]).then_inc(xn_made, 1)
            act.wait_ge(cols_made, 1)
            for c in range(1, KC, 2):
                act.wait_ge(xnT_ps, c + 1)
                nc.scalar.activation(xnT[:, c, :], ps[:, c % 4, 0:T], ACT.Copy,
                                     scale=cols[:, COL_NORM + c:COL_NORM + c + 1]).then_inc(xnT_made[1], 1)
            act.dma_start(wf[:], w_in0[:, OFF_F:OFF_GA].rearrange("(c p) m -> p c m", p=P)).then_inc(consts_loaded, 16)
            act.dma_start(bf[:], b_in[0, OFF_F:OFF_GA].rearrange("(h a) -> h a", a=1)).then_inc(consts_loaded, 16)
            act.dma_start(wr[:], router_w[0].rearrange("(c p) m -> p c m", p=P)).then_inc(consts_loaded, 16)
            act.dma_start(rb[:], router_b[0:1, :].to_broadcast([P, E])).then_inc(consts_loaded, 16)
            act.dma_start(gain[:], ffn_norm_g[0:1, :].to_broadcast([P, D])).then_inc(gain_loaded, 16)

            with act.Fori(0, KC // 2) as i:
                for k in range(2):
                    j = i * 2 + k
                    act.wait_ge(glu_ps, j + 1)
                    wait_seeded(act, glu_made, j)
                    nc.scalar.activation(sig_b[:], ps[:, 4 * k + 1, 0:T], ACT.Sigmoid,
                                         bias=cols[:, ds(j + COL_B, 1)]).then_inc(sig_made, 1)
                    act.wait_ge(gates_ps, j + 1)
                    nc.scalar.activation(sigs[:, 0, ds(j, 1), :], ps[:, 4 * k + 2:4 * k + 3, 0:SEQ], ACT.Sigmoid,
                                         bias=cols[:, ds(j + COL_GA, 1)]).then_inc(gates_made, 1)
                    nc.scalar.activation(sigs[:, 1, ds(j, 1), :], ps[:, 4 * k + 3:4 * k + 4, 0:SEQ], ACT.Sigmoid,
                                         bias=cols[:, ds(j + COL_GB, 1)]).then_inc(gates_made, 1)

            def evacuate_kv(p, k):
                act.wait_ge(v_ps, p + 1)
                nc.scalar.activation(v_T, ps[:, 2, 0:T], ACT.Identity,
                                     bias=cols[:, ds(p + COL_V, 1)]).then_inc(vT_made, 1)
                act.wait_ge(k_ps, p + 1)
                for h in range(2):
                    r = slice(h * DH, (h + 1) * DH)
                    nc.scalar.activation(k_s[k][h][r, :], ps[r, 1, 0:T], ACT.Identity,
                                         bias=cols[r, ds(p + COL_K, 1)]).then_inc(k_made, 1)
                act.wait_ge(vtr_ps, p + 1)
                nc.scalar.activation(v_s[k][0:META, 0:P], ps[0:META, 2, 0:P], ACT.Copy).then_inc(v_made, 1)
                nc.scalar.activation(v_s[k][:, P:3 * P], ps[:, 2, P:3 * P], ACT.Copy).then_inc(v_made, 1)

            def exponentials(p, h):
                act.wait_ge(max_made[h], p + 1)
                wait_seeded(act, probsT_ps[h], p)
                nm = stat[:, 4 + 4 * h:6 + 4 * h]
                nc.scalar.activation(pr[h][:, 0:K0], sc[h][:, 0:K0], ACT.Exp, bias=nm[:, 0:1],
                                     accum_out=stat2[:, 4 + 4 * h:5 + 4 * h]).then_inc(exp_made[h], 1)
                nc.scalar.activation(pr[h][:, K0:SCW], sc[h][:, K0:SCW], ACT.Exp, bias=nm[:, 1:2],
                                     accum_out=stat2[:, 5 + 4 * h:6 + 4 * h]).then_inc(exp_made[h], 1)

            def evacuate_probs(p, h):
                wait_seeded(act, probsT_ps[h], p + 1)
                nc.scalar.activation(pT[h], ps[:, 3 + h, 0:3 * P], ACT.Copy).then_inc(probsT[h], 1)
                nc.scalar.activation(pTm[h][0:META, :], ps[0:META, 5 + h, 0:SEQ], ACT.Copy).then_inc(probsT[h], 1)

            def pair(p, k, more):
                for h in range(2):
                    exponentials(p, h)
                if more:
                    evacuate_kv(p + 1, 1 - k)
                for h in range(2):
                    evacuate_probs(p, h)

            act.wait_ge(pads_made, 8)
            evacuate_kv(0, 0)
            act.wait_ge(f_abs, 1)
            nc.scalar.activation(ftmp[:, 1, :], ftmp[:, 1, :], ACT.Exp, scale=-1.0).then_inc(act_once, 1)
            act.wait_ge(act_once, 1)
            nc.scalar.activation(ftmp[:, 1, :], ftmp[:, 1, :], ACT.Ln, bias=1.0).then_inc(f_log, 1)
            act.wait_ge(centred, 1)
            nc.scalar.activation(squares, u_kc, ACT.Square).then_inc(sq_made, 1)
            evacuate_kv(1, 1)
            pair(0, 0, False)
            act.wait_ge(ln_var, 1)
            nc.scalar.activation(lnb[:, 1, :], lnb[:, 1, :], ACT.Sqrt).then_inc(ln_root, 1)
            pair(1, 1, True)
            act.wait_ge(sq_sum, 1)
            for c in range(KC):
                act.wait_ge(ln_made, c + 1)
                nc.scalar.activation(squares[:, c // 4, c % 4, :], u_c[:, c, :], ACT.Sigmoid,
                                     bias=cols[:, COL_LB + c:COL_LB + c + 1]).then_inc(silu_in, 1)
            with act.Fori(1, PAIRS // 2 - 1) as i:
                for k in range(2):
                    pair(i * 2 + k, k, True)
            pair(PAIRS - 2, 0, True)
            pair(PAIRS - 1, 1, False)

            for t in range(TT):
                for b in range(2):
                    act.wait_ge(h_ps, 2 * t + b + 1)
                    nc.scalar.activation(squares_x[:, b * BANK:(b + 1) * BANK], ps[:, 4 + 2 * t + b, :], ACT.Square,
                                         accum_out=stat[:, 2 * b + t:2 * b + t + 1]).then_inc(ffn_sq, 1)
                act.wait_ge(ffn_var, t + 1)
                nc.scalar.activation(stat2[:, t:t + 1], stat2[:, t:t + 1], ACT.Sqrt).then_inc(ffn_root, 1)
                for b in range(2):
                    act.wait_ge(hnT_ps, 2 * t + b + 1)
                    nc.scalar.activation(hnT[:, 4 * b:4 * b + 4, t * P:(t + 1) * P],
                                         ps[:, 2 * t + b, :].rearrange("p (c m) -> p c m", m=P),
                                         ACT.Copy).then_inc(hnT_made, 1)
            act.wait_ge(hn_made, 2 * TT)
            act.dma_start(gain[:], final_norm_g.rearrange("(a d) -> a d", a=1).to_broadcast([P, D])
                          ).then_inc(gain2_loaded, 16)

            def gathered(n):
                act.wait_ge(xg_ps, n + 1)
                nc.scalar.activation(xg, ps[:, 2, :], ACT.Copy).then_inc(xg_made, 1)

            def gathered_turned(n):
                act.wait_ge(xT_ps, n + 1)
                nc.scalar.activation(xT, ps[:, 2, :], ACT.Copy).then_inc(xT_made, 1)

            def sigmoid(n):
                act.wait_ge(gate_ready, n + 1)
                nc.scalar.activation(sg, gate_m, ACT.Sigmoid, scale=ALPHA).then_inc(sg_made, 1)

            def activations_turned(n):
                act.wait_ge(act_T_ps, n + 1)
                nc.scalar.activation(act_T, ps[:, 0, :], ACT.Copy).then_inc(act_T_made, 1)

            def weights_turned(n):
                act.wait_ge(G_ps, n + 1)
                nc.scalar.activation(G_s, ps[:, 1, :], ACT.Copy).then_inc(G_made, 1)

            def outputs(n):
                act.wait_ge(y_ps, n + 1)
                nc.scalar.activation(y_s, ps[:, 3, :], ACT.Copy).then_inc(y_made, 1)

            act.wait_ge(top_made, TT)
            for t in range(TT):
                nc.scalar.activation(route[:, 5 * E + 8 * t:5 * E + 8 * t + TOPK],
                                     route[:, 4 * E + 8 * t:4 * E + 8 * t + TOPK], ACT.Exp,
                                     bias=stat[:, 8 + t:9 + t], accum_out=stat[:, 10 + t:11 + t]).then_inc(exps_made, 1)
            gathered(0)
            gathered_turned(0)
            act.wait_ge(weight_ps, 1)
            nc.scalar.activation(weight_T, ps[:, 3, 0:SEQ], ACT.Copy).then_inc(weight_T_made, 1)
            sigmoid(0)
            activations_turned(0)
            gathered(1)
            weights_turned(0)
            gathered_turned(1)
            with act.Fori(1, E - 1) as n:
                outputs(n - 1)
                sigmoid(n)
                activations_turned(n)
                gathered(n + 1)
                weights_turned(n)
                gathered_turned(n + 1)
            outputs(E - 2)
            sigmoid(E - 1)
            activations_turned(E - 1)
            weights_turned(E - 1)
            outputs(E - 1)
            act.wait_ge(work_made, 1)
            n_work = act.value_load(work[0:1, 32:33], min_val=0, max_val=EXTRA)
            with act.If(n_work > 0):
                with act.Fori(0, EXTRA) as i:
                    with act.If(i < n_work):
                        gathered(i + E)
                        gathered_turned(i + E)
                        sigmoid(i + E)
                        activations_turned(i + E)
                        weights_turned(i + E)
                        outputs(i + E)
                    with act.Else():
                        act.nop()
            with act.Else():
                act.nop()

            for t in range(TT):
                act.wait_ge(scattered, (n_work + E) * TT - (TT - 1 - t))
                nc.scalar.activation(squares_y, ps[:, 4 + 2 * t:6 + 2 * t, :].rearrange("p b n -> p (b n)"),
                                     ACT.Square, accum_out=stat[:, t:t + 1]).then_inc(final_sq, 1)
                act.wait_ge(final_var, t + 1)
                nc.scalar.activation(stat2[:, t:t + 1], stat2[:, t:t + 1], ACT.Sqrt).then_inc(final_root, 1)

        @blk.vector
        def _(dve):
            V = nc.vector
            once = Chain(dve, dve_once)
            for s in (glu_made, conv_step, heads_out, merged_made):
                dve.sem_inc(s, 1)
            V.memset(glu[:, :, 0:TAPS - 1], 0.0).then_inc(pad_made, 1)
            dve.wait_ge(meta_loaded, 16)
            once.link(V.tensor_tensor(x_n[0:META, 2, :], x_meta, x_meta, ALU.mult))
            once.link(V.tensor_reduce(stat[0:META, 2:3], x_n[0:META, 2, :], AX_X, ALU.add))
            dve.wait_ge(sq_x, 2)
            V.tensor_scalar(stat2[:, 0:2], stat[:, 0:2], 1.0 / D, EPS, ALU.mult, ALU.add).then_inc(rms_var, 1)
            V.tensor_scalar(stat2[0:META, 2:3], stat[0:META, 2:3], 1.0 / D, EPS, ALU.mult, ALU.add).then_inc(rms_var, 1)
            dve.wait_ge(rms_root, 2)
            V.reciprocal(stat[:, 0:2], stat2[:, 0:2]).then_inc(rms_inv, 1)
            V.reciprocal(stat[0:META, 2:3], stat2[0:META, 2:3]).then_inc(rms_inv, 1)
            dve.wait_ge(rms_inv, 2)
            V.tensor_scalar(x_n[:, 0, :], x_tok[:, 0, :], stat[:, 0:1], None, ALU.mult).then_inc(xn_made, 1)
            V.tensor_scalar(x_n[0:META, 2, :], x_meta, stat[0:META, 2:3], None, ALU.mult).then_inc(xn_made, 1)
            dve.wait_ge(cols_ps, 1)
            V.tensor_copy(cols[:], ps[:, 7, 0:NCOLS]).then_inc(cols_made, 1)
            dve.wait_ge(cols_made, 1)
            for c in range(0, KC, 2):
                dve.wait_ge(xnT_ps, c + 1)
                V.tensor_scalar(xnT[:, c, :], ps[:, c % 4, 0:T], cols[:, COL_NORM + c:COL_NORM + c + 1],
                                None, ALU.mult).then_inc(xnT_made[0], 1)
            dve.wait_ge(taps_ps, 1)
            V.tensor_copy(taps[:], ps[:, 6, 0:KC * TAPS].rearrange("p (c w) -> p c w", w=TAPS)).then_inc(taps_made, 1)
            dve.wait_ge(taps_made, 1)
            dve.wait_ge(pad_made, 1)

            with dve.Fori(0, KC // 2) as i:
                for k in range(2):
                    j = i * 2 + k

                    def step(s):
                        return i * (2 * CONV_STEPS) + k * CONV_STEPS + s

                    wait_seeded(dve, sig_made, j + 1)
                    V.scalar_tensor_tensor(out=glu[:, k, TAPS - 1:], in0=ps[:, 4 * k, 0:T],
                                           scalar=cols[:, ds(j + COL_A, 1)], in1=sig_b[:],
                                           op0=ALU.add, op1=ALU.mult).then_inc(glu_made, 1)
                    wait_seeded(dve, glu_made, j + 1)
                    for w in range(TAPS):
                        src = glu[:, k, META + w:META + w + SEQ]
                        acc = conv_acc[:, w % 2, :]
                        tap = taps[:, ds(j, 1), w]
                        if w == 0:
                            wait_seeded(dve, conv_step, step(0))
                            V.tensor_scalar(acc, src, tap, cols[:, ds(j + COL_CB, 1)],
                                            ALU.mult, ALU.add).then_inc(conv_step, 1)
                        elif w == 1:
                            V.tensor_scalar(acc, src, tap, None, ALU.mult).then_inc(conv_step, 1)
                        else:
                            wait_seeded(dve, conv_step, step(w - 1))
                            V.scalar_tensor_tensor(out=acc, in0=src, scalar=tap, in1=acc,
                                                   op0=ALU.mult, op1=ALU.add).then_inc(conv_step, 1)
                    wait_seeded(dve, conv_step, step(TAPS))
                    V.tensor_tensor(u_c[:, ds(j, 1), :], conv_acc[:, 0:1, :], conv_acc[:, 1:2, :],
                                    ALU.add).then_inc(conv_step, 1)

            wait_seeded(dve, conv_step, KC * CONV_STEPS)
            V.tensor_reduce(lnb[:, 0, :], u_c.rearrange("p c t -> p t c"), AX_X, ALU.add).then_inc(u_sum, 1)
            dve.wait_ge(f_ps, 1)
            once.link(V.tensor_scalar(ftmp[:, 0, :], ps[0:HEADS, 7, 0:T], bf[:, 0:1], None, ALU.add))
            once.link(V.tensor_scalar(ftmp[:, 2, :], ftmp[:, 0, :], -1.0, None, ALU.mult))
            V.tensor_tensor(ftmp[:, 1, :], ftmp[:, 0, :], ftmp[:, 2, :], ALU.max).then_inc(f_abs, 1)
            dve.wait_ge(masks_made, 6)
            dve.wait_ge(pads_made, 8)

            def evacuate_q(p, k):
                dve.wait_ge(q_ps, p + 1)
                for h in range(2):
                    r = slice(h * DH, (h + 1) * DH)
                    V.tensor_scalar(q_s[k][h][r, :], ps[r, 0, 0:SEQ], cols[r, ds(p + COL_Q, 1)], DH ** -0.5,
                                    ALU.add, ALU.mult).then_inc(q_made, 1)

            def key_sums(p, k):
                for h in range(2):
                    other = slice((1 - h) * DH, (1 - h) * DH + HEADS)
                    V.tensor_scalar(k_s[k][h][other, :], cum[:], neg_head[:, ds(p * 2 + h, 1)], None,
                                    ALU.mult).then_inc(kc_made, 1)

            evacuate_q(0, 0)
            dve.wait_ge(mean_ps, 1)
            once.link(V.tensor_scalar(lnb[:, 0, :], ps[:, 4, 0:SEQ], 1.0 / D, None, ALU.mult))
            V.tensor_tensor(u_c, u_c, lnb[:, 0:1, :].to_broadcast([P, KC, SEQ]), ALU.subtract).then_inc(centred, 1)
            dve.wait_ge(f_log, 1)
            once.link(V.scalar_tensor_tensor(out=ftmp[:, 2, :], in0=ftmp[:, 0, :], scalar=0.0,
                                             in1=ftmp[:, 1, :], op0=ALU.min, op1=ALU.subtract))
            once.link(V.memset(ftmp[:, 0, :], 1.0))
            V.tensor_tensor_scan(cum[:], ftmp[:, 0, :], ftmp[:, 2, :], 0.0, ALU.mult, ALU.add).then_inc(cum_made, 1)

            PAIR_STEPS = 10
            pc = Chain(dve, dve_pair, PAIR_STEPS)

            def pair(p, k, more, meanwhile=None):
                pc.at(p)
                for h in range(2):
                    dve.wait_ge(scores[h], p + 1)
                    wait_seeded(dve, exp_made[h], p * 2)
                    for t, (a, b, m) in enumerate(((0, K0, mask0), (K0, SCW, mask1))):
                        pc.link(V.scalar_tensor_tensor(out=sc[h][:, a:b], in0=ps[:, 3 + h, a:b],
                                                       scalar=cum_q[:, t, ds(p * 2 + h, 1)], in1=m[:],
                                                       op0=ALU.add, op1=ALU.add))
                    nm = stat[:, 4 + 4 * h:6 + 4 * h]
                    pc.link(V.tensor_reduce(nm[:, 0:1], sc[h][:, 0:K0], AX_X, ALU.max, negate=True))
                    V.tensor_reduce(nm[:, 1:2], sc[h][:, K0:SCW], AX_X, ALU.max,
                                    negate=True).then_inc(max_made[h], 1)
                for h in range(2):
                    wait_seeded(dve, exp_made[h], p * 2 + 2)
                    pc.link(V.reciprocal(stat2[:, 6 + 4 * h:8 + 4 * h], stat2[:, 4 + 4 * h:6 + 4 * h]))
                    pc.link(V.tensor_scalar(pr[h][:, 0:K0], pr[h][:, 0:K0], stat2[:, 6 + 4 * h:7 + 4 * h],
                                            None, ALU.mult))
                    V.tensor_scalar(pr[h][:, K0:SCW], pr[h][:, K0:SCW], stat2[:, 7 + 4 * h:8 + 4 * h],
                                    None, ALU.mult).then_inc(probs[h], 1)
                assert pc.k == PAIR_STEPS
                if more:
                    key_sums(p + 1, 1 - k)
                if meanwhile is not None:
                    meanwhile()
                if more:
                    evacuate_q(p + 1, 1 - k)
                dve.wait_ge(heads_ps, p + 1)
                V.tensor_scalar(attn_T[:, ds(p, 1), :], ps[:, 7:8, 0:SEQ], 1.0, None, ALU.mult).then_inc(heads_out, 1)

            dve.wait_ge(cum_made, 1)
            key_sums(0, 0)
            key_sums(1, 1)
            dve.wait_ge(sq_made, 1)
            once.link(V.tensor_reduce(squares_of[0], squares[:, 0].rearrange("p c t -> p t c"), AX_X, ALU.add))
            once.link(V.tensor_reduce(squares_of[1], squares[:, 1].rearrange("p c t -> p t c"), AX_X, ALU.add))
            V.tensor_tensor(lnb[:, 1, :], squares_of[0], squares_of[1], ALU.add).then_inc(sq_sum, 1)
            evacuate_q(1, 1)
            dve.wait_ge(cumT_ps, 1)
            V.tensor_copy(cum_q[:], ps[:, 6, 0:TT * HEADS].rearrange("p (t h) -> p t h", h=HEADS)).then_inc(cum_q_made, 1)
            dve.wait_ge(cum_q_made, 1)
            pair(0, 0, False)
            dve.wait_ge(var_ps, 1)
            V.tensor_scalar(lnb[:, 1, :], ps[:, 0, 0:SEQ], 1.0 / D, EPS, ALU.mult, ALU.add).then_inc(ln_var, 1)
            def scale():
                dve.wait_ge(ln_root, 1)
                once.link(V.reciprocal(lnb[:, 1, :], lnb[:, 1, :]))
                for c in range(KC):
                    V.scalar_tensor_tensor(out=u_c[:, c, :], in0=u_c[:, c, :],
                                           scalar=cols[:, COL_LG + c:COL_LG + c + 1], in1=lnb[:, 1, :],
                                           op0=ALU.mult, op1=ALU.mult).then_inc(ln_made, 1)

            def silu():
                for c in range(KC):
                    dve.wait_ge(silu_in, c + 1)
                    V.scalar_tensor_tensor(out=u_c[:, c, :], in0=u_c[:, c, :],
                                           scalar=cols[:, COL_LB + c:COL_LB + c + 1],
                                           in1=squares[:, c // 4, c % 4, :], op0=ALU.add,
                                           op1=ALU.mult).then_inc(silu_made, 1)

            pair(1, 1, True, scale)
            with dve.Fori(1, PAIRS // 2 - 1) as i:
                for k in range(2):
                    pair(i * 2 + k, k, True)
            pair(PAIRS - 2, 0, True, silu)
            pair(PAIRS - 1, 1, False)

            with dve.Fori(0, KC // 2) as i:
                for k in range(2):
                    j = i * 2 + k
                    dve.wait_ge(br_ps, j + 1)
                    wait_seeded(dve, merged_made, j)
                    V.tensor_tensor(tmp_m[0], sigs[:, 0, ds(j, 1), :].rearrange("p a t -> p (a t)"),
                                    ps[:, 2 * k, 0:SEQ], ALU.mult).then_inc(dve_merge, 1)
                    V.tensor_tensor(tmp_m[1], sigs[:, 1, ds(j, 1), :].rearrange("p a t -> p (a t)"),
                                    ps[:, 2 * k + 1, 0:SEQ], ALU.mult).then_inc(dve_merge, 1)
                    dve.wait_ge(dve_merge, j * 2 + 2)
                    V.tensor_tensor(merged[:, ds(j, 1), :].rearrange("p a t -> p (a t)"),
                                    tmp_m[0], tmp_m[1], ALU.add).then_inc(merged_made, 1)

            def select_expert(n, e):
                if not isinstance(n, int) or n > 0:
                    dve.wait_ge(biased, n)
                V.tensor_scalar(sel_e, ones[:, 0:SLOTS], ident[:, ds(e, 1)], None, ALU.mult).then_inc(sel_e_made, 1)

            select_expert(0, 0)
            once.link(V.memset(weight[:], 0.0))
            once.link(V.memset(sel_w, 0.0))
            dve.wait_ge(gain_loaded, 16)
            dve.wait_ge(consts_loaded, 64)
            chosen = [route[:, (2 + t) * E:(3 + t) * E] for t in range(TT)]
            tops = [route[:, 4 * E + 8 * t:4 * E + 8 * t + 8] for t in range(TT)]
            wts = [route[:, 5 * E + 8 * t:5 * E + 8 * t + TOPK] for t in range(TT)]
            picks = [route[:, (8 + 4 * t) * E:(12 + 4 * t) * E].rearrange("p (c e) -> p c e", c=TOPK) for t in range(TT)]
            for t in range(TT):
                dve.wait_ge(ffn_sq, 2 * t + 1)
                once.link(V.tensor_scalar(stat2[:, t:t + 1], stat[:, t:t + 1], 1.0 / D, EPS, ALU.mult, ALU.add))
                dve.wait_ge(ffn_sq, 2 * t + 2)
                V.scalar_tensor_tensor(out=stat2[:, t:t + 1], in0=stat[:, 2 + t:3 + t], scalar=1.0 / D,
                                       in1=stat2[:, t:t + 1], op0=ALU.mult, op1=ALU.add).then_inc(ffn_var, 1)
                dve.wait_ge(ffn_root, t + 1)
                once.link(V.reciprocal(stat[:, t:t + 1], stat2[:, t:t + 1]))
                for b in range(2):
                    half = slice(b * BANK, (b + 1) * BANK)
                    V.scalar_tensor_tensor(out=hn[:, t, half], in0=ps[:, 4 + 2 * t + b, :], scalar=stat[:, t:t + 1],
                                           in1=gain[:, half], op0=ALU.mult, op1=ALU.mult).then_inc(hn_made, 1)
                lg = route[:, t * E:(t + 1) * E]
                idx = route[:, 7 * E + 8 * t:7 * E + 8 * t + 8]
                dve.wait_ge(logits_ps, t + 1)
                once.link(V.tensor_tensor(lg, ps[:, t, 0:E], rb[:], ALU.add))
                once.link(V.max(tops[t], lg))
                once.link(V.max_index(route_i[:, 0:8], tops[t], lg))
                once.link(V.tensor_copy(idx, route_i[:, 0:8]))
                once.link(V.tensor_tensor(picks[t],
                                          iota[:, 0:E].rearrange("p (a e) -> p a e", a=1).to_broadcast([P, TOPK, E]),
                                          idx[:, 0:TOPK].rearrange("p (c a) -> p c a", a=1).to_broadcast([P, TOPK, E]),
                                          ALU.is_equal))
                V.tensor_reduce(chosen[t], picks[t].rearrange("p c e -> p e c"), AX_X, ALU.add).then_inc(picks_made, 1)
                V.tensor_scalar(stat[:, 8 + t:9 + t], tops[t][:, 0:1], -1.0, None, ALU.mult).then_inc(top_made, 1)
            dve.wait_ge(picks_made, TT)
            dve.wait_ge(pos_ps, 3)
            for t in range(TT):
                pos = route[:, t * E:(t + 1) * E]
                once.link(V.scalar_tensor_tensor(out=pos, in0=ps[:, 3, t * E:(t + 1) * E], scalar=1.0,
                                                 in1=chosen[t], op0=ALU.add, op1=ALU.mult))
                V.tensor_scalar(slot_of[:, t, :], pos, -1.0, None, ALU.add).then_inc(table_made, 1)
            dve.wait_ge(table_made, TT)

            def select(n, e, first):
                if not isinstance(n, int) or n > 0:
                    dve.wait_ge(xg_ps, n)
                for t in range(TT):
                    V.tensor_scalar(sel[:, t, :], iota[:, ds(first, SLOTS)], slot_of[:, t, ds(e, 1)],
                                    None, ALU.is_equal).then_inc(sel_made, 1)

            def select_weighted(n, e, first):
                if not isinstance(n, int) or n > 0:
                    dve.wait_ge(G_ps, n)
                for t in range(TT):
                    V.tensor_scalar(sel_w[:, t, SLOTS:2 * SLOTS], iota[:, ds(first, SLOTS)],
                                    slot_of[:, t, ds(e, 1)], weight[:, t, ds(e, 1)],
                                    ALU.is_equal, ALU.mult).then_inc(sel_w_made, 1)

            def swiglu(n):
                dve.wait_ge(gu_ps, n + 1)
                V.tensor_scalar(gate_m, ps[:, 0, :], LIMIT, None, ALU.min).then_inc(gate_ready, 1)
                V.tensor_scalar(up_m, ps[:, 1, :], LIMIT, -LIMIT, ALU.min, ALU.max).then_inc(up_ready, 1)
                dve.wait_ge(up_ready, n + 1)
                V.scalar_tensor_tensor(out=gu_m, in0=up_m, scalar=1.0, in1=gate_m, op0=ALU.add,
                                       op1=ALU.mult).then_inc(gu_m_made, 1)
                dve.wait_ge(gu_m_made, n + 1)
                dve.wait_ge(sg_made, n + 1)
                V.tensor_tensor(act_s, gu_m, sg, ALU.mult).then_inc(act_made, 1)

            select(0, 0, 0)
            dve.wait_ge(exps_made, TT)
            once.link(V.reciprocal(stat2[:, 10:10 + TT], stat[:, 10:10 + TT]))
            for t in range(TT):
                once.link(V.tensor_scalar(wts[t], wts[t], stat2[:, 10 + t:11 + t], None, ALU.mult))
                once.link(V.tensor_tensor(picks[t], picks[t],
                                          wts[t].rearrange("p (c a) -> p c a", a=1).to_broadcast([P, TOPK, E]), ALU.mult))
                V.tensor_reduce(weight[:, t, 0:E], picks[t].rearrange("p c e -> p e c"), AX_X,
                                ALU.add).then_inc(weights_made, 1)
            dve.wait_ge(weights_made, TT)
            select(1, 1, 0)

            n_more = (BLOCKS - 1) * E
            lst = [gates[0:1, a * n_more:(a + 1) * n_more] for a in range(5)]
            active, rank, of_e, of_s = lst[0:4]
            counts = lst[4][:, 0:E]
            match = gates[0:1, 5 * n_more:(5 + EXTRA) * n_more].rearrange("p (r i) -> p r i", i=n_more)
            assert (5 + EXTRA) * n_more <= 4 * BANK
            once.link(V.tensor_copy(counts, ps[0:1, 3, TT * E:TT * E + E]))
            for b in range(1, BLOCKS):
                part = slice((b - 1) * E, b * E)
                once.link(V.tensor_scalar(active[:, part], counts, float(b * SLOTS), None, ALU.is_gt))
                once.link(V.tensor_copy(of_e[:, part], iota[0:1, 0:E]))
                once.link(V.memset(of_s[:, part], float(b * SLOTS)))
            once.link(V.tensor_tensor_scan(rank, ones[0:1, 0:n_more], active, 0.0, ALU.mult, ALU.add))
            once.link(V.memset(work_f[:], 0.0))
            once.link(V.tensor_copy(work_f[:, 32:33], rank[:, n_more - 1:n_more]))
            once.link(V.tensor_tensor(rank, rank, active, ALU.mult))
            shape = [1, EXTRA, n_more]
            for a, values in enumerate((of_e, of_s)):
                once.link(V.tensor_tensor(match, rank.rearrange("p (a i) -> p a i", a=1).to_broadcast(shape),
                                          iota[0:1, 1:1 + EXTRA].rearrange("p (r a) -> p r a", a=1).to_broadcast(shape),
                                          ALU.is_equal))
                once.link(V.tensor_tensor(match, match, values.rearrange("p (a i) -> p a i", a=1).to_broadcast(shape),
                                          ALU.mult))
                once.link(V.tensor_reduce(work_f[:, 16 * a:16 * a + EXTRA], match, AX_X, ALU.add))
            V.tensor_copy(work[:], work_f[:]).then_inc(work_made, 1)
            dve.wait_ge(work_made, 1)

            select_expert(1, 1)
            select_weighted(0, 0, 0)
            swiglu(0)
            with dve.Fori(1, E - 1) as n:
                select(n + 1, n + 1, 0)
                select_expert(n + 1, n + 1)
                select_weighted(n, n, 0)
                swiglu(n)
            select_weighted(E - 1, E - 1, 0)
            swiglu(E - 1)
            n_work = dve.value_load(work[0:1, 32:33], min_val=0, max_val=EXTRA)
            with dve.If(n_work > 0):
                with dve.Fori(0, EXTRA) as i:
                    with dve.If(i < n_work):
                        e = dve.value_load(work[0:1, ds(i, 1)], min_val=0, max_val=E - 1)
                        first = dve.value_load(work[0:1, ds(i + 16, 1)], min_val=0, max_val=SEQ - SLOTS)
                        select(i + E, e, first)
                        select_expert(i + E, e)
                        select_weighted(i + E, e, first)
                        swiglu(i + E)
                    with dve.Else():
                        dve.nop()
            with dve.Else():
                dve.nop()

            dve.wait_ge(gain2_loaded, 16)
            for t in range(TT):
                dve.wait_ge(final_sq, t + 1)
                V.tensor_scalar(stat2[:, t:t + 1], stat[:, t:t + 1], 1.0 / D, EPS, ALU.mult, ALU.add).then_inc(final_var, 1)
                dve.wait_ge(final_root, t + 1)
                once.link(V.reciprocal(stat[:, t:t + 1], stat2[:, t:t + 1]))
                V.scalar_tensor_tensor(out=result[:, t, :],
                                       in0=ps[:, 4 + 2 * t:6 + 2 * t, :].rearrange("p b n -> p (b n)"),
                                       scalar=stat[:, t:t + 1], in1=gain[:], op0=ALU.mult,
                                       op1=ALU.mult).then_inc(final_made, 1)

        @blk.tensor
        def _(pe):
            mm = nc.tensor.matmul

            for s in probsT_ps:
                pe.sem_inc(s, 1)
            pe.wait_ge(masks_made, 1)
            pe.wait_ge(rows_loaded, 16 * 3)
            pe.wait_ge(raws_loaded, 16 * 4)
            nc.tensor.transpose(ps[:, 7, 0:NCOLS], raw_cols, ident[0:NCOLS, 0:NCOLS]).then_inc(cols_ps, 1)
            for c in range(KC):
                last = nc.tensor.transpose(ps[:, 6, c * TAPS:(c + 1) * TAPS], raw_taps[:, c * P:(c + 1) * P],
                                           ident[0:TAPS, 0:TAPS])
            last.then_inc(taps_ps, 1)
            pe.wait_ge(xn_made, 3)
            for c in range(KC):
                if c >= 4:
                    pe.wait_ge(xnT_made[c % 2], (c - 2) // 2)
                for t in range(TT):
                    nc.tensor.transpose(ps[:, c % 4, META + t * P:META + (t + 1) * P],
                                        x_n[:, t, c * P:(c + 1) * P], ident[:])
                nc.tensor.transpose(ps[:, c % 4, 0:META], x_n[0:META, 2, c * P:(c + 1) * P],
                                    ident[0:META, 0:META]).then_inc(xnT_ps, 1)
            for made in xnT_made:
                pe.wait_ge(made, KC // 2)
            pe.wait_ge(cols_made, 1)
            pe.wait_ge(taps_made, 1)

            def project(bank, w, act, n):
                for c in range(KC):
                    last = mm(ps[:, bank, 0:n], w[:, c, :], act[:, c, :], start=(c == 0), stop=(c == KC - 1))
                return last

            x_all, x_seq = xnT[:], xnT[:, :, META:T]
            with pe.Fori(0, KC // 2) as i:
                for k in range(2):
                    pe.wait_ge(glu_w[k], i * 64 + 64)
                    wait_seeded(pe, sig_made, i * 2 + k)
                    project(4 * k + 1, fill(k, 1), x_all, T)
                    project(4 * k, fill(k, 0), x_all, T).then_inc(glu_ps, 1)
                    project(4 * k + 2, fill(k, 2), x_seq, SEQ)
                    project(4 * k + 3, fill(k, 3), x_seq, SEQ).then_inc(gates_ps, 1)

            pe.wait_ge(consts_loaded, 64)
            pe.wait_ge(gates_made, 2 * KC)
            for c in range(KC):
                last = mm(ps[0:HEADS, 7, 0:T], wf[:, c, :], xnT[:, c, :], start=(c == 0), stop=(c == KC - 1))
            last.then_inc(f_ps, 1)

            def turn_probs(p):
                for h in range(2):
                    pe.wait_ge(probs[h], p + 1)
                    wait_seeded(pe, probsT[h], p * 2)
                    b = 3 + h
                    nc.tensor.transpose(ps[:, b, 0:P], pr[h][:, META:K0], ident[:])
                    nc.tensor.transpose(ps[:, b, P:2 * P], pr[h][:, K0 + META:K0 + K0], ident[:])
                    nc.tensor.transpose(ps[:, b, 2 * P:3 * P], pr[h][:, K0 + K0:SCW], ident[:])
                    nc.tensor.transpose(ps[0:META, 5 + h, 0:P], pr[h][:, 0:META], ident[:])
                    nc.tensor.transpose(ps[0:META, 5 + h, P:2 * P], pr[h][:, K0:K0 + META],
                                        ident[:]).then_inc(probsT_ps[h], 1)

            def project_v(p, k, i):
                pe.wait_ge(qkv_w[k], i * 48 + 48)
                if not isinstance(p, int) or p > 0:
                    pe.wait_ge(v_made, p * 2)
                project(2, fill(k, 2), x_all, T).then_inc(v_ps, 1)

            def qkv(p, k, i, v_done=False, turn=None):
                if not v_done:
                    project_v(p, k, i)
                if not isinstance(p, int) or p > 0:
                    pe.wait_ge(k_made, p * 2)
                    pe.wait_ge(q_made, p * 2)
                project(1, fill(k, 1), x_all, T).then_inc(k_ps, 1)
                pe.wait_ge(vT_made, p + 1)
                nc.tensor.transpose(ps[0:META, 2, 0:P], v_T[:, 0:META], ident[:])
                nc.tensor.transpose(ps[:, 2, P:2 * P], v_T[:, META:META + P], ident[:])
                nc.tensor.transpose(ps[:, 2, 2 * P:3 * P], v_T[:, META + P:T], ident[:]).then_inc(vtr_ps, 1)
                if turn is not None:
                    turn_probs(turn)
                project(0, fill(k, 0), x_seq, SEQ).then_inc(q_ps, 1)

            def attend_scores(p, k):
                for h in range(2):
                    pe.wait_ge(q_made, p * 2 + h + 1)
                    pe.wait_ge(k_made, p * 2 + h + 1)
                    pe.wait_ge(kc_made, p * 2 + h + 1)
                    mm(ps[:, 3 + h, 0:K0], q_s[k][h][:, 0:P], k_s[k][h][:, 0:K0], start=True, stop=True)
                    mm(ps[:, 3 + h, K0:SCW], q_s[k][h][:, P:2 * P], k_s[k][h], start=True,
                       stop=True).then_inc(scores[h], 1)

            def attend_values(p, k):
                pe.wait_ge(v_made, p * 2 + 2)
                wait_seeded(pe, heads_out, p)
                for h in range(2):
                    wait_seeded(pe, probsT[h], p * 2 + 2)
                    o = ps[h * DH:(h + 1) * DH, 7, :]
                    hs = slice(h * DH, (h + 1) * DH)
                    for t in range(TT):
                        q = slice(t * P, (t + 1) * P)
                        mm(o[:, q], v_s[k][:, P + h * DH:P + (h + 1) * DH], pT[h][:, q], start=True, stop=False)
                        if t == 1:
                            mm(o[:, q], v_s[k][:, 2 * P + h * DH:2 * P + (h + 1) * DH], pT[h][:, SEQ:3 * P],
                               start=False, stop=False)
                        last = mm(o[:, q], v_s[k][:, hs], pTm[h][:, q], start=False, stop=True)
                last.then_inc(heads_ps, 1)

            qkv(0, 0, 0)
            pe.wait_ge(masks_made, 2)
            pe.wait_ge(u_sum, 1)
            mm(ps[:, 4, 0:SEQ], ones[:], lnb[:, 0, :], start=True, stop=True).then_inc(mean_ps, 1)
            qkv(1, 1, 0)
            pe.wait_ge(cum_made, 1)
            for t in range(TT):
                last = nc.tensor.transpose(ps[:, 6, t * HEADS:(t + 1) * HEADS],
                                           cum[:, META + t * P:META + (t + 1) * P], ident[0:HEADS, 0:HEADS])
            last.then_inc(cumT_ps, 1)
            pe.wait_ge(centred, 1)
            attend_scores(0, 0)
            pe.wait_ge(sq_sum, 1)
            pe.wait_ge(q_made, 4)
            mm(ps[:, 0, 0:SEQ], ones[:], lnb[:, 1, :], start=True, stop=True).then_inc(var_ps, 1)
            project_v(2, 0, 1)
            pe.wait_ge(cum_q_made, 1)
            turn_probs(0)
            attend_values(0, 0)
            attend_scores(1, 1)
            pe.wait_ge(ln_var, 1)
            qkv(2, 0, 1, v_done=True, turn=1)
            attend_values(1, 1)
            with pe.Fori(1, PAIRS // 2 - 1) as i:
                for k in range(2):
                    p = i * 2 + k
                    attend_scores(p, k)
                    qkv(p + 1, 1 - k, i + k, turn=p)
                    attend_values(p, k)
            attend_scores(PAIRS - 2, 0)
            qkv(PAIRS - 1, 1, PAIRS // 2 - 1, turn=PAIRS - 2)
            attend_values(PAIRS - 2, 0)
            attend_scores(PAIRS - 1, 1)

            def branch(j, k, b, need):
                pe.wait_ge(out_w[k], need)
                return project(2 * k + b, fill(k, b), attn_T if b else u_c, SEQ)

            pe.wait_ge(silu_made, KC)
            pe.wait_ge(q_made, PAIRS * 2)
            branch(0, 0, 0, 32)
            pe.wait_ge(v_made, PAIRS * 2)
            branch(1, 1, 0, 32)
            turn_probs(PAIRS - 1)
            pe.wait_ge(k_made, PAIRS * 2)
            attend_values(PAIRS - 1, 1)
            wait_seeded(pe, heads_out, PAIRS)
            branch(0, 0, 1, 32).then_inc(br_ps, 1)
            branch(1, 1, 1, 32).then_inc(br_ps, 1)
            with pe.Fori(1, KC // 2) as i:
                for k in range(2):
                    wait_seeded(pe, merged_made, i * 2 + (k - 1))
                    branch(i * 2 + k, k, 0, i * 32 + 32)
                    branch(i * 2 + k, k, 1, i * 32 + 32).then_inc(br_ps, 1)

            pe.wait_ge(mix_w, 32)
            for loaded_x in x_loaded:
                pe.wait_ge(loaded_x, 16)

            def halves(bank, lhsT, rhs, start, stop, **kw):
                for h in range(2):
                    last = mm(ps[h * SLOTS:(h + 1) * SLOTS, bank, :], lhsT, rhs[:, h * BANK:(h + 1) * BANK],
                              start=start, stop=stop, **kw)
                return last

            def bias(b):
                return halves(b, sel_e, bias_gu[:, b * D:(b + 1) * D], True, False)

            def mix(t, b, chunks):
                acc = ps[:, 4 + 2 * t + b, :]
                if chunks[0] == 0:
                    if t == 0 and b == 0:
                        wait_seeded(pe, merged_made, KC - 2)
                    mm(acc, ident[:], x_tok[:, t, b * BANK:(b + 1) * BANK], start=True, stop=False)
                for c in chunks:
                    if t == 0 and b == 0 and c >= KC - 2:
                        wait_seeded(pe, merged_made, c + 1)
                    a = (c % 4) * D + b * BANK
                    last = mm(acc, merged[:, c, t * P:(t + 1) * P], ring[:, 2 + c // 4, a:a + BANK],
                              start=False, stop=(c == KC - 1))
                return last

            def turn_tokens(t):
                for b in range(2):
                    pe.wait_ge(hn_made, 2 * t + b + 1)
                    for c in range(4 * b, 4 * b + 4):
                        last = nc.tensor.transpose(ps[:, 2 * t + b, (c % 4) * P:(c % 4 + 1) * P],
                                                   hn[:, t, c * P:(c + 1) * P], ident[:])
                    last.then_inc(hnT_ps, 1)

            def router(t):
                for c in range(KC):
                    if c % 4 == 0:
                        pe.wait_ge(hnT_made, 2 * t + c // 4 + 1)
                    last = mm(ps[:, t, 0:E], hnT[:, c, t * P:(t + 1) * P], wr[:, c, :],
                              start=(c == 0), stop=(c == KC - 1))
                last.then_inc(logits_ps, 1)

            every, split = list(range(KC)), KC // 4
            mix(0, 0, every).then_inc(h_ps, 1)
            mix(0, 1, every).then_inc(h_ps, 1)
            mix(1, 0, every).then_inc(h_ps, 1)
            turn_tokens(0)
            mix(1, 1, every[:split])
            router(0)
            mix(1, 1, every[split:]).then_inc(h_ps, 1)
            turn_tokens(1)
            router(1)
            pos = ps[:, 3, :]
            pe.wait_ge(picks_made, 1)
            pe.wait_ge(bias_loaded, 32)
            pe.wait_ge(sel_e_made, 1)
            bias(0)
            mm(pos[:, 0:E], before[:], route[:, 2 * E:3 * E], start=True, stop=True).then_inc(pos_ps, 1)
            mm(pos[:, E:2 * E], ones[:], route[:, 2 * E:3 * E], start=True, stop=False)
            pe.wait_ge(picks_made, 2)
            mm(pos[:, E:2 * E], before[:], route[:, 3 * E:4 * E], start=False, stop=True).then_inc(pos_ps, 1)
            mm(pos[0:1, 2 * E:3 * E], ones[:, 0:1], route[:, 2 * E:3 * E], start=True, stop=False)
            mm(pos[0:1, 2 * E:3 * E], ones[:, 0:1], route[:, 3 * E:4 * E], start=False, stop=True).then_inc(pos_ps, 1)
            bias(1).then_inc(biased, 1)

            def turn(bank, src):
                for j in range(4):
                    last = nc.tensor.transpose(ps[:, bank, j * P:(j + 1) * P], src[:, j * P:(j + 1) * P], ident[:])
                return last

            def chunk_of(turned, c):
                a = (c % 4) * P + (c // 4) * SLOTS
                return turned[:, a:a + SLOTS]

            def gather(n):
                pe.wait_ge(sel_made, n * 2 + 2)
                if not isinstance(n, int) or n > 0:
                    pe.wait_ge(xT_made, n)
                for t in range(TT):
                    last = halves(2, sel[:, t, :], hn[:, t, :], t == 0, t == TT - 1)
                last.then_inc(xg_ps, 1)

            def turn_gathered(n):
                pe.wait_ge(xg_made, n + 1)
                turn(2, xg).then_inc(xT_ps, 1)

            def loaded(n, q):
                skipped = 0
                if q < len(ahead) and not (isinstance(n, int) and n < 1):
                    skipped += 1
                if q == 0 and not (isinstance(n, int) and n < 3):
                    skipped += 1
                return n * 16 + (1 - skipped) * 16

            def gate_up(n):
                if not isinstance(n, int) or n > 0:
                    pe.wait_ge(sel_e_made, n + 1)
                    pe.wait_ge(act_T_made, n)
                    pe.wait_ge(G_made, n)
                    bias(0)
                    bias(1).then_inc(biased, 1)
                pe.wait_ge(xT_made, n + 1)
                for q in range(GU_CHUNKS):
                    if isinstance(n, int) and (n, q) in ((1, 0), (1, 1), (3, 0)):
                        pe.wait_ge(ahead_w[q], 32 if n == 1 else 64)
                        slabs = ahead[q]
                    else:
                        pe.wait_ge(chunk_w[q], loaded(n, q))
                        slabs = [ring[:, q, 0:GU], ring[:, q, GU:2 * GU]]
                    for cc, w in enumerate(slabs):
                        c = 2 * q + cc
                        for b in range(2):
                            last = halves(b, chunk_of(xT, c), w[:, b * D:(b + 1) * D], False, c == KC - 1)
                    last.then_inc(chunk_used[q], 1)

            def turn_activations(n):
                pe.wait_ge(act_made, n + 1)
                turn(0, act_s).then_inc(act_T_ps, 1)

            def down(n, q):
                if q == GU_CHUNKS:
                    pe.wait_ge(act_T_made, n + 1)
                    if not isinstance(n, int) or n > 0:
                        pe.wait_ge(y_made, n)
                pe.wait_ge(chunk_w[q], n * 16 + 16)
                w = ring[:, q, :].rearrange("p (c n) -> p c n", c=4)
                for cc in range(4):
                    c = 4 * (q - GU_CHUNKS) + cc
                    last = halves(3, chunk_of(act_T, c), w[:, cc, :], c == 0, c == KC - 1)
                last.then_inc(chunk_used[q], 1)

            def turn_weights(n):
                pe.wait_ge(sel_w_made, n * 2 + 2)
                for h in range(2):
                    for t in range(TT):
                        a = (2 * h + t) * P
                        last = nc.tensor.transpose(ps[:, 1, a:a + P],
                                                   sel_w[:, t, (1 - h) * SLOTS:(3 - h) * SLOTS], ident[:])
                last.then_inc(G_ps, 1)

            def scatter(n):
                pe.wait_ge(G_made, n + 1)
                pe.wait_ge(y_made, n + 1)
                for t in range(TT):
                    for h in range(2):
                        a = (2 * h + t) * P
                        last = mm(ps[:, 4 + 2 * t + h, :], G_s[:, a:a + P], y_s, start=False, stop=True,
                                  skip_group_check=True)
                    last.then_inc(scattered, 1)

            gather(0)
            turn_gathered(0)
            gate_up(0)
            pe.wait_ge(work_made, 1)
            pe.wait_ge(weights_made, TT)
            for t in range(TT):
                last = nc.tensor.transpose(ps[:, 3, t * P:(t + 1) * P], weight[:, t, :], ident[:])
            last.then_inc(weight_ps, 1)
            pe.wait_ge(weight_T_made, 1)
            for t in range(TT):
                for h in range(2):
                    mm(ps[:, 4 + 2 * t + h, :], weight_T[:, t * P:(t + 1) * P], bias_down[:, h * BANK:(h + 1) * BANK],
                       start=False, stop=True, skip_group_check=True)
            turn_activations(0)
            gather(1)
            down(0, 4)
            turn_weights(0)
            turn_gathered(1)
            down(0, 5)

            def block(n):
                gate_up(n)
                scatter(n - 1)
                turn_activations(n)
                gather(n + 1)
                down(n, 4)
                turn_weights(n)
                turn_gathered(n + 1)
                down(n, 5)

            for n in range(1, 4):
                block(n)
            with pe.Fori(4, E - 1) as n:
                block(n)
            gate_up(E - 1)
            scatter(E - 2)
            turn_activations(E - 1)
            turn_weights(E - 1)
            down(E - 1, 4)
            down(E - 1, 5)
            scatter(E - 1)
            n_work = pe.value_load(work[0:1, 32:33], min_val=0, max_val=EXTRA)
            with pe.If(n_work > 0):
                with pe.Fori(0, EXTRA) as i:
                    with pe.If(i < n_work):
                        gather(i + E)
                        turn_gathered(i + E)
                        gate_up(i + E)
                        turn_activations(i + E)
                        down(i + E, 4)
                        turn_weights(i + E)
                        down(i + E, 5)
                        scatter(i + E)
                    with pe.Else():
                        pe.nop()
            with pe.Else():
                pe.nop()


_INS = ['x', 'meta_tokens', 'attn_norm_g', 'w_in', 'b_in', 'conv_w', 'conv_b', 'conv_ln_g', 'conv_ln_b',
        'w_conv_out', 'w_attn_out', 'w_mix_out', 'ffn_norm_g', 'router_w', 'router_b', 'w_gu', 'b_gu',
        'w_down', 'b_down', 'final_norm_g']
_OUTS = [((1, SEQ, D), 'float32')]


def kernel(**inputs):
    import numpy as _np
    import concourse.bacc as _bacc
    from concourse import mybir as _mybir
    from concourse.bass_utils import run_bass_kernel_spmd as _run

    nc = _bacc.Bacc("TRN2", target_bir_lowering=False, num_devices=1)
    arrays, args = {}, []
    for name in _INS:
        a = _np.ascontiguousarray(inputs[name])
        arrays[f"in_{name}_dram"] = a
        args.append(nc.dram_tensor(f"in_{name}_dram", a.shape, _mybir.dt.from_np(a.dtype), kind="ExternalInput").ap())
    for i, (shape, dtype) in enumerate(_OUTS):
        dt = _mybir.dt.from_np(_np.dtype(dtype))
        args.append(nc.dram_tensor(f"out_{i}_dram", shape, dt, kind="ExternalOutput").ap())
    build(nc, *args)
    r = _run(nc, [arrays], core_ids=[0])
    return _np.asarray(r.results[0]["out_0_dram"])
```
